# Optimizing a Trainium2 kernel written in Bass

```python
import math
import jax, jax.numpy as jnp
from jax import lax
import numpy as np

D_MODEL = 1024
BATCH = 1
SEQ = 256
DEPTH = 1

N_META = 16
BLOCK_Q = 128
EPS = 1e-6
NEG_INF = -1e30

SSM_WIDTH = D_MODEL // 2
SSM_GROUP = 16
SSM_GROUPS = SSM_WIDTH // SSM_GROUP
SSM_STATE = 64
DT_MIN = 1e-3
DT_MAX = 1e-1

ATT_HEADS = 4
QK_DIM = 64
V_DIM = 2 * QK_DIM
ATT_WIDTH = ATT_HEADS * V_DIM
QK_COLS = ATT_HEADS * 2 * QK_DIM

IN_COLS = SSM_WIDTH + 2 * QK_COLS + ATT_WIDTH + 2 * D_MODEL
SPLITS = (SSM_WIDTH,
          SSM_WIDTH + QK_COLS,
          SSM_WIDTH + 2 * QK_COLS,
          SSM_WIDTH + 2 * QK_COLS + ATT_WIDTH,
          SSM_WIDTH + 2 * QK_COLS + ATT_WIDTH + D_MODEL)

D_FF = ((8 * D_MODEL // 3 + 127) // 128) * 128
CONV_W = 3


def rmsnorm(x, g):
    xf = x.astype(jnp.float32)
    r = lax.rsqrt(jnp.mean(xf * xf, axis=-1, keepdims=True) + EPS)
    return (xf * r).astype(x.dtype) * g

def s5_mixer(u, a_re, a_im, log_dt, b_re, b_im, c_re, c_im, d, glu_w, glu_b):
    bsz, seq_len, _ = u.shape
    ug = u.astype(jnp.float32).reshape(bsz, seq_len, SSM_GROUPS, SSM_GROUP)
    a_re = a_re.astype(jnp.float32); a_im = a_im.astype(jnp.float32)
    dt = jnp.exp(log_dt.astype(jnp.float32))[:, None]
    mag = jnp.exp(a_re * dt)
    lb_re = mag * jnp.cos(a_im * dt)
    lb_im = mag * jnp.sin(a_im * dt)
    den = a_re * a_re + a_im * a_im
    n_re = lb_re - 1.0
    f_re = (n_re * a_re + lb_im * a_im) / den
    f_im = (lb_im * a_re - n_re * a_im) / den
    b_re = b_re.astype(jnp.float32); b_im = b_im.astype(jnp.float32)
    bb_re = f_re[..., None] * b_re - f_im[..., None] * b_im
    bb_im = f_re[..., None] * b_im + f_im[..., None] * b_re
    x_re = jnp.einsum('blgc,gpc->blgp', ug, bb_re)
    x_im = jnp.einsum('blgc,gpc->blgp', ug, bb_im)
    shp = (1, seq_len, SSM_GROUPS, SSM_STATE)
    a_re_t = jnp.broadcast_to(lb_re, shp)
    a_im_t = jnp.broadcast_to(lb_im, shp)

    def combine(left, right):
        ar_l, ai_l, br_l, bi_l = left
        ar_r, ai_r, br_r, bi_r = right
        return (ar_r * ar_l - ai_r * ai_l,
                ar_r * ai_l + ai_r * ar_l,
                ar_r * br_l - ai_r * bi_l + br_r,
                ar_r * bi_l + ai_r * br_l + bi_r)

    _, _, s_re, s_im = lax.associative_scan(combine, (a_re_t, a_im_t, x_re, x_im), axis=1)
    y = (jnp.einsum('blgp,gcp->blgc', s_re, c_re.astype(jnp.float32))
         - jnp.einsum('blgp,gcp->blgc', s_im, c_im.astype(jnp.float32))
         + d.astype(jnp.float32) * ug)
    y = jax.nn.gelu(y.reshape(bsz, seq_len, SSM_WIDTH)).astype(u.dtype)
    return y * jax.nn.sigmoid(y @ glu_w + glu_b)

def diff_attention(q, k, v, lam, slopes):
    bsz, seq_len = q.shape[:2]
    nb = seq_len // BLOCK_Q
    qb = jnp.moveaxis(q.reshape(bsz, nb, BLOCK_Q, ATT_HEADS, 2, QK_DIM), 1, 0)
    starts = jnp.arange(nb, dtype=jnp.int32) * BLOCK_Q
    kpos = jnp.arange(seq_len, dtype=jnp.int32)

    def one_block(args):
        q_blk, start = args
        s = jnp.einsum('bqhjd,bkhjd->bhjqk', q_blk, k,
                       preferred_element_type=jnp.float32)
        dist = (start + jnp.arange(BLOCK_Q, dtype=jnp.int32))[:, None] - kpos[None, :]
        s = s - slopes[None, :, None, None, None] * dist.astype(jnp.float32)[None, None, None]
        s = jnp.where(dist[None, None, None] >= 0, s, NEG_INF)
        p = jax.nn.softmax(s, axis=-1)
        w = p[:, :, 0] - lam * p[:, :, 1]
        return jnp.einsum('bhqk,bkhe->bqhe', w.astype(v.dtype), v)

    o = lax.map(one_block, (qb, starts))
    return jnp.moveaxis(o, 0, 1).reshape(bsz, seq_len, ATT_HEADS, V_DIM)

def conv_glu_ffn(h, w_up, conv_w, conv_b, w_down):
    seq_len = h.shape[1]
    up = h @ w_up
    a, b = up[..., :D_FF], up[..., D_FF:]
    a_pad = jnp.pad(a, ((0, 0), (CONV_W - 1, 0), (0, 0)))
    c = (a_pad[:, 0:seq_len] * conv_w[0] + a_pad[:, 1:seq_len + 1] * conv_w[1]
         + a_pad[:, 2:seq_len + 2] * conv_w[2] + conv_b)
    return (jax.nn.gelu(c) * b) @ w_down

def first_inputs(seed: int = 0) -> dict:
    key = jax.random.key(seed)
    ks = jax.random.split(key, 32)
    f32 = jnp.float32
    nrm = lambda k, shp, s: s * jax.random.normal(k, shp, f32)
    L_ = DEPTH
    return {
        'x': jax.random.normal(ks[0], (BATCH, SEQ, D_MODEL), f32),
        'meta_tokens': nrm(ks[1], (N_META, D_MODEL), 1.0),
        'norm1_g': 1.0 + nrm(ks[2], (L_, D_MODEL), 0.02),
        'w_in': nrm(ks[3], (L_, D_MODEL, IN_COLS), D_MODEL ** -0.5),
        'ssm_a_re': -0.5 + nrm(ks[4], (L_, SSM_GROUPS, SSM_STATE), 0.01),
        'ssm_a_im': math.pi * jnp.arange(SSM_STATE, dtype=f32)[None, None, :]
                    + nrm(ks[5], (L_, SSM_GROUPS, SSM_STATE), 0.01),
        'ssm_log_dt': jax.random.uniform(ks[6], (L_, SSM_GROUPS), f32,
                                         math.log(DT_MIN), math.log(DT_MAX)),
        'ssm_b_re': nrm(ks[7], (L_, SSM_GROUPS, SSM_STATE, SSM_GROUP), (2 * SSM_GROUP) ** -0.5),
        'ssm_b_im': nrm(ks[8], (L_, SSM_GROUPS, SSM_STATE, SSM_GROUP), (2 * SSM_GROUP) ** -0.5),
        'ssm_c_re': nrm(ks[9], (L_, SSM_GROUPS, SSM_GROUP, SSM_STATE), (2 * SSM_STATE) ** -0.5),
        'ssm_c_im': nrm(ks[10], (L_, SSM_GROUPS, SSM_GROUP, SSM_STATE), (2 * SSM_STATE) ** -0.5),
        'ssm_d': nrm(ks[11], (L_, SSM_GROUPS, SSM_GROUP), 1.0),
        'ssm_glu_w': nrm(ks[12], (L_, SSM_WIDTH, SSM_WIDTH), SSM_WIDTH ** -0.5),
        'ssm_glu_b': nrm(ks[13], (L_, SSM_WIDTH), 0.01),
        'q_norm_g': 1.0 + nrm(ks[14], (L_, QK_DIM), 0.02),
        'k_norm_g': 1.0 + nrm(ks[15], (L_, QK_DIM), 0.02),
        'lam_q1': nrm(ks[16], (L_, QK_DIM), 0.1),
        'lam_k1': nrm(ks[17], (L_, QK_DIM), 0.1),
        'lam_q2': nrm(ks[18], (L_, QK_DIM), 0.1),
        'lam_k2': nrm(ks[19], (L_, QK_DIM), 0.1),
        'subln_g': 1.0 + nrm(ks[20], (L_, V_DIM), 0.02),
        'w_ssm_out': nrm(ks[21], (L_, SSM_WIDTH, D_MODEL), SSM_WIDTH ** -0.5),
        'w_att_out': nrm(ks[22], (L_, ATT_WIDTH, D_MODEL), ATT_WIDTH ** -0.5),
        'w_o': nrm(ks[23], (L_, D_MODEL, D_MODEL), D_MODEL ** -0.5),
        'norm2_g': 1.0 + nrm(ks[24], (L_, D_MODEL), 0.02),
        'w_up': nrm(ks[25], (L_, D_MODEL, 2 * D_FF), D_MODEL ** -0.5),
        'conv_w': nrm(ks[26], (L_, CONV_W, D_FF), CONV_W ** -0.5),
        'conv_b': nrm(ks[27], (L_, D_FF), 0.01),
        'w_down': nrm(ks[28], (L_, D_FF, D_MODEL), D_FF ** -0.5),
    }

def first_block(x, meta_tokens, norm1_g, w_in, ssm_a_re, ssm_a_im, ssm_log_dt, ssm_b_re, ssm_b_im,
              ssm_c_re, ssm_c_im, ssm_d, ssm_glu_w, ssm_glu_b, q_norm_g, k_norm_g,
              lam_q1, lam_k1, lam_q2, lam_k2, subln_g, w_ssm_out, w_att_out, w_o,
              norm2_g, w_up, conv_w, conv_b, w_down):
    bsz, seq, _ = x.shape
    seq_len = seq + N_META
    seq_pad = -(-seq_len // BLOCK_Q) * BLOCK_Q
    meta = jnp.broadcast_to(meta_tokens[None].astype(x.dtype), (bsz, N_META, D_MODEL))
    h = jnp.concatenate([meta, x, jnp.zeros((bsz, seq_pad - seq_len, D_MODEL), x.dtype)], axis=1)
    slopes = 2.0 ** (-8.0 * jnp.arange(1, ATT_HEADS + 1, dtype=jnp.float32) / ATT_HEADS)
    q_scale = QK_DIM ** -0.5

    for l in range(DEPTH):
        lam_init = 0.8 - 0.6 * math.exp(-0.3 * l)
        hn = rmsnorm(h, norm1_g[l])
        proj = hn @ w_in[l]
        u, q, k, v, g_ssm, g_att = jnp.split(proj, SPLITS, axis=-1)
        y_ssm = s5_mixer(u, ssm_a_re[l], ssm_a_im[l], ssm_log_dt[l], ssm_b_re[l], ssm_b_im[l],
                         ssm_c_re[l], ssm_c_im[l], ssm_d[l], ssm_glu_w[l], ssm_glu_b[l])
        q = rmsnorm(q.reshape(bsz, seq_pad, ATT_HEADS, 2, QK_DIM), q_norm_g[l]) * q_scale
        k = rmsnorm(k.reshape(bsz, seq_pad, ATT_HEADS, 2, QK_DIM), k_norm_g[l])
        v = v.reshape(bsz, seq_pad, ATT_HEADS, V_DIM)
        lam = (jnp.exp(jnp.sum(lam_q1[l] * lam_k1[l]).astype(jnp.float32))
               - jnp.exp(jnp.sum(lam_q2[l] * lam_k2[l]).astype(jnp.float32)) + lam_init)
        o = diff_attention(q, k, v, lam, slopes)
        y_att = (rmsnorm(o, subln_g[l]) * (1.0 - lam_init)).reshape(bsz, seq_pad, ATT_WIDTH)
        mixed = (jax.nn.sigmoid(g_ssm) * (y_ssm @ w_ssm_out[l])
                 + jax.nn.sigmoid(g_att) * (y_att @ w_att_out[l]))
        h = h + mixed @ w_o[l]
        h = h + conv_glu_ffn(rmsnorm(h, norm2_g[l]), w_up[l], conv_w[l], conv_b[l], w_down[l])

    return h[:, N_META:N_META + seq]


D_MIX = D_MODEL
LRU_WIDTH = D_MIX // 4
LRU_BLOCKS = 4
LRU_CONV = 4
LRU_C = 8.0
HG_HEADS = 4
HG_DK = 64
HG_DV = 64
HG_CHUNK = 64
ATT_HEADS_2 = 8
ATT_HD = 64
MOBA_BLOCK = 256
MOBA_TOPK = 3
Q_BLOCK = 64
D_FF_2 = 4 * D_MODEL
NEG = -1e30
TINY = 1e-30

SPLITS_2 = (LRU_WIDTH, LRU_WIDTH,
          HG_HEADS * HG_DK, HG_HEADS * HG_DK, HG_HEADS * HG_DV, HG_HEADS * HG_DV,
          ATT_HEADS_2 * ATT_HD, ATT_HEADS_2 * ATT_HD, ATT_HEADS_2 * ATT_HD)
D_IN = sum(SPLITS_2)
D_OUT_CAT = LRU_WIDTH + HG_HEADS * HG_DV + ATT_HEADS_2 * ATT_HD


def rms_norm(x, g):
    xf = x.astype(jnp.float32)
    y = xf * lax.rsqrt(jnp.mean(xf * xf, axis=-1, keepdims=True) + EPS)
    return (y * g.astype(jnp.float32)).astype(x.dtype)

def rglru_group(xb, yb, conv_w, conv_b, wa, ba, wx, bx, lam):
    Bn, S, W = xb.shape
    xc = lax.conv_general_dilated(
        xb, conv_w.reshape(LRU_CONV, 1, W).astype(xb.dtype), window_strides=(1,),
        padding=[(LRU_CONV - 1, 0)], dimension_numbers=('NWC', 'WIO', 'NWC'),
        feature_group_count=W) + conv_b.astype(xb.dtype)
    xg = xc.reshape(Bn, S, LRU_BLOCKS, W // LRU_BLOCKS)
    r = jax.nn.sigmoid(jnp.einsum('bsgi,gij->bsgj', xg, wa).reshape(Bn, S, W).astype(jnp.float32)
                       + ba.astype(jnp.float32))
    i = jax.nn.sigmoid(jnp.einsum('bsgi,gij->bsgj', xg, wx).reshape(Bn, S, W).astype(jnp.float32)
                       + bx.astype(jnp.float32))
    log_a = -LRU_C * r * jax.nn.softplus(-lam.astype(jnp.float32))
    a = jnp.exp(log_a)
    u = jnp.sqrt(-jnp.expm1(2.0 * log_a)) * (i * xc.astype(jnp.float32))

    def combine(c1, c2):
        a1, b1 = c1
        a2, b2 = c2
        return a1 * a2, a2 * b1 + b2

    _, h = lax.associative_scan(combine, (a, u), axis=1)
    return (h * jax.nn.gelu(yb.astype(jnp.float32))).astype(xb.dtype)

def hgrn2_group(q, f, i, g, lb, norm_w):
    Bn, S, _ = q.shape
    nc = S // HG_CHUNK
    lb = lb.astype(jnp.float32)
    fpre = f.astype(jnp.float32)
    log_f = jnp.logaddexp(jnp.log(jnp.maximum(lb, TINY)), jnp.log1p(-lb) + jax.nn.log_sigmoid(fpre))
    k = (1.0 - lb) * jax.nn.sigmoid(-fpre)
    qs = jax.nn.silu(q.astype(jnp.float32))

    def heads(t, d):
        return t.astype(jnp.float32).reshape(Bn, nc, HG_CHUNK, HG_HEADS, d).transpose(1, 0, 3, 2, 4)

    qh, kh, lfh, vh = heads(qs, HG_DK), heads(k, HG_DK), heads(log_f, HG_DK), heads(i, HG_DV)
    mask = jnp.tril(jnp.ones((HG_CHUNK, HG_CHUNK), dtype=bool))

    def step(state, inp):
        qc, kc, lfc, vc = inp
        b = jnp.cumsum(lfc, axis=2)
        diff = b[:, :, :, None, :] - b[:, :, None, :, :]
        decay = jnp.exp(jnp.where(mask[:, :, None], diff, NEG))
        att = jnp.einsum('bhtd,bhsd,bhtsd->bhts', qc, kc, decay)
        o = jnp.einsum('bhts,bhse->bhte', att, vc) + jnp.einsum('bhtd,bhde->bhte', qc * jnp.exp(b), state)
        b_last = b[:, :, -1:, :]
        new_state = jnp.exp(b_last[:, :, 0, :])[..., None] * state + \
            jnp.einsum('bhsd,bhse->bhde', kc * jnp.exp(b_last - b), vc)
        return new_state, o

    s0 = jnp.zeros((Bn, HG_HEADS, HG_DK, HG_DV), jnp.float32)
    _, o = lax.scan(step, s0, (qh, kh, lfh, vh))
    o = o.transpose(1, 0, 3, 2, 4).reshape(Bn, S, HG_HEADS, HG_DV)
    o = rms_norm(o, norm_w) * jax.nn.silu(g.reshape(Bn, S, HG_HEADS, HG_DV).astype(jnp.float32))
    return o.reshape(Bn, S, HG_HEADS * HG_DV).astype(q.dtype)

def moba_group(cq, ck, cv):
    Bn, S, _ = cq.shape
    H, hd = ATT_HEADS_2, ATT_HD
    s_pad = -(-S // MOBA_BLOCK) * MOBA_BLOCK
    pad = s_pad - S

    def heads(t):
        t = t.reshape(Bn, S, H, hd).transpose(0, 2, 1, 3)
        return jnp.pad(t, ((0, 0), (0, 0), (0, pad), (0, 0)))

    q, k, v = heads(cq), heads(ck), heads(cv)
    nblk = s_pad // MOBA_BLOCK
    topk = min(MOBA_TOPK, nblk)
    kb = k.reshape(Bn, H, nblk, MOBA_BLOCK, hd)
    vb = v.reshape(Bn, H, nblk, MOBA_BLOCK, hd)
    kmean = jnp.mean(kb.astype(jnp.float32), axis=3).astype(k.dtype)
    scale = 1.0 / math.sqrt(hd)
    slopes = jnp.asarray(2.0 ** (-8.0 * np.arange(1, H + 1) / H), dtype=jnp.float32)
    nq = s_pad // Q_BLOCK
    qs = q.reshape(Bn, H, nq, Q_BLOCK, hd).transpose(2, 0, 1, 3, 4)
    bi = jnp.arange(Bn)[:, None, None, None]
    hi = jnp.arange(H)[None, :, None, None]
    blk_pos = jnp.arange(MOBA_BLOCK)

    def step(args):
        qi, q_blk = args
        t = qi * Q_BLOCK + jnp.arange(Q_BLOCK)
        j = (qi * Q_BLOCK) // MOBA_BLOCK
        gate = jnp.einsum('bhqd,bhnd->bhqn', q_blk, kmean).astype(jnp.float32)
        gate = jnp.where(jnp.arange(nblk) < j, gate, NEG)
        _, sel = lax.top_k(gate, topk)
        valid = jnp.arange(topk) < j
        ksel = kb[bi, hi, sel]
        vsel = vb[bi, hi, sel]
        s_sel = jnp.einsum('bhqd,bhqkld->bhqkl', q_blk, ksel).astype(jnp.float32) * scale
        pos_sel = sel[..., None] * MOBA_BLOCK + blk_pos
        s_sel = s_sel - slopes[:, None, None, None] * (t[:, None, None] - pos_sel).astype(jnp.float32)
        s_sel = jnp.where(valid[:, None], s_sel, NEG)
        k_own = lax.dynamic_slice_in_dim(kb, j, 1, axis=2)[:, :, 0]
        v_own = lax.dynamic_slice_in_dim(vb, j, 1, axis=2)[:, :, 0]
        s_own = jnp.einsum('bhqd,bhld->bhql', q_blk, k_own).astype(jnp.float32) * scale
        rel = t[:, None] - (j * MOBA_BLOCK + blk_pos)[None, :]
        s_own = jnp.where(rel >= 0, s_own - slopes[:, None, None] * rel.astype(jnp.float32), NEG)
        scores = jnp.concatenate([s_own, s_sel.reshape(Bn, H, Q_BLOCK, topk * MOBA_BLOCK)], axis=-1)
        p = jax.nn.softmax(scores, axis=-1).astype(v.dtype)
        p_own = p[..., :MOBA_BLOCK]
        p_sel = p[..., MOBA_BLOCK:].reshape(Bn, H, Q_BLOCK, topk, MOBA_BLOCK)
        out = jnp.einsum('bhql,bhld->bhqd', p_own, v_own) + jnp.einsum('bhqkl,bhqkld->bhqd', p_sel, vsel)
        return out.astype(v.dtype)

    o = lax.map(step, (jnp.arange(nq), qs))
    o = o.transpose(1, 2, 0, 3, 4).reshape(Bn, H, s_pad, hd)[:, :, :S]
    return o.transpose(0, 2, 1, 3).reshape(Bn, S, H * hd)

def second_inputs(seed: int = 0) -> dict:
    key = jax.random.key(seed)
    ks = jax.random.split(key, 20)
    f32 = jnp.float32
    L = DEPTH
    nrm = lambda k, shape, fan: jax.random.normal(k, shape, f32) * (fan ** -0.5)
    gain = lambda k, shape: 1.0 + 0.05 * jax.random.normal(k, shape, f32)
    bw = LRU_WIDTH // LRU_BLOCKS
    u = jax.random.uniform(ks[10], (L, LRU_WIDTH), f32, 0.9, 0.999)
    a_base = u ** (1.0 / LRU_C)
    lam = jnp.log(a_base) - jnp.log1p(-a_base)
    return {
        "x": jax.random.normal(ks[0], (BATCH, SEQ, D_MODEL), f32),
        "w_in": nrm(ks[1], (L, D_MODEL, D_IN), D_MODEL),
        "w_out": nrm(ks[2], (L, D_OUT_CAT, D_MODEL), D_OUT_CAT),
        "norm_mix": gain(ks[3], (L, D_MODEL)),
        "norm_mlp": gain(ks[4], (L, D_MODEL)),
        "lru_conv_w": nrm(ks[5], (L, LRU_CONV, LRU_WIDTH), LRU_CONV),
        "lru_conv_b": 0.01 * jax.random.normal(ks[6], (L, LRU_WIDTH), f32),
        "lru_wa": nrm(ks[7], (L, LRU_BLOCKS, bw, bw), bw),
        "lru_ba": 0.01 * jax.random.normal(ks[8], (L, LRU_WIDTH), f32),
        "lru_wx": nrm(ks[9], (L, LRU_BLOCKS, bw, bw), bw),
        "lru_bx": 0.01 * jax.random.normal(ks[11], (L, LRU_WIDTH), f32),
        "lru_lambda": lam,
        "hg_lower_bounds": 0.1 * jax.random.normal(ks[12], (L, HG_HEADS * HG_DK), f32),
        "hg_norm_w": gain(ks[13], (L, HG_DV)),
        "lru_out_norm": gain(ks[14], (L, LRU_WIDTH)),
        "att_out_norm": gain(ks[15], (L, ATT_HEADS_2 * ATT_HD)),
        "w_ff1": nrm(ks[16], (L, D_MODEL, D_FF_2), D_MODEL),
        "w_ff2": nrm(ks[17], (L, D_FF_2, D_MODEL), D_FF_2),
        "norm_final": gain(ks[18], (D_MODEL,)),
    }

def second_block(x, w_in, w_out, norm_mix, norm_mlp, lru_conv_w, lru_conv_b, lru_wa, lru_ba, lru_wx, lru_bx,
              lru_lambda, hg_lower_bounds, hg_norm_w, lru_out_norm, att_out_norm, w_ff1, w_ff2, norm_final):
    lb_soft = jax.nn.softmax(hg_lower_bounds.astype(jnp.float32), axis=0)
    lower_bounds = jnp.cumsum(lb_soft, axis=0) - lb_soft[0]
    split_at = np.cumsum(SPLITS_2)[:-1].tolist()
    for l in range(DEPTH):
        h = rms_norm(x, norm_mix[l])
        z = jnp.einsum('bsd,de->bse', h, w_in[l])
        a_x, a_y, b_q, b_f, b_i, b_g, c_q, c_k, c_v = jnp.split(z, split_at, axis=-1)
        ya = rglru_group(a_x, a_y, lru_conv_w[l], lru_conv_b[l], lru_wa[l], lru_ba[l],
                         lru_wx[l], lru_bx[l], lru_lambda[l])
        yb = hgrn2_group(b_q, b_f, b_i, b_g, lower_bounds[l], hg_norm_w[l])
        yc = moba_group(c_q, c_k, c_v)
        y = jnp.concatenate([rms_norm(ya, lru_out_norm[l]), yb.astype(x.dtype),
                             rms_norm(yc, att_out_norm[l])], axis=-1)
        x = x + jnp.einsum('bse,ed->bsd', y, w_out[l])
        h = rms_norm(x, norm_mlp[l])
        u = jnp.square(jax.nn.relu(jnp.einsum('bsd,df->bsf', h, w_ff1[l])))
        x = x + jnp.einsum('bsf,fd->bsd', u, w_ff2[l])
    return rms_norm(x, norm_final)


def setup_inputs(seed=0):
    out = dict(first_inputs(seed))
    for name, value in second_inputs(seed + 1).items():
        if name != "x":
            out[name + "_2"] = value
    return out


def reference(
    x, meta_tokens, norm1_g, w_in, ssm_a_re, ssm_a_im, ssm_log_dt, ssm_b_re, ssm_b_im, ssm_c_re,
    ssm_c_im, ssm_d, ssm_glu_w, ssm_glu_b, q_norm_g, k_norm_g, lam_q1, lam_k1, lam_q2, lam_k2,
    subln_g, w_ssm_out, w_att_out, w_o, norm2_g, w_up, conv_w, conv_b, w_down, w_in_2, w_out_2,
    norm_mix_2, norm_mlp_2, lru_conv_w_2, lru_conv_b_2, lru_wa_2, lru_ba_2, lru_wx_2, lru_bx_2,
    lru_lambda_2, hg_lower_bounds_2, hg_norm_w_2, lru_out_norm_2, att_out_norm_2, w_ff1_2,
    w_ff2_2, norm_final_2,
):
    x = first_block(
        x, meta_tokens, norm1_g, w_in, ssm_a_re, ssm_a_im, ssm_log_dt, ssm_b_re, ssm_b_im,
        ssm_c_re, ssm_c_im, ssm_d, ssm_glu_w, ssm_glu_b, q_norm_g, k_norm_g, lam_q1, lam_k1,
        lam_q2, lam_k2, subln_g, w_ssm_out, w_att_out, w_o, norm2_g, w_up, conv_w, conv_b,
        w_down,
    )
    return second_block(
        x, w_in_2, w_out_2, norm_mix_2, norm_mlp_2, lru_conv_w_2, lru_conv_b_2, lru_wa_2,
        lru_ba_2, lru_wx_2, lru_bx_2, lru_lambda_2, hg_lower_bounds_2, hg_norm_w_2,
        lru_out_norm_2, att_out_norm_2, w_ff1_2, w_ff2_2, norm_final_2,
    )


_drawn_inputs = setup_inputs


def setup_inputs(seed=0):
    import zlib

    import numpy as np

    out = dict(_drawn_inputs(seed))
    spreads = {}
    factors = {'norm1_g': 2.818,
     'ssm_a_re': 64.0,
     'ssm_a_im': 32.152,
     'ssm_log_dt': 32.416,
     'ssm_b_re': 44.264,
     'ssm_b_im': 44.672,
     'ssm_c_re': 44.368,
     'ssm_c_im': 44.2,
     'ssm_glu_b': 47.66,
     'q_norm_g': 5.911,
     'k_norm_g': 6.143,
     'subln_g': 4.968,
     'norm2_g': 3.234,
     'conv_b': 8.0,
     'lru_conv_b_2': 3.26,
     'lru_ba_2': 64.0,
     'lru_bx_2': 64.0,
     'hg_norm_w_2': 34.562,
     'lru_out_norm_2': 19.247,
     'norm_mlp_2': 6.816,
     'att_out_norm_2': 25.453}
    for name, (base, spread) in spreads.items():
        noise = np.random.default_rng([zlib.crc32(name.encode()), seed]).standard_normal(out[name].shape)
        drawn = base * np.exp(spread * noise) if base else spread * noise
        out[name] = __import__('jax').numpy.asarray(drawn.astype(out[name].dtype))
    for name, factor in factors.items():
        out[name] = (out[name] * factor).astype(out[name].dtype)
    return out
```

```python
import concourse.bass as bass
from concourse import mybir
from contextlib import ExitStack

F32 = mybir.dt.float32
F32R = mybir.dt.float32r
I32 = mybir.dt.int32
ALU = mybir.AluOpType
ACT = mybir.ActivationFunctionType
AXX = mybir.AxisListType.X

P = 128
D = 1024
KD = D // P
META = 16
SEQ = 256
TOK = META + SEQ
T0 = META - 2
NQ = TOK - T0
FF = 2816
KF = FF // P
FF2 = 4 * D
KF2 = FF2 // P
NS = 16
LC = TOK // 2
EPS = 1e-6
BIG = 1e30 * 256.0
TINY = 1e-30
SQRT_MIN = 2.0 ** -110
TWO_PI_1 = 6.28125
TWO_PI_2 = 0.0019350051879882812
TWO_PI_3 = 3.0198120544e-07
INV_TWO_PI = 0.15915494309189535
ROUND = 12582912.0
NRAW, NW = 3, 3
UNIT = 2048
CONSTANTS = {"ident": 1, "small": 2, "ones": 3, "half": 4, "sel": 5, "bias": 6, "masks": 7}
NM = 3
NB = 3
KEYS_B = META + P

POOL_LO = range(3, 21)
PROWS = {}
at_ = 0
for name_, n_ in (("norm1", 8), ("a_re", 16), ("a_im", 16), ("ssm_d", 4), ("glu_b", 4), ("qn", 1), ("kn", 1),
                  ("subln", 1), ("norm2", 8), ("conv_b", 22), ("norm_mix", 8), ("norm_mlp", 8), ("att_norm", 4),
                  ("lru_norm", 2), ("hg_norm", 1)):
    PROWS[name_] = at_
    at_ += n_
NP1 = at_
PROWS2 = {}
at_ = 0
for name_, n_ in (("conv_w", 66), ("lru_w", 8), ("lru_b", 2), ("lru_ba", 2), ("lru_bx", 2), ("lru_lam", 2),
                  ("hg_lb", 2)):
    PROWS2[name_] = at_
    at_ += n_
NP2 = at_
PTILES = [(0, 8), (8, 36), (44, NP1 - 44), (0, NP2)]


def weight_units(ins):
    def rows(w):
        return w.rearrange("(k p) n -> p k n", p=P)
    units = []

    def add(name, src, kk, kind, groups):
        units.append(dict(name=name, src=src, kk=kk, kind=kind, groups=groups))

    w_in = rows(ins["w_in"][0])
    for name, c0 in (("u", 0), ("k", 1024), ("q", 512)):
        for i in range(2):
            add((name, i), w_in[:, :, c0 + 256 * i:c0 + 256 * i + 256], 8, "feat", 2)
    for i in range(2):
        add(("v", i), w_in[:, :, 1536 + 256 * i:1792 + 256 * i], 8, "tok", 3)
    for i in range(8):
        add(("gate", i), w_in[:, :, 2048 + 256 * i:2304 + 256 * i], 8, "feat", 2)
    add(("glu", 0), rows(ins["ssm_glu_w"][0]), 4, "feat", 4)
    for name, key in (("ssm_out", "w_ssm_out"), ("att_out", "w_att_out")):
        for i in range(2):
            add((name, i), rows(ins[key][0])[:, :, 512 * i:512 * i + 512], 4, "feat", 4)
    for i in range(4):
        add(("w_o", i), rows(ins["w_o"][0])[:, :, 256 * i:256 * i + 256], 8, "feat", 2)
    w_up, w_down = rows(ins["w_up"][0]), rows(ins["w_down"][0])
    for i in range(KF // 2 + 1):
        if i < KF // 2:
            add(("up_a", i), w_up[:, :, 256 * i:256 * i + 256], 8, "feat", 2)
            add(("up_b", i), w_up[:, :, FF + 256 * i:FF + 256 * i + 256], 8, "feat", 2)
        if i:
            add(("down", i - 1), w_down[:, 2 * i - 2:2 * i, :], 2, "acc", 0)
    w2 = rows(ins["w_in_2"][0])
    for name, c0, n in (("lru_x", 0, 1), ("hg_f", 768, 1), ("hg_q", 512, 1), ("hg_i", 1024, 1), ("cq", 1536, 2),
                        ("ck", 2048, 2), ("cv", 2560, 2), ("hg_g", 1280, 1), ("lru_y", 256, 1)):
        for i in range(n):
            tok = name in ("hg_i", "cv")
            add((name, i), w2[:, :, c0 + 256 * i:c0 + 256 * i + 256], 8, "tok" if tok else "feat", 2)
    for i in range(4):
        add(("w_out2", i), rows(ins["w_out_2"][0])[:, :, 256 * i:256 * i + 256], 8, "feat", 2)
    w_ff1, w_ff2 = rows(ins["w_ff1_2"][0]), rows(ins["w_ff2_2"][0])
    for i in range(KF2 // 2 + 1):
        if i < KF2 // 2:
            add(("ff1", i), w_ff1[:, :, 256 * i:256 * i + 256], 8, "feat", 2)
        if i:
            add(("ff2", i - 1), w_ff2[:, 2 * i - 2:2 * i, :], 2, "acc", 0)
    g = a = 0
    for n, u in enumerate(units):
        u["n"], u["g0"] = n, g
        g += u["groups"]
        a += u["kind"] == "acc"
        u["acc_done"] = a
    return units


def program(nc, ins, out):
    ctx = ExitStack()
    with ctx:
        sems = {}

        def sem(name):
            if name not in sems:
                sems[name] = ctx.enter_context(nc.semaphore(name))
            return sems[name]

        base = 16512
        top = [base]

        def sb(name, shape, dt=F32, at=None):
            size = 4
            for n in shape[1:]:
                size *= n
            size = (size + 31) // 32 * 32
            if at is None:
                at = top[0]
                top[0] += size
            assert at + size <= 229344, name
            return nc.alloc_sbuf_tensor_at(name, list(shape), dt, offset=at)

        units = weight_units(ins)
        unit_at = {u["name"]: u for u in units}

        raw = sb("w_raw", [P, NRAW, UNIT])
        w_hi = sb("w_hi", [P, NW, UNIT], F32R)
        w_lo = sb("w_lo", [P, NW, UNIT], F32R)
        ident = sb("ident", [P, P])
        ones = sb("ones", [P, P])
        sel = sb("sel", [P, 8, 16])
        selT = sb("selT", [16, 8, P])
        selH = sb("selH", [P, 4, 4])
        selHT = sb("selHT", [4, 4, P])
        C1 = sb("C1", [P, NP1])
        C2 = sb("C2", [P, NP2])
        neg_dist = sb("neg_dist", [P, 272])
        bias = sb("bias", [P, 8, 272])
        small = sb("small", [P, 86, 16])
        R = top[0]
        k = lambda off: R + off

        def col(name, i=0, n=1):
            if name in PROWS:
                return C1[:, PROWS[name] + i:PROWS[name] + i + n]
            return C2[:, PROWS2[name] + i:PROWS2[name] + i + n]

        xn_hi = sb("xn_hi", [P, KD, TOK], F32R, k(0))
        xn_lo = sb("xn_lo", [P, KD, TOK], F32R, k(8704))
        mix_hi = sb("mix_hi", [P, KD, NQ], F32R, k(0))
        mix_lo = sb("mix_lo", [P, KD, NQ], F32R, k(8704))
        hT = sb("hT", [P, KD, NQ], F32, k(17408))
        xtok = sb("xtok", [P, 3, D], F32, k(25664))
        yg = sb("yg", [P, 4, TOK], F32, k(25664))
        yg_hi = sb("yg_hi", [P, 4, NQ], F32R, k(30016))
        yg_lo = sb("yg_lo", [P, 4, NQ], F32R, k(34144))
        uT = sb("uT", [P, 4, TOK], F32, k(38272))
        qkT = sb("qkT", [P, 8, TOK], F32, k(42624))
        v_tok = sb("v_tok", [P, 3, 512], F32, k(51328))
        Ec = sb("Ec", [P, NS, LC], F32, k(57472))
        Es = sb("Es", [P, NS, LC], F32, k(66176))
        mprod = sb("mprod", [P, NM, 4, 2 * LC], F32, k(74880))
        zbuf = sb("zbuf", [P, 2, 2 * LC], F32, k(87936))
        xr = sb("xr", [P, 3, D], F32, k(74880))
        BT = sb("BT", [P, 4, 2, P], F32, k(90112))
        CT = sb("CT", [P, 4, 2, P], F32, k(94208))
        gate = sb("gate", [P, 16, NQ], F32, k(98304))
        b_raw = sb("b_raw", [P, 2, NS, 16], F32, k(98304))
        b_prod = sb("b_prod", [P, 4, NS, 16], F32, k(100352))
        b_blk = sb("b_blk", [P, 2, NS, 2, 16], F32, k(104448))
        c_raw = sb("c_raw", [P, 2, 4, 64], F32, k(108544))
        c_blk = sb("c_blk", [P, 2, 4, 2, 64], F32, k(110592))
        lamv = sb("lamv", [P, 4, 64], F32, k(53504))
        params = sb("params", [P, 4, P], F32, k(51328))
        log_dt = sb("log_dt", [P, 32], F32, k(53376))
        junk_x = sb("junk_x", [P, D], F32, k(57472))
        e_tmp = sb("e_tmp", [P, 2, NS, 64], F32, k(74880))
        glu_t = sb("glu_t", [P, 4, NQ], F32, k(38272))
        eps_col = small[:, 83, 0:1]
        A0 = 57472
        p_a = sb("p_a", [P, 2, TOK], F32, k(A0))
        p_b = sb("p_b", [P, 2, 2, KEYS_B], F32, k(A0 + 2176))
        w_a = sb("w_a", [P, TOK], F32, k(A0 + 4480))
        w_b = sb("w_b", [P, 2, KEYS_B], F32, k(A0 + 5568))
        wT0 = sb("wT0", [16, TOK], F32, k(A0 + 6720))
        wT12 = sb("wT12", [P, 384], F32, k(A0 + 7808))
        oT = sb("oT", [P, 4, TOK], F32, k(A0 + 9344))
        yatt_hi = sb("yatt_hi", [P, 4, NQ], F32R, k(A0 + 13696))
        yatt_lo = sb("yatt_lo", [P, 4, NQ], F32R, k(A0 + 17824))
        sq = sb("sq", [P, 2, TOK], F32, k(A0 + 21952))
        rs = sb("rs", [16, TOK], F32, k(A0 + 24128))
        rs2 = sb("rs2", [4, TOK], F32, k(A0 + 25216))
        junk = sb("junk", [P, 2, TOK], F32, k(A0 + 26304))
        rstd = sb("rstd", [P, NQ], F32, k(A0 + 28480))
        hs_hi = sb("hs_hi", [P, KD, NQ], F32R, k(98304))
        hs_lo = sb("hs_lo", [P, KD, NQ], F32R, k(106560))
        cv_ = sb("cv_", [P, 2, 2, 256], F32, k(A0))
        gl = sb("gl", [P, 2, 2, 256], F32, k(A0 + 4096))
        ff_hi = sb("ff_hi", [P, 2, 2, 256], F32R, k(A0 + 8192))
        ff_lo = sb("ff_lo", [P, 2, 2, 256], F32R, k(A0 + 12288))
        ff = sb("ff", [P, 2, 2, 256], F32, k(A0 + 16384))
        x2 = sb("x2", [P, KD, 256], F32, k(25664))

        x2n_hi = sb("x2n_hi", [P, KD, 256], F32R, k(0))
        x2n_lo = sb("x2n_lo", [P, KD, 256], F32R, k(8704))
        hgv = sb("hgv", [P, 2, 256], F32, k(17408))
        masks = sb("masks", [P, 8, P], F32, k(19456))
        hgg = sb("hgg", [P, 2, 256], F32, k(23552))
        ycat_hi = sb("ycat_hi", [P, KD, 256], F32R, k(33856))
        ycat_lo = sb("ycat_lo", [P, KD, 256], F32R, k(42048))
        xc = sb("xc", [P, 2, 256], F32, k(50240))
        lru_r = sb("lru_r", [P, 2, 256], F32, k(52288))
        lru_i = sb("lru_i", [P, 2, 256], F32, k(54336))
        lru_a = sb("lru_a", [P, 2, 256], F32, k(56384))
        lru_t = sb("lru_t", [P, 2, 256], F32, k(58432))
        lru_g = sb("lru_g", [P, 2, 256], F32, k(60480))
        hgq = sb("hgq", [P, 2, 256], F32, k(62528))
        hgk = sb("hgk", [P, 2, 256], F32, k(64576))
        hgf = sb("hgf", [P, 2, 256], F32, k(66624))
        hqf = sb("hqf", [P, 2, 256], F32, k(68672))
        htot = sb("htot", [P, 512], F32, k(70720))
        hA = sb("hA", [P, 8, P], F32, k(72768))
        hX = sb("hX", [P, 4, P], F32, k(76864))
        hgo = sb("hgo", [P, 2, 256], F32, k(78912))
        cq = sb("cq", [P, 4, 256], F32, k(80960))
        ck = sb("ck", [P, 4, 256], F32, k(85056))
        cv = sb("cv", [P, 2, 512], F32, k(89152))
        mp = sb("mp", [P, 2, 256], F32, k(93248))
        mpT = sb("mpT", [P, 2, 384], F32, k(95296))
        mo = sb("mo", [P, 4, 256], F32, k(98368))
        sq2 = sb("sq2", [P, 2, 256], F32, k(102464))
        rst2 = sb("rst2", [P, 256], F32, k(104512))
        rsm2 = sb("rsm2", [4, 256], F32, k(105536))
        tmp2 = sb("tmp2", [P, 2, 256], F32, k(106560))
        lru_w = sb("lru_w", [P, 2, 2, P], F32, k(108608))
        relu = sb("relu", [P, 2, 2, 256], F32, k(50240))
        uu = sb("uu", [P, 2, 2, 256], F32, k(54336))
        u_hi = sb("u_hi", [P, 2, 2, 256], F32R, k(58432))
        u_lo = sb("u_lo", [P, 2, 2, 256], F32R, k(62528))
        outb = sb("outb", [P, 2, D], F32, k(66624))
        nf = sb("nf", [P, D], F32, k(74816))
        sqj = sb("sqj", [P, 512], F32, k(78912))

        psum = ctx.enter_context(nc.psum_tensor("psum", [P, 8, 512], F32))
        banks = [psum[:, i, :] for i in range(8)]

        slot = {}

        def sm(name, n=16):
            if name not in slot:
                slot[name] = len(slot) + 2
            return small[:, slot[name], 0:n]

        def need(eng, name, n):
            if n > 0:
                eng.wait_ge(sem(name), n)

        def used(eng, n):
            if n < 0:
                return
            u = units[n]
            if u["kind"] == "acc":
                need(eng, "acc_unit_done", u["acc_done"])
            else:
                need(eng, "group_done", u["g0"] + u["groups"])

        def free_count(g):
            return g // NB

        def taken(eng, g):
            eng.wait_ge(sem(f"group_free{g % NB}"), free_count(g) + 1)

        def group(name, m):
            u = unit_at[name]
            return u["g0"] + m

        def par(eng, signal, dst, src):
            eng.dma_start(dst, src).then_inc(sem(signal), 16)

        def par_rows(eng, signal, tile, row, key):
            src = ins[key][0]
            if len(src.shape) == 2:
                src = src.rearrange("a b -> (a b)")
            cnt = src.shape[0] // P
            par(eng, signal, params[:, tile][row:row + cnt, :], src.rearrange("(r c) -> r c", c=P))

        block = ctx.enter_context(nc.Block())

        @block.sync
        def _(sp):
            x = ins["x"]
            sp.dma_start(xtok[0:META, 0, :], ins["meta_tokens"]).then_inc(sem("meta_in"), 16)
            for t in range(2):
                sp.dma_start(xtok[:, 1 + t, :], x[0, P * t:P * t + P, :]).then_inc(sem(f"x_in{t}"), 16)
            for u in units:
                n = u["n"]
                need(sp, "hi_ready", n - NRAW + 1)
                need(sp, "lo_ready", n - NRAW + 1)
                dst = raw[:, n % NRAW, :].rearrange("p (k n) -> p k n", k=u["kk"])
                sp.dma_start(dst, u["src"]).then_inc(sem(f"w_in{n % NRAW}"), 16)
                if n == NRAW - 1:
                    for name, key in (("glu_b", "ssm_glu_b"), ("norm2", "norm2_g"), ("conv_b", "conv_b"),
                                      ("subln", "subln_g"), ("norm_mix", "norm_mix_2"), ("norm_mlp", "norm_mlp_2"),
                                      ("att_norm", "att_out_norm_2"), ("lru_norm", "lru_out_norm_2")):
                        par_rows(sp, "par_in", 2, PROWS[name] - PROWS["glu_b"], key)
                    for name, key in (("qn", "q_norm_g"), ("kn", "k_norm_g"), ("hg_norm", "hg_norm_w_2")):
                        r = PROWS[name] - PROWS["glu_b"]
                        for j in range(2):
                            par(sp, "par_in", params[:, 2][r:r + 1, 64 * j:64 * j + 64], ins[key])
                    for name, key in (("conv_w", "conv_w"), ("lru_w", "lru_conv_w_2"), ("lru_b", "lru_conv_b_2"),
                                      ("lru_ba", "lru_ba_2"), ("lru_bx", "lru_bx_2"), ("lru_lam", "lru_lambda_2"),
                                      ("hg_lb", "hg_lower_bounds_2")):
                        par_rows(sp, "par_in", 3, PROWS2[name], key)
                    for i, key in enumerate(("lam_q1", "lam_k1", "lam_q2", "lam_k2")):
                        par(sp, "lam_in", lamv[:, i], ins[key].to_broadcast([P, 64]))
                if u["name"] == ("ff2", 0):
                    sp.wait_ge(sem("x3_hi"), 8)
                    sp.dma_start(nf[:, :], ins["norm_final_2"].rearrange("(a d) -> a d", a=1).to_broadcast(
                        [P, D])).then_inc(sem("nf_in"), 16)
            for t in range(2):
                sp.wait_ge(sem("out_ready"), t + 1)
                sp.dma_start(out[0, P * t:P * t + P, :], outb[:, t, :]).then_inc(sem("out_done"), 16)
            sp.wait_ge(sem("out_done"), 32)

        @block.gpsimd
        def _(pool):
            n = [0]

            def seq(i):
                n[0] += 1
                i.then_inc(sem("pool_seq"), 1)
                pool.wait_ge(sem("pool_seq"), n[0])

            seq(pool.memset(ident[:], 0.0))
            pool.affine_select(out=ident[:], in_=ident[:], compare_op=ALU.not_equal, fill=1.0, base=0,
                               pattern=[[-1, P]], channel_multiplier=1).then_inc(sem("constants"), 1)
            seq(pool.memset(small[:, 0:2, :], 1.0))
            pool.memset(small[:, 83, :], EPS).then_inc(sem("constants"), 1)
            pool.memset(ones[:], 1.0).then_inc(sem("constants"), 1)
            half = small[:, 84, 0:8].rearrange("p (g a) -> p g a", g=2)
            seq(pool.memset(small[:, 84, 0:8], 1.0))
            seq(pool.affine_select(out=half, in_=half, compare_op=ALU.is_ge, fill=0.0, base=0,
                                   pattern=[[-16, 2], [-32, 4]], channel_multiplier=1))
            pool.affine_select(out=half, in_=half, compare_op=ALU.is_ge, fill=0.0, base=15,
                               pattern=[[16, 2], [32, 4]], channel_multiplier=-1).then_inc(sem("constants"), 1)
            seq(pool.memset(b_blk[:], 0.0))
            seq(pool.memset(sel[:], 1.0))
            seq(pool.affine_select(out=sel[:], in_=sel[:], compare_op=ALU.is_ge, fill=0.0, base=0,
                                   pattern=[[128, 8], [-64, 16]], channel_multiplier=1))
            seq(pool.affine_select(out=sel[:], in_=sel[:], compare_op=ALU.is_ge, fill=0.0, base=63,
                                   pattern=[[-128, 8], [64, 16]], channel_multiplier=-1))
            seq(pool.memset(selT[:], 1.0))
            seq(pool.affine_select(out=selT[:], in_=selT[:], compare_op=ALU.is_ge, fill=0.0, base=0,
                                   pattern=[[128, 8], [1, P]], channel_multiplier=-64))
            seq(pool.affine_select(out=selT[:], in_=selT[:], compare_op=ALU.is_ge, fill=0.0, base=63,
                                   pattern=[[-128, 8], [-1, P]], channel_multiplier=64))
            seq(pool.memset(selH[:], 0.0))
            for h in range(4):
                seq(pool.memset(selH[:, h, h:h + 1], 1.0))
            seq(pool.memset(selHT[:], 1.0))
            seq(pool.affine_select(out=selHT[:], in_=selHT[:], compare_op=ALU.is_equal, fill=0.0, base=0,
                                   pattern=[[-1, 4], [0, P]], channel_multiplier=1))
            seq(pool.iota(neg_dist[:], [[1, TOK]], base=-144, channel_multiplier=-1,
                          allow_small_or_imprecise_dtypes=True))
            seq(pool.affine_select(out=neg_dist[:], in_=neg_dist[:], compare_op=ALU.is_ge, fill=-BIG, base=144,
                                   pattern=[[-1, TOK]], channel_multiplier=1))
            pool.memset(small[:, 85, 1:2], 0.0).then_inc(sem("constants"), 1)

            for i in range(8):
                seq(pool.tensor_scalar(bias[:, i, :], neg_dist[:], 2.0 ** -(i + 1), None, ALU.mult))
            pool.memset(small[:, 85, 2:3], 0.0).then_inc(sem("constants"), 1)
            pool.wait_ge(sem("bc_in"), 64)
            pool.wait_ge(sem("f_ready"), 1)
            fre = sm("fre")[:, :, None].to_broadcast([P, NS, 16])
            fim = sm("fim")[:, :, None].to_broadcast([P, NS, 16])
            for i, (part, f) in enumerate(((0, fre), (1, fim), (1, fre), (0, fim))):
                seq(pool.tensor_tensor(b_prod[:, i], b_raw[:, part], f, ALU.mult))
            for g in range(2):
                r = slice(64 * g, 64 * g + 64)
                pool.tensor_tensor(b_blk[r, 0, :, g, :], b_prod[r, 0], b_prod[r, 1], ALU.subtract).then_inc(
                    sem("bc_blk"), 1)
                pool.wait_ge(sem("bc_blk"), 2 * g + 1)
                pool.tensor_tensor(b_blk[r, 1, :, g, :], b_prod[r, 2], b_prod[r, 3], ALU.add).then_inc(
                    sem("bc_blk"), 1)
                pool.wait_ge(sem("bc_blk"), 2 * g + 2)
            for i in range(2):
                for g in range(2):
                    pool.tensor_scalar(c_blk[:, i, :, g, :], c_raw[:, i], sm("halfc", 2)[:, g:g + 1], None,
                                       ALU.mult).then_inc(sem("bc_blk"), 1)

            def s5_w(b):
                pool.wait_ge(sem("s5_m"), b + 1)
                m = mprod[:, b % NM]
                pool.tensor_tensor(m[:, 0], m[:, 0], m[:, 1], ALU.add).then_inc(sem("s5_w"), 1)
                pool.tensor_tensor(m[:, 2], m[:, 2], m[:, 3], ALU.subtract).then_inc(sem("s5_w"), 1)

            def lo_half(half_):
                u, c = POOL_LO[half_ // 2], slice(UNIT // 2 * (half_ % 2), UNIT // 2 * (half_ % 2) + UNIT // 2)
                pool.wait_ge(sem("hi_ready"), u + 1)
                i = pool.tensor_tensor(w_lo[:, u % NW, c], raw[:, u % NRAW, c], w_hi[:, u % NW, c].bitcast(F32),
                                       ALU.subtract)
                if half_ % 2:
                    i.then_inc(sem("lo_ready"), 1)
                else:
                    seq(i)

            pool.wait_ge(sem("lo_ready"), POOL_LO[0])
            for b in range(16):
                if b == 0:
                    for i in range(6):
                        lo_half(i)
                s5_w(b)
                lo_half(b + 6)
            for half_ in range(22, 2 * len(POOL_LO)):
                lo_half(half_)
            b_last = unit_at[("up_b", KF // 2 - 1)]
            pool.wait_ge(sem("group_done"), b_last["g0"] + 2)
            seq(pool.memset(lru_w[:], 0.0))
            for i, key in enumerate(("lru_wa_2", "lru_wx_2")):
                for g in range(2):
                    r = slice(64 * g, 64 * g + 64)
                    pool.dma_start(lru_w[r, i, :, r], ins[key][0, g:4:2].rearrange("t i j -> i t j")).then_inc(
                        sem("lru_w_in"), 16)
            pool.wait_ge(sem("x2_ready"), 8)
            for lv in range(8):
                m = masks[:, lv, :]
                seq(pool.memset(m, 1.0))
                if lv == 0:
                    seq(pool.affine_select(out=m, in_=m, compare_op=ALU.is_equal, fill=0.0, base=0,
                                           pattern=[[-1, P]], channel_multiplier=1))
                    continue
                L = 1 << (lv - 1)
                mv = m.rearrange("p (b h l) -> p b h l", h=2, l=L)
                seq(pool.memset(mv[:, :, 0, :], 0.0))
                mv = mv[:, :, 1, :]
                seq(pool.affine_select(out=mv, in_=mv, compare_op=ALU.is_ge, fill=0.0, base=0,
                                       pattern=[[-2 * L, P // (2 * L)], [0, L]], channel_multiplier=1))
                seq(pool.affine_select(out=mv, in_=mv, compare_op=ALU.is_ge, fill=0.0, base=L - 1,
                                       pattern=[[2 * L, P // (2 * L)], [0, L]], channel_multiplier=-1))
            pool.memset(hA[:], 0.0).then_inc(sem("constants"), 1)

        @block.scalar
        def _(act):
            A = nc.scalar

            par_rows(act, "par0_in", 0, 0, "norm1_g")
            par(act, "ssm_in", log_dt[:, :], ins["ssm_log_dt"].to_broadcast([P, 32]))
            for name, key in (("a_re", "ssm_a_re"), ("a_im", "ssm_a_im"), ("ssm_d", "ssm_d")):
                par_rows(act, "ssm_in", 1, PROWS[name] - PROWS["a_re"], key)
            for i, key in enumerate(("ssm_b_re", "ssm_b_im")):
                par(act, "bc_in", b_raw[:, i], ins[key][0].rearrange("(j g) p c -> (g p) j c", g=2))
            for i, key in enumerate(("ssm_c_re", "ssm_c_im")):
                par(act, "bc_in", c_raw[:, i], ins[key][0].rearrange("(a g) c p -> (g c) a p", g=8))

            act.wait_ge(sem("constants"), CONSTANTS["small"])
            A.activation(small[:, 1, 8:9], eps_col, ACT.Sqrt)
            ss = small[:, 0, 0:3]
            for t, rows, signal in ((0, META, "meta_in"), (1, P, "x_in0")):
                act.wait_ge(sem(signal), 16)
                A.activation(junk_x[0:rows, :], xtok[0:rows, t, :], ACT.Square,
                             accum_out=small[0:rows, 0, t:t + 1]).then_inc(sem("x_sq"), 1)
                act.wait_ge(sem("x_sq"), t + 1)
            act.wait_ge(sem("x_sq2"), 1)
            A.activation(small[:, 1, 0:3], ss, ACT.Sqrt, bias=eps_col, scale=1.0 / D).then_inc(sem("x_rms"), 1)

            done = [0]

            def split_to(n):
                while done[0] < min(n, len(units)):
                    u = done[0]
                    act.wait_ge(sem(f"w_in{u % NRAW}"), 16 * (u // NRAW + 1))
                    used(act, u - NW)
                    A.activation(w_hi[:, u % NW, :], raw[:, u % NRAW, :], ACT.Copy).then_inc(sem("hi_ready"), 1)
                    done[0] += 1

            def evac(name, i, fn, ms=None):
                u = unit_at[(name, i)]
                for m in ms or range(u["groups"]):
                    g = u["g0"] + m
                    act.wait_ge(sem("group_done"), g + 1)
                    fn(m, banks[g % NB]).then_inc(sem(f"group_free{g % NB}"), 1)

            split_to(1)
            for kt in range(KD):
                act.wait_ge(sem("xrT"), kt + 1)
                if kt == 0:
                    act.wait_ge(sem("C_ready"), 1)
                A.activation(xn_hi[:, kt, :], banks[4 + kt % 4][:, 0:TOK], ACT.Copy,
                             scale=col("norm1", kt)).then_inc(sem("xn_hi"), 1)
            split_to(2)
            act.wait_ge(sem("ssm_in"), 64)
            for g in range(2):
                r = slice(64 * g, 64 * g + 64)
                A.activation(sm("dt")[r], log_dt[r, g:32:2], ACT.Exp).then_inc(sem("s5p_a"), 1)
            act.wait_ge(sem("s5p_v"), 1)
            A.activation(sm("mag"), sm("zr"), ACT.Exp).then_inc(sem("s5p_a"), 1)
            A.activation(sm("tnh"), sm("zr"), ACT.Tanh, scale=0.5).then_inc(sem("s5p_a"), 1)
            act.wait_ge(sem("s5p_v"), 2)
            A.activation(sm("sin"), sm("thr"), ACT.Sin).then_inc(sem("s5p_a"), 1)
            A.activation(sm("sinh_"), sm("thr"), ACT.Sin, scale=0.5).then_inc(sem("s5p_a"), 1)
            act.wait_ge(sem("lam_v"), 2)
            A.activation(sm("lam_e", 2), sm("lam_s", 2), ACT.Exp).then_inc(sem("lam_a"), 1)
            split_to(3)
            evac("u", 0, lambda m, b: A.activation(uT[:, m, :], b[:, 0:TOK], ACT.Copy))
            split_to(4)
            for kt in range(KD):
                act.wait_ge(sem("xT"), kt + 1)
                A.activation(hT[:, kt, :], banks[4 + kt % 4][:, T0:TOK], ACT.Copy).then_inc(sem("hT_copy"), 1)
            evac("u", 1, lambda m, b: A.activation(uT[:, 2 + m, :], b[:, 0:TOK], ACT.Copy))
            for i in range(2):
                split_to(5 + i)
                evac("k", i, lambda m, b: A.activation(qkT[:, 2 * i + m, :], b[:, 0:TOK], ACT.Copy))
            for i in range(4):
                act.wait_ge(sem("bcT"), i + 1)
                dst = (BT, BT, CT, CT)[i][:, :, i % 2, :]
                A.activation(dst, banks[4 + i][:, :].rearrange("p (a b) -> p a b", a=4), ACT.Copy,
                             scale=-1.0 if i == 3 else 1.0).then_inc(sem("bc_ready"), 1)
            for i in range(2):
                split_to(7 + i)
                evac("q", i, lambda m, b: A.activation(qkT[:, 4 + 2 * i + m, :], b[:, 0:TOK], ACT.Copy))
            vrows = (META, P, P)
            for i in range(2):
                split_to(9 + i)
                evac("v", i, lambda m, b: A.activation(v_tok[0:vrows[m], m, 256 * i:256 * i + 256],
                                                       b[0:vrows[m], 0:256], ACT.Copy))

            def gates(i, ms=(0, 1)):
                if i == 0:
                    act.wait_ge(sem("bcT"), 4)
                evac("gate", i, lambda m, b: A.activation(gate[:, 2 * i + m, :], b[:, 0:NQ], ACT.Tanh, scale=0.5), ms)

            for i in range(4):
                split_to(unit_at[("gate", i)]["n"] + 3)
                gates(i)
            for i in range(8):
                need(act, "qk_stat", i - 1)
                if i == 0:
                    act.wait_ge(sem("s5_out"), 16)
                A.activation(sq[:, i % 2, :], qkT[:, i, :], ACT.Square).then_inc(sem("qk_sq"), 1)
                if i == 1:
                    gates(4)
                    split_to(unit_at[("gate", 4)]["n"] + 4)
            for i in range(4):
                act.wait_ge(sem("y_pre"), 4 + i + 1)
                A.activation(yg[:, i, :], yg[:, i, :], ACT.Gelu_apprx_tanh).then_inc(sem("yg"), 1)
            for i in range(4):
                act.wait_ge(sem("yg"), i + 1)
                A.activation(yg_hi[:, i, :], yg[:, i, T0:TOK], ACT.Copy).then_inc(sem("yg_hi"), 1)
            act.wait_ge(sem("qk_stat"), 8)
            A.activation(rs[:, :], banks[4][0:16, 0:TOK], ACT.Sqrt, bias=eps_col[0:16, :],
                         scale=1.0 / 64).then_inc(sem("qk_rms"), 1)
            gates(5)
            split_to(unit_at[("gate", 5)]["n"] + 4)

            def exp_a(h):
                act.wait_ge(sem("max_a"), h + 1)
                for j in range(2):
                    A.activation(p_a[:, j, :], p_a[:, j, :], ACT.Exp, bias=sm("nmx_a", 2)[:, j:j + 1],
                                 accum_out=sm("l_a", 2)[:, j:j + 1]).then_inc(sem("exp_a"), 1)

            def exp_b(h):
                act.wait_ge(sem("max_b"), h + 1)
                for t, nk in ((0, KEYS_B), (1, META)):
                    for j in range(2):
                        c = 2 * t + j
                        A.activation(p_b[:, t, j, 0:nk], p_b[:, t, j, 0:nk], ACT.Exp,
                                     bias=sm("nmx_b", 4)[:, c:c + 1],
                                     accum_out=sm("l_b", 4)[:, c:c + 1]).then_inc(sem("exp_b"), 1)

            def copy_a(h):
                act.wait_ge(sem("turn_a"), h + 1)
                need(act, "att_o", h)
                A.activation(wT0[:, KEYS_B:TOK], banks[7][0:META, 256:384], ACT.Copy).then_inc(sem("copied_a"), 1)
                A.activation(wT12[:, P:384], banks[7][:, 0:256], ACT.Copy).then_inc(sem("copied_a"), 1)

            def copy_b(h):
                act.wait_ge(sem("turn_b"), h + 1)
                A.activation(wT0[:, 0:KEYS_B], banks[6][0:META, P:P + KEYS_B], ACT.Copy).then_inc(sem("copied_b"), 1)
                A.activation(wT12[:, 0:P], banks[6][:, 0:P], ACT.Copy).then_inc(sem("copied_b"), 1)

            def copy_o(h):
                act.wait_ge(sem("att_o"), h + 1)
                A.activation(oT[:, h, :], banks[3][:, 0:TOK], ACT.Copy).then_inc(sem("o_copied"), 1)

            def glu(ms):
                evac("glu", 0, lambda m, b: A.activation(glu_t[:, m, :], b[:, 0:NQ], ACT.Tanh, scale=0.5,
                                                         bias=sm("glu_bh", 4)[:, m:m + 1]), ms)

            exp_a(0)
            exp_b(0)
            for h in range(4):
                if h:
                    copy_o(h - 1)
                copy_a(h)
                if h < 3:
                    exp_a(h + 1)
                if h < 2:
                    gates(6 + h, (0,))
                if h == 2:
                    glu((0, 1))
                copy_b(h)
                if h < 3:
                    exp_b(h + 1)
                if h < 2:
                    gates(6 + h, (1,))
                    split_to(unit_at[("gate", 6 + h)]["n"] + 4)
                if h == 2:
                    glu((2, 3))
                    split_to(unit_at[("glu", 0)]["n"] + 4)
                    for i in range(4):
                        act.wait_ge(sem("yssm"), i + 1)
                        A.activation(yg_hi[:, i, :], glu_t[:, i, :], ACT.Copy, scale=0.5).then_inc(sem("yssm_hi"), 1)
            copy_o(3)
            act.wait_ge(sem("yssm_hi"), 4)
            act.wait_ge(sem("o_copied"), 4)
            for h in range(4):
                need(act, "o_stat", h - 1)
                A.activation(sq[:, h % 2, :], oT[:, h, :], ACT.Square).then_inc(sem("o_sq"), 1)
            act.wait_ge(sem("o_stat"), 4)
            A.activation(rs2[:, :], banks[4][0:4, 0:TOK], ACT.Sqrt, bias=eps_col[0:4, :],
                         scale=1.0 / P).then_inc(sem("o_rms"), 1)
            for h in range(4):
                act.wait_ge(sem("yatt"), h + 1)
                A.activation(yatt_hi[:, h, :], oT[:, h, T0:TOK], ACT.Copy).then_inc(sem("yatt_hi"), 1)
            split_to(unit_at[("att_out", 0)]["n"] + 2)
            for m in range(8):
                if m == 4:
                    split_to(unit_at[("att_out", 1)]["n"] + 2)
                act.wait_ge(sem("mixed"), m + 1)
                A.activation(mix_hi[:, m, :], gate[:, m, :], ACT.Copy, scale=0.5).then_inc(sem("mix_hi"), 1)
            for m in range(8):
                if m % 2 == 0:
                    split_to(unit_at[("w_o", m // 2)]["n"] + 3)
                taken(act, group(("w_o", m // 2), m % 2))
                need(act, "h1_stat", m - 1)
                A.activation(sq[:, m % 2, 0:NQ], hT[:, m, :], ACT.Square).then_inc(sem("h1_sq"), 1)
            act.wait_ge(sem("h1_stat"), 8)
            A.activation(rstd[:, :], banks[3][:, 0:NQ], ACT.Sqrt, bias=eps_col, scale=1.0 / D).then_inc(sem("h1_rms"), 1)
            for m in range(8):
                act.wait_ge(sem("hs"), m + 1)
                A.activation(hs_hi[:, m, :], junk[:, m % 2, 0:NQ], ACT.Copy).then_inc(sem("hs_hi"), 1)
            split_to(unit_at[("up_a", 0)]["n"] + 2)
            for i in range(KF // 2):
                split_to(unit_at[("up_a", i)]["n"] + 3)
                for m in range(2):
                    taken(act, group(("up_a", i), m))
                    A.activation(gl[:, i % 2, m, :], cv_[:, i % 2, m, :], ACT.Gelu_apprx_tanh).then_inc(sem("gl"), 1)
                split_to(unit_at[("up_b", i)]["n"] + 3)
                for m in range(2):
                    taken(act, group(("up_b", i), m))
                    if i >= 2:
                        need(act, "acc_unit_done", i - 1)
                    A.activation(ff_hi[:, i % 2, m, :], ff[:, i % 2, m, :], ACT.Copy).then_inc(sem("ff_hi"), 1)
            split_to(unit_at[("down", KF // 2 - 1)]["n"] + 1)

            def norm_in(ready, stat, rms, hi, src, dst_hi, first):
                for m in range(8):
                    ready(m)
                    need(act, stat, m - 1)
                    A.activation(sq2[:, m % 2, :], src[:, m, :], ACT.Square).then_inc(sem(stat + "_sq"), 1)
                act.wait_ge(sem(stat), 8)
                A.activation(rst2[:, :], banks[3][:, 0:256], ACT.Sqrt, bias=eps_col, scale=1.0 / D).then_inc(
                    sem(rms), 1)
                split_to(first)
                for m in range(8):
                    act.wait_ge(sem(hi + "_f"), m + 1)
                    A.activation(dst_hi[:, m, :], tmp2[:, m % 2, :], ACT.Copy).then_inc(sem(hi), 1)

            norm_in(lambda m: act.wait_ge(sem("x2_ready"), m + 1), "x2_stat", "x2_rms", "x2n_hi", x2, x2n_hi,
                    unit_at[("lru_x", 0)]["n"] + 2)
            act.wait_ge(sem("tiny_v"), 1)
            A.activation(sm("sp_e", 2), sm("sp_ab", 2), ACT.Exp, scale=-1.0).then_inc(sem("tiny_a"), 1)
            A.activation(sm("lb_e", 2), sm("lb_z", 2), ACT.Exp).then_inc(sem("tiny_a"), 1)
            act.wait_ge(sem("tiny_a"), 2)
            A.activation(sm("sp_l", 2), sm("sp_e", 2), ACT.Ln, bias=ones[:, 0:1]).then_inc(sem("tiny_a"), 1)
            split_to(unit_at[("hg_f", 0)]["n"] + 3)
            u = unit_at[("hg_f", 0)]
            for m in range(2):
                g = u["g0"] + m
                act.wait_ge(sem("group_done"), g + 1)
                A.activation(hgf[:, m, :], banks[g % NB][:, 0:256], ACT.Sigmoid).then_inc(sem("hg_sig"), 1)
                A.activation(hgk[:, m, :], banks[g % NB][:, 0:256], ACT.Sigmoid, scale=-1.0).then_inc(
                    sem(f"group_free{g % NB}"), 1)
            split_to(unit_at[("hg_q", 0)]["n"] + 3)
            for m in range(2):
                act.wait_ge(sem("lru_gate"), 2)
                A.activation(lru_r[:, m, :], banks[6][:, 256 * m:256 * m + 256], ACT.Sigmoid,
                             bias=col("lru_ba", m)).then_inc(sem("lru_ri"), 1)
                A.activation(lru_i[:, m, :], banks[7][:, 256 * m:256 * m + 256], ACT.Sigmoid,
                             bias=col("lru_bx", m)).then_inc(sem("lru_ri"), 1)
            evac("hg_q", 0, lambda m, b: A.activation(hgq[:, m, :], b[:, 0:256], ACT.Silu))
            act.wait_ge(sem("lru_ri"), 4)
            act.wait_ge(sem("tiny_v"), 2)
            for m in range(2):
                A.activation(lru_a[:, m, :], lru_r[:, m, :], ACT.Exp, scale=sm("n8sp", 2)[:, m:m + 1]).then_inc(
                    sem("lru_at"), 1)
                A.activation(lru_t[:, m, :], lru_r[:, m, :], ACT.Tanh, scale=sm("n8sp", 2)[:, m:m + 1]).then_inc(
                    sem("lru_at"), 1)
            split_to(unit_at[("hg_i", 0)]["n"] + 3)
            evac("hg_i", 0, lambda m, b: A.activation(hgv[:, m, :], b[:, 0:256], ACT.Copy))
            act.wait_ge(sem("lru_e"), 2)
            for m in range(2):
                A.activation(lru_t[:, m, :], lru_t[:, m, :], ACT.Sqrt).then_inc(sem("lru_s"), 1)
            for i in range(2):
                split_to(unit_at[("cq", i)]["n"] + 3)
                evac("cq", i, lambda m, b: A.activation(cq[:, 2 * i + m, :], b[:, 0:256], ACT.Copy, scale=0.125))
            for i in range(2):
                split_to(unit_at[("ck", i)]["n"] + 3)
                evac("ck", i, lambda m, b: A.activation(ck[:, 2 * i + m, :], b[:, 0:256], ACT.Copy))
            for i in range(2):
                split_to(unit_at[("cv", i)]["n"] + 3)
                evac("cv", i, lambda m, b: A.activation(cv[:, m, 256 * i:256 * i + 256], b[:, 0:256], ACT.Copy))
            act.wait_ge(sem("hg_o"), 1)
            A.activation(hgo[:, :, :], banks[3][:, :].rearrange("p (a t) -> p a t", a=2), ACT.Copy).then_inc(
                sem("hgo"), 1)
            act.wait_ge(sem("hgo"), 1)
            for m in range(2):
                A.activation(sq2[:, m, :], hgo[:, m, :], ACT.Square).then_inc(sem("hgo"), 1)
            act.wait_ge(sem("hg_stat"), 2)
            A.activation(rsm2[:, :], banks[3][0:4, 0:256], ACT.Sqrt, bias=eps_col[0:4, :], scale=1.0 / 64).then_inc(
                sem("hg_rms"), 1)

            def m_exp(it):
                nk = 128 * (it % 2) + 128
                act.wait_ge(sem("m_max"), it + 1)
                A.activation(mp[:, it % 2, 0:nk], mp[:, it % 2, 0:nk], ACT.Exp, bias=sm(f"mn{it % 2}", 1),
                             accum_out=sm(f"ml{it % 2}", 1)).then_inc(sem("m_exp"), 1)

            def m_copy(h):
                act.wait_ge(sem("m_T"), 2 * h + 2)
                need(act, "m_val", h - 1)
                A.activation(mpT[:, h % 2, :], banks[6 + h % 2][:, 0:384], ACT.Copy).then_inc(sem("m_copied"), 1)

            def m_out(p_):
                act.wait_ge(sem("m_val"), 2 * p_ + 2)
                A.activation(mo[:, p_, :], banks[3][:, 0:256], ACT.Copy).then_inc(sem("m_out"), 1)

            for it in range(16):
                m_exp(it)
                if it == 0:
                    split_to(unit_at[("hg_g", 0)]["n"] + 3)
                    evac("hg_g", 0, lambda m, b: A.activation(hgg[:, m, :], b[:, 0:256], ACT.Silu))
                if it == 2:
                    split_to(unit_at[("lru_y", 0)]["n"] + 3)
                    evac("lru_y", 0, lambda m, b: A.activation(lru_g[:, m, :], b[:, 0:256], ACT.Gelu_apprx_tanh))
                if it == 4:
                    for m in range(2):
                        act.wait_ge(sem("yb"), m + 1)
                        A.activation(ycat_hi[:, 2 + m, :], hgo[:, m, :], ACT.Copy).then_inc(sem("ycat_hi"), 1)
                    for m in range(2):
                        act.wait_ge(sem("lru_h"), m + 1)
                        A.activation(sq2[:, m, :], xc[:, m, :], ACT.Square).then_inc(sem("ya_sq"), 1)
                    act.wait_ge(sem("ya_stat"), 2)
                    A.activation(rst2[:, :], banks[3][:, 256:512], ACT.Sqrt, bias=eps_col, scale=1.0 / 256).then_inc(
                        sem("ya_rms"), 1)
                if it == 6:
                    for m in range(2):
                        act.wait_ge(sem("ya"), m + 1)
                        A.activation(ycat_hi[:, m, :], xc[:, m, :], ACT.Copy).then_inc(sem("ycat_hi"), 1)
                if it % 2 == 1 and it >= 3:
                    m_copy((it - 3) // 2)
                if it in (7, 11, 15):
                    m_out((it - 7) // 4)
            m_copy(7)
            m_out(3)
            for p_ in range(4):
                act.wait_ge(sem("m_out"), p_ + 1)
                need(act, "yc_stat", p_ - 1)
                A.activation(sq2[:, p_ % 2, :], mo[:, p_, :], ACT.Square).then_inc(sem("yc_sq"), 1)
            act.wait_ge(sem("yc_stat"), 4)
            A.activation(rst2[:, :], banks[3][:, 0:256], ACT.Sqrt, bias=eps_col, scale=1.0 / 512).then_inc(
                sem("yc_rms"), 1)
            for p_ in range(4):
                act.wait_ge(sem("yc"), p_ + 1)
                A.activation(ycat_hi[:, 4 + p_, :], mo[:, p_, :], ACT.Copy).then_inc(sem("ycat_hi"), 1)
            split_to(unit_at[("w_out2", 0)]["n"] + 2)

            def x3_ready(m):
                if m % 2 == 0:
                    split_to(unit_at[("w_out2", m // 2)]["n"] + 3)
                taken(act, group(("w_out2", m // 2), m % 2))

            norm_in(x3_ready, "x3_stat", "x3_rms", "x3_hi", x2, x2n_hi, unit_at[("ff1", 0)]["n"] + 2)
            for i in range(KF2 // 2):
                split_to(unit_at[("ff1", i)]["n"] + 3)
                for m in range(2):
                    g = group(("ff1", i), m)
                    act.wait_ge(sem("group_done"), g + 1)
                    A.activation(relu[:, i % 2, m, :], banks[g % NB][:, 0:256], ACT.Relu).then_inc(
                        sem(f"group_free{g % NB}"), 1)
                for m in range(2):
                    act.wait_ge(sem("uu"), 2 * i + m + 1)
                    if i >= 2:
                        used(act, unit_at[("ff2", i - 2)]["n"])
                    A.activation(u_hi[:, i % 2, m, :], uu[:, i % 2, m, :], ACT.Copy).then_inc(sem("u_hi"), 1)
            split_to(len(units))
            used(act, len(units) - 1)
            for t in range(2):
                for h in range(2):
                    A.activation(sqj[:, :], banks[4 + 2 * t + h][:, :], ACT.Square,
                                 accum_out=sm("fs", 4)[:, 2 * t + h:2 * t + h + 1]).then_inc(sem("f_sq"), 1)
                    act.wait_ge(sem("f_sq"), 2 * t + h + 1)
            act.wait_ge(sem("f_sum"), 1)
            A.activation(sm("fr", 2), sm("fr", 2), ACT.Sqrt, bias=eps_col, scale=1.0 / D).then_inc(sem("f_rms"), 1)

        @block.vector
        def _(dve):
            V = nc.vector
            n = [0]

            def mark(i):
                n[0] += 1
                i.then_inc(sem("dve_seq"), 1)
                return n[0]

            def seq(i):
                dve.wait_ge(sem("dve_seq"), mark(i))

            dve.wait_ge(sem("constants"), CONSTANTS["small"])
            dve.wait_ge(sem("x_in1"), 16)
            V.tensor_tensor_reduce(xr[:, 2, :], xtok[:, 2, :], xtok[:, 2, :], 1.0, 0.0, ALU.mult, ALU.add,
                                   small[:, 0, 2:3]).then_inc(sem("x_sq2"), 1)
            dve.wait_ge(sem("x_rms"), 1)
            seq(V.reciprocal(small[:, 1, 4:7], small[:, 1, 0:3]))
            for t, rows in ((0, META), (1, P), (2, P)):
                V.tensor_scalar(xr[0:rows, t, :], xtok[0:rows, t, :], small[0:rows, 1, 4 + t:5 + t], None,
                                ALU.mult).then_inc(sem("xr"), 1)

            def param_cols(i):
                dst, n_ = PTILES[i]
                dve.wait_ge(sem("par_T"), (1, 2, 4, 4)[i])
                V.tensor_copy((C1[:, dst:dst + n_] if i < 3 else C2[:, 0:n_]), banks[3][:, P * i:P * i + n_]).then_inc(
                    sem("C_ready"), 1)
                dve.wait_ge(sem("C_ready"), i + 1)

            param_cols(0)

            done = [0]

            def split_to(n):
                while done[0] < min(n, len(units)):
                    u = done[0]
                    done[0] += 1
                    if u in POOL_LO:
                        continue
                    dve.wait_ge(sem("hi_ready"), u + 1)
                    if u - 1 in POOL_LO:
                        dve.wait_ge(sem("lo_ready"), u)
                    V.tensor_tensor(w_lo[:, u % NW, :], raw[:, u % NRAW, :], w_hi[:, u % NW, :].bitcast(F32),
                                    ALU.subtract).then_inc(sem("lo_ready"), 1)

            split_to(1)
            for kt in range(KD):
                dve.wait_ge(sem("xn_hi"), kt + 1)
                V.scalar_tensor_tensor(out=xn_lo[:, kt, :], in0=banks[4 + kt % 4][:, 0:TOK], scalar=col("norm1", kt),
                                       in1=xn_hi[:, kt, :].bitcast(F32), op0=ALU.mult,
                                       op1=ALU.subtract).then_inc(sem("xn_lo"), 1)
            split_to(2)
            param_cols(1)
            are, aim = col("a_re", 0, 16), col("a_im", 0, 16)
            tt = lambda o, a, b, op: V.tensor_tensor(o, a, b, op)
            dve.wait_ge(sem("s5p_a"), 2)
            tt(sm("zr"), are, sm("dt"), ALU.mult).then_inc(sem("s5p_v"), 1)
            seq(tt(sm("th"), aim, sm("dt"), ALU.mult))
            seq(V.tensor_scalar(sm("kk"), sm("th"), INV_TWO_PI, ROUND, ALU.mult, ALU.add))
            seq(V.tensor_scalar(sm("kk"), sm("kk"), -ROUND, None, ALU.add))
            for c in (TWO_PI_1, TWO_PI_2, TWO_PI_3):
                seq(V.scalar_tensor_tensor(out=sm("th"), in0=sm("kk"), scalar=-c, in1=sm("th"), op0=ALU.mult,
                                           op1=ALU.add))
            V.tensor_scalar(sm("thr"), sm("th"), 3.1415925, -3.1415925, ALU.min, ALU.max).then_inc(sem("s5p_v"), 1)
            dve.wait_ge(sem("s5p_a"), 6)
            seq(V.scalar_tensor_tensor(out=sm("mm1"), in0=sm("mag"), scalar=1.0, in1=sm("tnh"), op0=ALU.add,
                                       op1=ALU.mult))
            seq(tt(sm("omc"), sm("sinh_"), sm("sinh_"), ALU.mult))
            seq(V.tensor_scalar(sm("omc"), sm("omc"), 2.0, None, ALU.mult))
            seq(tt(sm("lbi"), sm("mag"), sm("sin"), ALU.mult))
            seq(tt(sm("q1"), sm("mag"), sm("omc"), ALU.mult))
            seq(tt(sm("nre"), sm("mm1"), sm("q1"), ALU.subtract))
            seq(tt(sm("q1"), are, are, ALU.mult))
            seq(tt(sm("q2"), aim, aim, ALU.mult))
            seq(tt(sm("q1"), sm("q1"), sm("q2"), ALU.add))
            seq(V.reciprocal(sm("rden"), sm("q1")))
            seq(tt(sm("q1"), sm("nre"), are, ALU.mult))
            seq(tt(sm("q2"), sm("lbi"), aim, ALU.mult))
            seq(tt(sm("q1"), sm("q1"), sm("q2"), ALU.add))
            seq(tt(sm("fre"), sm("q1"), sm("rden"), ALU.mult))
            seq(tt(sm("q1"), sm("lbi"), are, ALU.mult))
            seq(tt(sm("q2"), sm("nre"), aim, ALU.mult))
            seq(tt(sm("q1"), sm("q1"), sm("q2"), ALU.subtract))
            dve.wait_ge(sem("constants"), CONSTANTS["half"])
            half = small[:, 84, 0:8].rearrange("p (g a) -> p g a", g=2)
            seq(V.tensor_reduce(sm("halfc", 2), half, AXX, ALU.add))
            tt(sm("fim"), sm("q1"), sm("rden"), ALU.mult).then_inc(sem("f_ready"), 1)
            dve.wait_ge(sem("lam_in"), 64)
            for i in range(2):
                V.tensor_tensor_reduce(lamv[:, i * 2], lamv[:, i * 2], lamv[:, i * 2 + 1], 1.0, 0.0, ALU.mult, ALU.add,
                                       sm("lam_s", 2)[:, i:i + 1]).then_inc(sem("lam_v"), 1)
            split_to(3)
            dve.wait_ge(sem("xrT"), 8)
            mark(V.memset(Ec[:, :, 0:1], 1.0))
            mark(V.memset(Es[:, :, 0:1], 0.0))
            mark(V.tensor_scalar(Ec[:, :, 1], sm("omc"), -1.0, 1.0, ALU.mult, ALU.add))
            seq(V.tensor_copy(Es[:, :, 1], sm("sin")))
            have = 1
            while have < LC - 1:
                m = min(have, LC - 1 - have)
                pc, ps = (e_[:, :, have:have + 1].to_broadcast([P, NS, m]) for e_ in (Ec, Es))
                lo, hi = slice(1, m + 1), slice(have + 1, have + m + 1)
                t1, t2 = e_tmp[:, 0, :, 0:m], e_tmp[:, 1, :, 0:m]
                mark(tt(t1, Es[:, :, lo], ps, ALU.mult))
                mark(tt(Ec[:, :, hi], Ec[:, :, lo], pc, ALU.mult))
                mark(tt(t2, Ec[:, :, lo], ps, ALU.mult))
                seq(tt(Es[:, :, hi], Es[:, :, lo], pc, ALU.mult))
                mark(tt(Ec[:, :, hi], Ec[:, :, hi], t1, ALU.subtract))
                seq(tt(Es[:, :, hi], Es[:, :, hi], t2, ALU.add))
                have += m
            param_cols(2)
            param_cols(3)
            dve.wait_ge(sem("lam_a"), 1)
            seq(V.tensor_scalar(sm("lam_e", 2)[:, 1:2], sm("lam_e", 2)[:, 1:2], -1.0, 0.8 - 0.6, ALU.mult, ALU.add))
            seq(tt(sm("nlam", 1), sm("lam_e", 2)[:, 0:1], sm("lam_e", 2)[:, 1:2], ALU.add))
            seq(V.tensor_scalar(sm("nlam", 1), sm("nlam", 1), -1.0, None, ALU.mult))
            seq(V.tensor_scalar(sm("qg", 1), col("qn"), 0.125, None, ALU.mult))
            seq(V.tensor_scalar(sm("subg", 1), col("subln"), 1.0 - (0.8 - 0.6), None, ALU.mult))
            seq(V.tensor_scalar(sm("glu_bh", 4), col("glu_b", 0, 4), 0.5, None, ALU.mult))
            seq(tt(sm("q1"), Ec[:, :, LC - 1], Ec[:, :, 1], ALU.mult))
            seq(tt(sm("q2"), Es[:, :, LC - 1], Es[:, :, 1], ALU.mult))
            seq(tt(sm("kc"), sm("q1"), sm("q2"), ALU.subtract))
            seq(tt(sm("q1"), Ec[:, :, LC - 1], Es[:, :, 1], ALU.mult))
            seq(tt(sm("q2"), Es[:, :, LC - 1], Ec[:, :, 1], ALU.mult))
            seq(tt(sm("ks"), sm("q1"), sm("q2"), ALU.add))

            def s5_mults(b):
                jp = b % 8
                c, s = Ec[:, 2 * jp:2 * jp + 2, :], Es[:, 2 * jp:2 * jp + 2, :]
                pair = psum[:, 4 + 2 * (b % 2):6 + 2 * (b % 2), :]
                xre, xim = pair[:, :, 0:LC], pair[:, :, LC:2 * LC]
                m = mprod[:, b % NM].rearrange("p n (a t) -> p n a t", a=2)
                dve.wait_ge(sem("s5_x"), b + 1)
                need(dve, "s5_out", b - NM + 1)
                mark(tt(m[:, 0], xre, c, ALU.mult))
                mark(tt(m[:, 1], xim, s, ALU.mult))
                mark(tt(m[:, 2], xim, c, ALU.mult))
                tt(m[:, 3], xre, s, ALU.mult).then_inc(sem("s5_m"), 1)

            def s5_scan(b):
                jp, m = b % 8, mprod[:, b % NM]
                dve.wait_ge(sem("s5_w"), 2 * (b + 1))
                last = 0
                for p_ in range(2):
                    for i in range(2):
                        j = 2 * jp + i
                        init = 0.0 if b < 8 else sm("zi" if p_ else "zr0")[:, j:j + 1]
                        last = mark(V.tensor_tensor_scan(zbuf[:, p_, LC * i:LC * i + LC],
                                                         sm("mag")[:, j:j + 1].to_broadcast([P, LC]),
                                                         m[:, 2 * p_, LC * i:LC * i + LC], init, ALU.mult, ALU.add))
                dve.wait_ge(sem("dve_seq"), last)
                c = Ec[:, 2 * jp:2 * jp + 2, :].rearrange("p a t -> p (a t)")
                s = Es[:, 2 * jp:2 * jp + 2, :].rearrange("p a t -> p (a t)")
                if b < 8:
                    for p_, nm in ((0, "zer"), (1, "zei")):
                        src = zbuf[:, p_].rearrange("p (a t) -> p a t", a=2)[:, :, LC - 1]
                        mark(V.tensor_copy(sm(nm)[:, 2 * jp:2 * jp + 2], src))
                mark(tt(m[:, 0], zbuf[:, 0], c, ALU.mult))
                mark(V.scalar_tensor_tensor(out=m[:, 1], in0=zbuf[:, 1], scalar=-1.0, in1=s, op0=ALU.mult,
                                            op1=ALU.mult))
                mark(tt(m[:, 2], zbuf[:, 0], s, ALU.mult))
                tt(m[:, 3], zbuf[:, 1], c, ALU.mult).then_inc(sem("s5_n"), 1)
                dve.wait_ge(sem("s5_n"), b + 1)

            def carry():
                a, b, c, s = sm("zer"), sm("zei"), sm("kc"), sm("ks")
                mark(tt(sm("q1"), a, c, ALU.mult))
                mark(tt(sm("q2"), b, s, ALU.mult))
                mark(tt(sm("q3"), a, s, ALU.mult))
                seq(tt(sm("q4"), b, c, ALU.mult))
                mark(tt(sm("zr0"), sm("q1"), sm("q2"), ALU.subtract))
                seq(tt(sm("zi"), sm("q3"), sm("q4"), ALU.add))

            def s5_y(kk):
                c, jj = divmod(kk, 4)
                dve.wait_ge(sem("s5_out"), 2 * kk + 2)
                V.scalar_tensor_tensor(out=yg[:, jj, LC * c:LC * c + LC], in0=uT[:, jj, LC * c:LC * c + LC],
                                       scalar=col("ssm_d", jj), in1=banks[3][:, 0:LC], op0=ALU.mult,
                                       op1=ALU.add).then_inc(sem("y_pre"), 1)

            dve.wait_ge(sem("xT"), 8)
            s5_mults(0)
            for b in range(1, 16):
                s5_mults(b)
                if b % 2 == 0 and b > 2:
                    s5_y(b // 2 - 2)
                s5_scan(b - 1)
                if b == 8:
                    carry()
            s5_scan(15)
            s5_y(6)
            split_to(12)
            s5_y(7)
            for i in range(4):
                dve.wait_ge(sem("yg_hi"), i + 1)
                tt(yg_lo[:, i, :], yg[:, i, T0:TOK], yg_hi[:, i, :].bitcast(F32), ALU.subtract).then_inc(sem("yg_lo"), 1)
            split_to(13)
            dve.wait_ge(sem("qk_rms"), 1)
            V.reciprocal(rs[:, :], rs[:, :]).then_inc(sem("qk_r"), 1)
            for i in range(8):
                dve.wait_ge(sem("qk_bc"), i + 1)
                V.scalar_tensor_tensor(out=qkT[:, i, :], in0=qkT[:, i, :], scalar=col("kn") if i < 4 else sm("qg", 1),
                                       in1=banks[5 + i % 3][:, 0:TOK], op0=ALU.mult, op1=ALU.mult).then_inc(
                                           sem("qkn"), 1)


            def att_max(part, h, pieces):
                dve.wait_ge(sem(f"scores_{part}"), h + 1)
                n_ = len(pieces)
                need(dve, f"w_{part}", n_ // 2 * h)
                for c, (dst, src, b0, nk) in enumerate(pieces):
                    mark(V.tensor_tensor_reduce(dst, src, bias[:, 2 * h + 1, b0:b0 + nk], 1.0, -3e38, ALU.add,
                                                ALU.max, sm(f"mx_{part}", n_)[:, c:c + 1]))
                dve.wait_ge(sem("dve_seq"), n[0])
                V.tensor_scalar(sm(f"nmx_{part}", n_), sm(f"mx_{part}", n_), -1.0, None, ALU.mult).then_inc(
                    sem(f"max_{part}"), 1)

            def max_a(h):
                if h == 0:
                    dve.wait_ge(sem("constants"), CONSTANTS["bias"])
                att_max("a", h, [(p_a[:, j, :], banks[4 + j][:, 0:TOK], 0, TOK) for j in range(2)])

            def max_b(h):
                att_max("b", h, [(p_b[:, 0, j, :], banks[6 + j][:, 0:KEYS_B], P, KEYS_B) for j in range(2)]
                        + [(p_b[:, 1, j, 0:META], banks[6 + j][:, KEYS_B:KEYS_B + META], KEYS_B, META)
                           for j in range(2)])

            def att_mix(part, h, pieces):
                n_ = 2 * len(pieces)
                dve.wait_ge(sem(f"exp_{part}"), n_ * (h + 1))
                need(dve, f"turn_{part}", h)
                rl = sm(f"rl_{part}", n_)
                seq(V.reciprocal(rl, sm(f"l_{part}", n_)))
                pair = rl.rearrange("p (t j) -> p t j", j=2)
                mark(V.tensor_scalar(pair[:, :, 1], pair[:, :, 1], sm("nlam", 1), None, ALU.mult))
                for c, (w, p0, _) in enumerate(pieces):
                    mark(V.tensor_scalar(w, p0, rl[:, 2 * c:2 * c + 1], None, ALU.mult))
                dve.wait_ge(sem("dve_seq"), n[0])
                for c, (w, _, p1) in enumerate(pieces):
                    i = V.scalar_tensor_tensor(out=w, in0=p1, scalar=rl[:, 2 * c + 1:2 * c + 2], in1=w,
                                               op0=ALU.mult, op1=ALU.add)
                    i.then_inc(sem(f"w_{part}"), 1)

            def mix_a(h):
                att_mix("a", h, [(w_a[:, :], p_a[:, 0, :], p_a[:, 1, :])])

            def mix_b(h):
                att_mix("b", h, [(w_b[:, t, 0:nk], p_b[:, t, 0, 0:nk], p_b[:, t, 1, 0:nk])
                                 for t, nk in ((0, KEYS_B), (1, META))])

            max_a(0)
            max_b(0)
            for h in range(4):
                mix_a(h)
                if h < 3:
                    max_a(h + 1)
                else:
                    for i in range(4):
                        dve.wait_ge(sem("yssm_hi"), i + 1)
                        V.scalar_tensor_tensor(out=yg_lo[:, i, :], in0=glu_t[:, i, :], scalar=0.5,
                                               in1=yg_hi[:, i, :].bitcast(F32), op0=ALU.mult,
                                               op1=ALU.subtract).then_inc(sem("yssm_lo"), 1)
                mix_b(h)
                if h < 3:
                    max_b(h + 1)
                if h == 2:
                    for i in range(4):
                        taken(dve, unit_at[("glu", 0)]["g0"] + i)
                        V.scalar_tensor_tensor(out=glu_t[:, i, :], in0=glu_t[:, i, :], scalar=1.0,
                                               in1=yg[:, i, T0:TOK], op0=ALU.add, op1=ALU.mult).then_inc(
                                                   sem("yssm"), 1)

            def evac(name, i, fn):
                u = unit_at[(name, i)]
                for m in range(u["groups"]):
                    g = u["g0"] + m
                    dve.wait_ge(sem("group_done"), g + 1)
                    fn(m, banks[g % NB]).then_inc(sem(f"group_free{g % NB}"), 1)

            for i in range(2):
                evac("ssm_out", i, lambda m, b: V.scalar_tensor_tensor(
                    out=gate[:, 4 * i + m, :], in0=gate[:, 4 * i + m, :], scalar=1.0, in1=b[:, 0:NQ],
                    op0=ALU.add, op1=ALU.mult))

            def yatt_low(h):
                dve.wait_ge(sem("yatt_hi"), h + 1)
                tt(yatt_lo[:, h, :], oT[:, h, T0:TOK], yatt_hi[:, h, :].bitcast(F32), ALU.subtract).then_inc(
                    sem("yatt_lo"), 1)

            dve.wait_ge(sem("o_rms"), 1)
            V.reciprocal(rs2[:, :], rs2[:, :]).then_inc(sem("o_r"), 1)
            for h in range(4):
                dve.wait_ge(sem("o_bc"), h + 1)
                V.scalar_tensor_tensor(out=oT[:, h, T0:TOK], in0=oT[:, h, T0:TOK], scalar=sm("subg", 1),
                                       in1=banks[4 + h][:, T0:TOK], op0=ALU.mult, op1=ALU.mult).then_inc(
                                           sem("yatt"), 1)
                if h:
                    yatt_low(h - 1)
            yatt_low(3)
            for i in range(2):
                split_to(unit_at[("att_out", i)]["n"] + 2)
                u = unit_at[("att_out", i)]
                evac("att_out", i, lambda m, b: V.scalar_tensor_tensor(
                    out=gate[:, 8 + 4 * i + m, :], in0=gate[:, 8 + 4 * i + m, :], scalar=1.0, in1=b[:, 0:NQ],
                    op0=ALU.add, op1=ALU.mult))
                for m in range(4):
                    g = u["g0"] + m
                    taken(dve, g)
                    j = 4 * i + m
                    tt(gate[:, j, :], gate[:, j, :], gate[:, 8 + j, :], ALU.add).then_inc(sem("mixed"), 1)
                for m in range(4):
                    j = 4 * i + m
                    dve.wait_ge(sem("mix_hi"), j + 1)
                    V.scalar_tensor_tensor(out=mix_lo[:, j, :], in0=gate[:, j, :], scalar=0.5,
                                           in1=mix_hi[:, j, :].bitcast(F32), op0=ALU.mult,
                                           op1=ALU.subtract).then_inc(sem("mix_lo"), 1)
            for i in range(4):
                u = unit_at[("w_o", i)]
                split_to(u["n"] + 2)
                for m in range(2):
                    g = u["g0"] + m
                    dve.wait_ge(sem("group_done"), g + 1)
                    dve.wait_ge(sem("hT_copy"), 8)
                    j = 2 * i + m
                    tt(hT[:, j, :], hT[:, j, :], banks[g % NB][:, 0:NQ], ALU.add).then_inc(sem(f"group_free{g % NB}"), 1)
            split_to(unit_at[("up_a", 0)]["n"] + 2)
            dve.wait_ge(sem("h1_rms"), 1)
            seq(V.reciprocal(rstd[:, :], rstd[:, :]))
            for m in range(8):
                taken(dve, group(("w_o", m // 2), m % 2))
                need(dve, "hs_lo", m - 1)
                V.scalar_tensor_tensor(out=junk[:, m % 2, 0:NQ], in0=hT[:, m, :], scalar=col("norm2", m),
                                       in1=rstd[:, :], op0=ALU.mult, op1=ALU.mult).then_inc(sem("hs"), 1)
                if m:
                    dve.wait_ge(sem("hs_hi"), m)
                    tt(hs_lo[:, m - 1, :], junk[:, (m - 1) % 2, 0:NQ], hs_hi[:, m - 1, :].bitcast(F32),
                       ALU.subtract).then_inc(sem("hs_lo"), 1)
            dve.wait_ge(sem("hs_hi"), 8)
            tt(hs_lo[:, 7, :], junk[:, 1, 0:NQ], hs_hi[:, 7, :].bitcast(F32), ALU.subtract).then_inc(sem("hs_lo"), 1)
            for i in range(KF // 2):
                ua, ub = unit_at[("up_a", i)], unit_at[("up_b", i)]
                split_to(ua["n"] + 3)
                for m in range(2):
                    j, g = 2 * i + m, ua["g0"] + m
                    dve.wait_ge(sem("group_done"), g + 1)
                    ps = banks[g % NB]
                    c = cv_[:, i % 2, m, :]
                    seq(V.tensor_scalar(c, ps[:, 0:256], col("conv_w", j), col("conv_b", j), ALU.mult, ALU.add))
                    seq(V.scalar_tensor_tensor(out=c, in0=ps[:, 1:257], scalar=col("conv_w", KF + j), in1=c,
                                               op0=ALU.mult, op1=ALU.add))
                    V.scalar_tensor_tensor(out=c, in0=ps[:, 2:258], scalar=col("conv_w", 2 * KF + j), in1=c,
                                           op0=ALU.mult, op1=ALU.add).then_inc(sem(f"group_free{g % NB}"), 1)
                split_to(ub["n"] + 3)
                for m in range(2):
                    j, g = 2 * i + m, ub["g0"] + m
                    dve.wait_ge(sem("group_done"), g + 1)
                    dve.wait_ge(sem("gl"), j + 1)
                    tt(ff[:, i % 2, m, :], gl[:, i % 2, m, :], banks[g % NB][:, 0:256], ALU.mult).then_inc(
                        sem(f"group_free{g % NB}"), 1)
                for m in range(2):
                    taken(dve, group(("up_b", i), m))
                    dve.wait_ge(sem("ff_hi"), 2 * i + m + 1)
                    tt(ff_lo[:, i % 2, m, :], ff[:, i % 2, m, :], ff_hi[:, i % 2, m, :].bitcast(F32),
                       ALU.subtract).then_inc(sem("ff_lo"), 1)
            split_to(unit_at[("down", KF // 2 - 1)]["n"] + 1)
            dve.wait_ge(sem("acc_unit_done"), KF // 2)
            for m in range(8):
                tt(x2[:, m, :], hT[:, m, 2:NQ], banks[4 + m // 2][:, 256 * (m % 2):256 * (m % 2) + 256],
                   ALU.add).then_inc(sem("x2_ready"), 1)

            STT = V.scalar_tensor_tensor
            lam, lb = col("lru_lam", 0, 2), col("hg_lb", 0, 2)
            seq(STT(out=sm("sp_ab", 2), in0=lam, scalar=-1.0, in1=lam, op0=ALU.mult, op1=ALU.max))
            tt(sm("lb_z", 2), lb, lb, ALU.subtract).then_inc(sem("tiny_v"), 1)

            def norm_in(stat, rms, hi, lo, src, dst_hi, dst_lo, gain, first):
                split_to(first)
                dve.wait_ge(sem(rms), 1)
                seq(V.reciprocal(rst2[:, :], rst2[:, :]))
                for m in range(9):
                    if m < 8:
                        need(dve, lo, m - 1)
                        STT(out=tmp2[:, m % 2, :], in0=src[:, m, :], scalar=col(gain, m), in1=rst2[:, :],
                            op0=ALU.mult, op1=ALU.mult).then_inc(sem(hi + "_f"), 1)
                    if m:
                        dve.wait_ge(sem(hi), m)
                        tt(dst_lo[:, m - 1, :], tmp2[:, (m - 1) % 2, :], dst_hi[:, m - 1, :].bitcast(F32),
                           ALU.subtract).then_inc(sem(lo), 1)

            dve.wait_ge(sem("x2_ready"), 8)
            norm_in("x2_stat", "x2_rms", "x2n_hi", "x2n_lo", x2, x2n_hi, x2n_lo, "norm_mix",
                    unit_at[("lru_x", 0)]["n"] + 2)
            dve.wait_ge(sem("tiny_a"), 3)
            seq(V.tensor_scalar(sm("sp_m", 2), lam, -1.0, 0.0, ALU.mult, ALU.max))
            seq(tt(sm("sp_m", 2), sm("sp_m", 2), sm("sp_l", 2), ALU.add))
            seq(V.reciprocal(sm("lb_s", 2), sm("lb_e", 2)))
            seq(tt(sm("lb_s", 2), sm("lb_s", 2), sm("lb_e", 2), ALU.mult))
            seq(tt(sm("lb_0", 2), sm("lb_s", 2), sm("lb_s", 2), ALU.subtract))
            seq(V.tensor_scalar(sm("lb_m", 2), sm("lb_0", 2), TINY, None, ALU.max))
            seq(V.tensor_scalar(sm("lb_c", 2), sm("lb_0", 2), -1.0, 1.0, ALU.mult, ALU.add))
            V.tensor_scalar(sm("n8sp", 2), sm("sp_m", 2), -8.0, None, ALU.mult).then_inc(sem("tiny_v"), 1)
            u = unit_at[("lru_x", 0)]
            split_to(u["n"] + 3)
            for m in range(2):
                g = u["g0"] + m
                dve.wait_ge(sem("group_done"), g + 1)
                ps = banks[g % NB]
                seq(V.tensor_scalar(xc[:, m, :], ps[:, 0:256], col("lru_w", 6 + m), col("lru_b", m), ALU.mult,
                                    ALU.add))
                for d in range(1, 4):
                    i = STT(out=xc[:, m, d:256], in0=ps[:, 0:256 - d], scalar=col("lru_w", 2 * (3 - d) + m),
                            in1=xc[:, m, d:256], op0=ALU.mult, op1=ALU.add)
                    if d < 3:
                        seq(i)
                i.then_inc(sem(f"group_free{g % NB}"), 1)
            split_to(unit_at[("hg_f", 0)]["n"] + 3)
            dve.wait_ge(sem("hg_sig"), 2)
            for m in range(2):
                taken(dve, group(("hg_f", 0), m))
                seq(V.tensor_scalar(hgf[:, m, :], hgf[:, m, :], sm("lb_c", 2)[:, m:m + 1], sm("lb_m", 2)[:, m:m + 1],
                                    ALU.mult, ALU.add))
                seq(V.tensor_scalar(hgk[:, m, :], hgk[:, m, :], sm("lb_c", 2)[:, m:m + 1], None, ALU.mult))
            split_to(unit_at[("hg_q", 0)]["n"] + 3)
            for m in range(2):
                taken(dve, group(("hg_q", 0), m))
            tt(hqf[:, :, :], hgq[:, :, :], hgf[:, :, :], ALU.mult).then_inc(sem("h_level"), 1)
            split_to(unit_at[("hg_i", 0)]["n"] + 3)
            dve.wait_ge(sem("lru_at"), 4)
            seq(tt(hgo[:, :, :], lru_a[:, :, :], lru_a[:, :, :], ALU.mult))
            seq(STT(out=lru_t[:, :, :], in0=hgo[:, :, :], scalar=1.0, in1=lru_t[:, :, :], op0=ALU.add, op1=ALU.mult))
            V.tensor_scalar(lru_t[:, 0, :], lru_t[:, 0, :], -1.0, SQRT_MIN, ALU.mult, ALU.max).then_inc(sem("lru_e"), 1)
            V.tensor_scalar(lru_t[:, 1, :], lru_t[:, 1, :], -1.0, SQRT_MIN, ALU.mult, ALU.max).then_inc(sem("lru_e"), 1)
            seq(tt(lru_i[:, :, :], lru_i[:, :, :], xc[:, :, :], ALU.mult))

            def level(lv):
                dve.wait_ge(sem("h_scores"), lv + 1)
                if lv == 0:
                    dve.wait_ge(sem("constants"), CONSTANTS["masks"])
                b = 4 + 2 * (lv % 2)
                if lv == 8:
                    V.tensor_copy(hX[:, :, :].rearrange("p (a b) t -> p a (b t)", a=2),
                                  psum[:, b:b + 2, 0:256]).then_inc(sem("h_taken"), 1)
                    return
                data = psum[:, b:b + 2, :].rearrange("p a (b t) -> p (a b) t", t=P)
                m = masks[:, lv, :][:, None, :].to_broadcast([P, 8, P]).bitcast(I32)
                if lv:
                    dve.wait_ge(sem("h_taken"), lv)
                V.copy_predicated(hA[:, :, :], m, data).then_inc(sem("h_taken"), 1)
                if lv == 0:
                    return
                L = 1 << (lv - 1)
                nb = 512 // (2 * L)
                src = hgf[:, :, :].rearrange("p a t -> p (a t)") if L == 1 else htot[:, 512 - 1024 // L:512 - 512 // L]
                dst = htot[:, 512 - 512 // L:512 - 256 // L]
                tot = src.rearrange("p (b h) -> p b h", h=2)
                qv = hqf[:, :, :].rearrange("p a t -> p (a t)").rearrange("p (b h l) -> p b h l", h=2, l=L)
                kv = hgk[:, :, :].rearrange("p a t -> p (a t)").rearrange("p (b h l) -> p b h l", h=2, l=L)
                mark(tt(qv[:, :, 1, :], qv[:, :, 1, :], tot[:, :, 0:1].to_broadcast([P, nb, L]), ALU.mult))
                seq(tt(kv[:, :, 0, :], kv[:, :, 0, :], tot[:, :, 1:2].to_broadcast([P, nb, L]), ALU.mult))
                tt(dst, tot[:, :, 0], tot[:, :, 1], ALU.mult).then_inc(sem("h_level"), 1)
                dve.wait_ge(sem("h_level"), lv + 1)

            level(0)
            level(1)
            split_to(unit_at[("cq", 0)]["n"] + 3)
            dve.wait_ge(sem("lru_s"), 2)
            seq(tt(lru_i[:, :, :], lru_i[:, :, :], lru_t[:, :, :], ALU.mult))
            for m in range(2):
                mark(V.tensor_tensor_scan(lru_r[:, m, :], lru_a[:, m, :], lru_i[:, m, :], 0.0, ALU.mult, ALU.add))
            level(2)
            level(3)
            split_to(unit_at[("cq", 1)]["n"] + 3)
            level(4)
            level(5)
            split_to(unit_at[("ck", 0)]["n"] + 3)
            level(6)
            split_to(unit_at[("ck", 1)]["n"] + 3)
            level(7)
            level(8)
            split_to(unit_at[("cv", 1)]["n"] + 3)
            dve.wait_ge(sem("hg_rms"), 1)
            V.reciprocal(rsm2[:, :], rsm2[:, :]).then_inc(sem("hg_r"), 1)

            def m_max(it):
                h, t = it // 2, it % 2
                nk, c0 = 128 * t + 128, 144 - 128 * t
                dve.wait_ge(sem("m_s"), it + 1)
                need(dve, "m_T", it - 1)
                seq(V.tensor_tensor_reduce(mp[:, it % 2, 0:nk], banks[4 + it % 2][:, 0:nk], bias[:, h, c0:c0 + nk],
                                           1.0, -3e38, ALU.add, ALU.max, sm(f"mx{it % 2}", 1)))
                V.tensor_scalar(sm(f"mn{it % 2}", 1), sm(f"mx{it % 2}", 1), -1.0, None, ALU.mult).then_inc(
                    sem("m_max"), 1)

            def m_norm(it):
                nk = 128 * (it % 2) + 128
                dve.wait_ge(sem("m_exp"), it + 1)
                seq(V.reciprocal(sm(f"mr{it % 2}", 1), sm(f"ml{it % 2}", 1)))
                V.tensor_scalar(mp[:, it % 2, 0:nk], mp[:, it % 2, 0:nk], sm(f"mr{it % 2}", 1), None, ALU.mult).then_inc(
                    sem("m_w"), 1)

            for m in range(2):
                dve.wait_ge(sem("hg_bc"), m + 1)
                STT(out=hgo[:, m, :], in0=hgo[:, m, :], scalar=col("hg_norm"), in1=banks[6 + m][:, 0:256],
                    op0=ALU.mult, op1=ALU.mult).then_inc(sem("hg_n"), 1)
            m_max(0)
            for it in range(16):
                if it < 15:
                    m_max(it + 1)
                if it == 0:
                    split_to(unit_at[("hg_g", 0)]["n"] + 3)
                if it == 1:
                    for m in range(2):
                        taken(dve, group(("hg_g", 0), m))
                        dve.wait_ge(sem("hg_n"), m + 1)
                        tt(hgo[:, m, :], hgo[:, m, :], hgg[:, m, :], ALU.mult).then_inc(sem("yb"), 1)
                if it == 2:
                    split_to(unit_at[("lru_y", 0)]["n"] + 3)
                if it == 3:
                    for m in range(2):
                        taken(dve, group(("lru_y", 0), m))
                        tt(xc[:, m, :], lru_r[:, m, :], lru_g[:, m, :], ALU.mult).then_inc(sem("lru_h"), 1)
                if it == 5:
                    for m in range(2):
                        dve.wait_ge(sem("ycat_hi"), m + 1)
                        tt(ycat_lo[:, 2 + m, :], hgo[:, m, :], ycat_hi[:, 2 + m, :].bitcast(F32),
                           ALU.subtract).then_inc(sem("ycat_lo"), 1)
                    dve.wait_ge(sem("ya_rms"), 1)
                    seq(V.reciprocal(rst2[:, :], rst2[:, :]))
                    for m in range(2):
                        STT(out=xc[:, m, :], in0=xc[:, m, :], scalar=col("lru_norm", m), in1=rst2[:, :],
                            op0=ALU.mult, op1=ALU.mult).then_inc(sem("ya"), 1)
                if it == 7:
                    for m in range(2):
                        dve.wait_ge(sem("ycat_hi"), 3 + m)
                        tt(ycat_lo[:, m, :], xc[:, m, :], ycat_hi[:, m, :].bitcast(F32), ALU.subtract).then_inc(
                            sem("ycat_lo"), 1)
                m_norm(it)
            dve.wait_ge(sem("yc_rms"), 1)
            seq(V.reciprocal(rst2[:, :], rst2[:, :]))
            for p_ in range(4):
                STT(out=mo[:, p_, :], in0=mo[:, p_, :], scalar=col("att_norm", p_), in1=rst2[:, :],
                    op0=ALU.mult, op1=ALU.mult).then_inc(sem("yc"), 1)
            for p_ in range(4):
                dve.wait_ge(sem("ycat_hi"), 5 + p_)
                tt(ycat_lo[:, 4 + p_, :], mo[:, p_, :], ycat_hi[:, 4 + p_, :].bitcast(F32), ALU.subtract).then_inc(
                    sem("ycat_lo"), 1)
            for i in range(4):
                split_to(unit_at[("w_out2", i)]["n"] + 2)
                for m in range(2):
                    g = group(("w_out2", i), m)
                    dve.wait_ge(sem("group_done"), g + 1)
                    tt(x2[:, 2 * i + m, :], x2[:, 2 * i + m, :], banks[g % NB][:, 0:256], ALU.add).then_inc(
                        sem(f"group_free{g % NB}"), 1)
            for m in range(8):
                taken(dve, group(("w_out2", m // 2), m % 2))
            norm_in("x3_stat", "x3_rms", "x3_hi", "x3_lo", x2, x2n_hi, x2n_lo, "norm_mlp", unit_at[("ff1", 0)]["n"] + 2)
            for i in range(KF2 // 2):
                split_to(unit_at[("ff1", i)]["n"] + 3)
                for m in range(2):
                    taken(dve, group(("ff1", i), m))
                    r = relu[:, i % 2, m, :]
                    tt(uu[:, i % 2, m, :], r, r, ALU.mult).then_inc(sem("uu"), 1)
                for m in range(2):
                    dve.wait_ge(sem("u_hi"), 2 * i + m + 1)
                    tt(u_lo[:, i % 2, m, :], uu[:, i % 2, m, :], u_hi[:, i % 2, m, :].bitcast(F32),
                       ALU.subtract).then_inc(sem("u_lo"), 1)
            split_to(len(units))
            dve.wait_ge(sem("f_sq"), 4)
            fs = sm("fs", 4).rearrange("p (t h) -> p t h", h=2)
            tt(sm("fr", 2), fs[:, :, 0], fs[:, :, 1], ALU.add).then_inc(sem("f_sum"), 1)
            dve.wait_ge(sem("f_rms"), 1)
            dve.wait_ge(sem("nf_in"), 16)
            seq(V.reciprocal(sm("fr", 2), sm("fr", 2)))
            for t in range(2):
                i = STT(out=outb[:, t, :].rearrange("p (a n) -> p a n", a=2), in0=psum[:, 4 + 2 * t:6 + 2 * t, :],
                        scalar=sm("fr", 2)[:, t:t + 1], in1=nf[:, :].rearrange("p (a n) -> p a n", a=2),
                        op0=ALU.mult, op1=ALU.mult)
                i.then_inc(sem("out_ready"), 1)

        @block.tensor
        def _(pe):
            T = nc.tensor

            def mm3(out_, lh, ll, rh, rl, start, stop):
                T.matmul(out_, lh, rh, start=start, stop=False)
                T.matmul(out_, lh, rl, start=False, stop=False)
                return T.matmul(out_, ll, rh, start=False, stop=stop)

            def unit(name, i, lhs_or_rhs, kk, width, tok_cols=None, ready=None, between=None, ms=None):
                u = unit_at[(name, i)]
                un = u["n"]
                pe.wait_ge(sem("lo_ready"), un + 1)
                ah, al, lo_c, hi_c = lhs_or_rhs
                wh = w_hi[:, un % NW, :].rearrange("p (k n) -> p k n", k=kk)
                wl = w_lo[:, un % NW, :].rearrange("p (k n) -> p k n", k=kk)
                for m in ms or range(u["groups"]):
                    g = u["g0"] + m
                    need(pe, f"group_free{g % NB}", free_count(g))
                    bank = banks[g % NB]
                    for kt in range(kk):
                        a, z = kt == 0, kt == kk - 1
                        if ready and m == 0:
                            pe.wait_ge(sem(ready), kt + 1)
                        if u["kind"] == "feat":
                            c = slice(P * m, P * m + P)
                            last = mm3(bank[:, 0:hi_c - lo_c], wh[:, kt, c], wl[:, kt, c], ah[:, kt, lo_c:hi_c],
                                       al[:, kt, lo_c:hi_c], a, z)
                        else:
                            c = slice(tok_cols[m], tok_cols[m] + P)
                            last = mm3(bank[:, 0:256], ah[:, kt, c], al[:, kt, c], wh[:, kt, :], wl[:, kt, :], a, z)
                    last.then_inc(sem("group_done"), 1)
                    if between and m == 0:
                        between()

            def param_cols(i, signal, n_):
                pe.wait_ge(sem(signal), 16 * n_)
                w = PTILES[i][1]
                need(pe, "C_ready", min(i, 2))
                T.transpose(banks[3][:, P * i:P * i + w], params[:, i][0:w, :], ident[0:w, 0:w]).then_inc(
                    sem("par_T"), 1)

            pe.wait_ge(sem("constants"), CONSTANTS["ident"])
            param_cols(0, "par0_in", 1)

            def to_features(src, kt):
                b = banks[4 + kt % 4]
                T.transpose(b[:, 0:META], src[0:META, 0, P * kt:P * kt + P], ident[0:META, 0:META])
                T.transpose(b[:, META:META + P], src[:, 1, P * kt:P * kt + P], ident[:])
                return T.transpose(b[:, META + P:TOK], src[:, 2, P * kt:P * kt + P], ident[:])

            pe.wait_ge(sem("xr"), 3)
            for kt in range(KD):
                need(pe, "xn_lo", kt - 3)
                to_features(xr, kt).then_inc(sem("xrT"), 1)
            param_cols(1, "ssm_in", 4)
            xn = (xn_hi, xn_lo, 0, TOK)
            xq = (xn_hi, xn_lo, T0, TOK)
            unit("u", 0, xn, 8, 256, ready="xn_lo")
            unit("u", 1, xn, 8, 256)
            for kt in range(KD):
                need(pe, "hT_copy", kt - 3)
                to_features(xtok, kt).then_inc(sem("xT"), 1)
            param_cols(2, "par_in", 21)
            param_cols(3, "par_in", 21)
            unit("k", 0, xn, 8, 256)
            unit("k", 1, xn, 8, 256)
            pe.wait_ge(sem("bc_blk"), 8)
            pe.wait_ge(sem("hT_copy"), 8)
            for i in range(4):
                src = (b_blk, c_blk)[i // 2][:, i % 2]
                src = src.rearrange("p a b c -> p (a b c)")
                for a in range(4):
                    last = T.transpose(banks[4 + i][:, P * a:P * a + P], src[:, P * a:P * a + P], ident[:])
                last.then_inc(sem("bcT"), 1)
            pe.wait_ge(sem("bc_ready"), 4)
            u1 = unit_at[("u", 1)]
            for m in range(2):
                g = u1["g0"] + m
                taken(pe, g)

            def s5_in(b):
                c, jp = divmod(b, 8)
                jj = jp // 2
                need(pe, "s5_m", b - 1)
                for part in range(2):
                    for i in range(2):
                        bank = banks[4 + 2 * (b % 2) + i]
                        r = 64 * (jp % 2) + 32 * i
                        last = T.matmul(bank[:, LC * part:LC * part + LC], BT[r:r + 32, jj, part, :],
                                        uT[r:r + 32, jj, LC * c:LC * c + LC], start=True, stop=True)
                last.then_inc(sem("s5_x"), 1)

            def s5_out(b):
                c, jp = divmod(b, 8)
                jj = jp // 2
                pe.wait_ge(sem("s5_n"), b + 1)
                if b % 2 == 0:
                    need(pe, "y_pre", b // 2)
                for i in range(2):
                    r = 64 * (jp % 2) + 32 * i
                    for q in range(4):
                        last = T.matmul(banks[3][r:r + 32, 0:LC], CT[:, jj, q // 2, r:r + 32],
                                        mprod[:, b % NM, q, LC * i:LC * i + LC], start=(q == 0), stop=(q == 3))
                last.then_inc(sem("s5_out"), 1)

            v_cols = (0, META, META + P)
            seq_units = [("q", 0, xn, None), ("q", 1, xn, None),
                         ("v", 0, xn, v_cols), ("v", 1, xn, v_cols), ("gate", 0, xq, None), ("gate", 1, xq, None),
                         ("gate", 2, xq, None), ("gate", 3, xq, None)]

            def s5_step(b):
                if b < 16:
                    s5_in(b)
                if b > 2:
                    s5_out(b - 3)

            s5_in(0)
            s5_in(1)
            for i, (name, j, x_, tc) in enumerate(seq_units):
                s5_step(2 * i + 2)
                unit(name, j, x_, 8, 256, tc, between=lambda: s5_step(2 * i + 3))
            s5_out(15)
            unit("gate", 4, xq, 8, 256)
            pe.wait_ge(sem("constants"), CONSTANTS["sel"])
            for i in range(8):
                pe.wait_ge(sem("qk_sq"), i + 1)
                T.matmul(banks[4][0:16, 0:TOK], sel[:, i, :], sq[:, i % 2, :], start=(i == 0),
                         stop=(i == 7)).then_inc(sem("qk_stat"), 1)
            unit("gate", 5, xq, 8, 256)
            pe.wait_ge(sem("qk_r"), 1)

            def norm_bc(i):
                need(pe, "qkn", i - 2)
                T.matmul(banks[5 + i % 3][:, 0:TOK], selT[:, i, :], rs[:, :], start=True, stop=True).then_inc(
                    sem("qk_bc"), 1)

            for i in range(8):
                norm_bc(i)
            pe.wait_ge(sem("qkn"), 8)

            def scores_a(h):
                need(pe, "max_a", h)
                for j in range(2):
                    r = slice(64 * j, 64 * j + 64)
                    last = T.matmul(banks[4 + j][:, 0:TOK], qkT[r, 4 + h, KEYS_B:TOK], qkT[r, h, 0:TOK],
                                    start=True, stop=True)
                last.then_inc(sem("scores_a"), 1)

            def scores_b(h):
                need(pe, "copied_a", 2 * h)
                need(pe, "copied_b", 2 * h)
                for t, t0, nk in ((0, META, KEYS_B), (1, 0, META)):
                    for j in range(2):
                        r, c = slice(64 * j, 64 * j + 64), KEYS_B * t
                        last = T.matmul(banks[6 + j][:, c:c + nk], qkT[r, 4 + h, t0:t0 + P], qkT[r, h, 0:nk],
                                        start=True, stop=True)
                last.then_inc(sem("scores_b"), 1)

            def turn_a(h):
                pe.wait_ge(sem("w_a"), h + 1)
                need(pe, "copied_a", 2 * h)
                T.transpose(banks[7][:, 0:P], w_a[:, META:META + P], ident[:])
                T.transpose(banks[7][:, P:2 * P], w_a[:, META + P:TOK], ident[:])
                T.transpose(banks[7][0:META, 2 * P:3 * P], w_a[:, 0:META], ident[:]).then_inc(sem("turn_a"), 1)

            def turn_b(h):
                pe.wait_ge(sem("w_b"), 2 * h + 2)
                T.transpose(banks[6][:, 0:P], w_b[:, 0, META:KEYS_B], ident[:])
                T.transpose(banks[6][0:META, P:P + META], w_b[0:META, 1, 0:META], ident[0:META, 0:META])
                T.transpose(banks[6][0:META, P + META:P + KEYS_B], w_b[:, 0, 0:META], ident[:]).then_inc(
                    sem("turn_b"), 1)

            def values(h):
                pe.wait_ge(sem("copied_a"), 2 * h + 2)
                pe.wait_ge(sem("copied_b"), 2 * h + 2)
                need(pe, "o_copied", h)
                c = slice(P * h, P * h + P)
                T.matmul(banks[3][:, 0:TOK], v_tok[0:META, 0, c], wT0[:, :], start=True, stop=False)
                T.matmul(banks[3][:, META:TOK], v_tok[:, 1, c], wT12[:, 0:256], start=False, stop=False)
                T.matmul(banks[3][:, META + P:TOK], v_tok[:, 2, c], wT12[:, 256:384], start=False,
                         stop=True).then_inc(sem("att_o"), 1)

            def step_a(h):
                if h:
                    scores_b(h)
                    values(h - 1)
                if h < 3:
                    scores_a(h + 1)
                turn_a(h)

            y_in = (yg_hi, yg_lo, 0, NQ)
            scores_a(0)
            scores_b(0)
            for h in range(2):
                step_a(h)
                unit("gate", 6 + h, xq, 8, 256, ms=(0,))
                turn_b(h)
                unit("gate", 6 + h, xq, 8, 256, ms=(1,))
            step_a(2)
            pe.wait_ge(sem("yg_lo"), 4)
            unit("glu", 0, y_in, 4, 512, ms=(0, 1))
            turn_b(2)
            unit("glu", 0, y_in, 4, 512, ms=(2, 3))
            step_a(3)
            unit("ssm_out", 0, y_in, 4, 512, ms=(0, 1), ready="yssm_lo")
            turn_b(3)
            unit("ssm_out", 0, y_in, 4, 512, ms=(2, 3))
            values(3)
            unit("ssm_out", 1, y_in, 4, 512, ms=(0, 1))
            for h in range(4):
                pe.wait_ge(sem("o_sq"), h + 1)
                T.matmul(banks[4][0:4, 0:TOK], selH[:, h, :], sq[:, h % 2, :], start=(h == 0),
                         stop=(h == 3)).then_inc(sem("o_stat"), 1)
            unit("ssm_out", 1, y_in, 4, 512, ms=(2, 3))
            pe.wait_ge(sem("o_r"), 1)
            for h in range(4):
                T.matmul(banks[4 + h][:, 0:TOK], selHT[:, h, :], rs2[:, :], start=True, stop=True).then_inc(
                    sem("o_bc"), 1)
            for i in range(2):
                unit("att_out", i, (yatt_hi, yatt_lo, 0, NQ), 4, 512, ready=None if i else "yatt_lo")

            def h1_stat(m):
                pe.wait_ge(sem("h1_sq"), m + 1)
                T.matmul(banks[3][:, 0:NQ], ones[:], sq[:, m % 2, 0:NQ], start=(m == 0), stop=(m == 7)).then_inc(
                    sem("h1_stat"), 1)

            for i in range(4):
                unit("w_o", i, (mix_hi, mix_lo, 0, NQ), 8, 256, ready=None if i else "mix_lo")
                if i:
                    h1_stat(2 * i - 2)
                    h1_stat(2 * i - 1)
            h1_stat(6)
            h1_stat(7)

            def down(i):
                un = unit_at[("down", i)]["n"]
                pe.wait_ge(sem("lo_ready"), un + 1)
                pe.wait_ge(sem("ff_lo"), 2 * i + 2)
                wh = w_hi[:, un % NW, :].rearrange("p (k n) -> p k n", k=2)
                wl = w_lo[:, un % NW, :].rearrange("p (k n) -> p k n", k=2)
                for m in range(8):
                    for kt in range(2):
                        o = banks[4 + m // 2][:, 256 * (m % 2):256 * (m % 2) + 256]
                        c = slice(P * m, P * m + P)
                        first = i == 0 and kt == 0 and m % 2 == 0
                        z = i == KF // 2 - 1 and kt == 1 and m % 2 == 1
                        T.matmul(o, wh[:, kt, c], ff_hi[:, i % 2, kt, :], start=first, stop=False,
                                 skip_group_check=True)
                        T.matmul(o, wh[:, kt, c], ff_lo[:, i % 2, kt, :], start=False, stop=False,
                                 skip_group_check=True)
                        last = T.matmul(o, wl[:, kt, c], ff_hi[:, i % 2, kt, :], start=False, stop=z,
                                        skip_group_check=True)
                last.then_inc(sem("acc_unit_done"), 1)

            for i in range(KF // 2):
                unit("up_a", i, (hs_hi, hs_lo, 0, NQ), 8, 256, ready=None if i else "hs_lo")
                unit("up_b", i, (hs_hi, hs_lo, 2, NQ), 8, 256)
                if i:
                    down(i - 1)
            down(KF // 2 - 1)

            def stat(name, ready, src, k_, i, n_, cols=slice(0, 256)):
                pe.wait_ge(sem(ready), i + 1)
                T.matmul(banks[3][:, cols], ones[:], src[:, i % 2, :], start=(i == 0), stop=(i == n_ - 1)).then_inc(
                    sem(name), 1)

            for m in range(8):
                stat("x2_stat", "x2_stat_sq", sq2, None, m, 8)
            pe.wait_ge(sem("x2n_lo"), 8)
            x2n = (x2n_hi, x2n_lo, 0, 256)
            unit("lru_x", 0, x2n, 8, 256)
            unit("hg_f", 0, x2n, 8, 256)
            for m in range(2):
                taken(pe, group(("lru_x", 0), m))
            pe.wait_ge(sem("lru_w_in"), 64)
            for i in range(2):
                for m in range(2):
                    last = T.matmul(banks[6 + i][:, 256 * m:256 * m + 256], lru_w[:, i, m, :], xc[:, m, :], start=True,
                                    stop=True)
                last.then_inc(sem("lru_gate"), 1)
            unit("hg_q", 0, x2n, 8, 256)
            unit("hg_i", 0, x2n, 8, 256, (0, P))

            def h_scores(lv):
                pe.wait_ge(sem("h_level"), max(lv, 1))
                need(pe, "h_taken", lv - 1)
                if lv == 1:
                    pe.wait_ge(sem("lru_ri"), 4)
                q = hgq if lv == 0 else hqf
                for par in range(2):
                    r = slice(64 * par, 64 * par + 64)
                    bank = banks[4 + 2 * (lv % 2) + par]
                    for hp in range(2):
                        for t in range(1 if lv == 8 else 2):
                            c = P * (hp if lv == 8 else 2 * t + hp)
                            tq = P if lv == 8 else P * t
                            last = T.matmul(bank[:, c:c + P], hgk[r, hp, P * t:P * t + P], q[r, hp, tq:tq + P],
                                            start=True, stop=True)
                last.then_inc(sem("h_scores"), 1)

            for m in range(2):
                taken(pe, group(("hg_i", 0), m))
            h_scores(0)
            h_scores(1)
            unit("cq", 0, x2n, 8, 256)
            h_scores(2)
            h_scores(3)
            unit("cq", 1, x2n, 8, 256)
            h_scores(4)
            h_scores(5)
            unit("ck", 0, x2n, 8, 256)
            h_scores(6)
            unit("ck", 1, x2n, 8, 256)
            h_scores(7)
            unit("cv", 0, x2n, 8, 256, (0, P))
            h_scores(8)
            unit("cv", 1, x2n, 8, 256, (0, P))
            pe.wait_ge(sem("h_taken"), 9)
            for par in range(2):
                r = slice(64 * par, 64 * par + 64)
                for hp in range(2):
                    c = slice(64 * (2 * hp + par), 64 * (2 * hp + par) + 64)
                    T.matmul(banks[3][r, 256 * hp:256 * hp + P], hgv[:, 0, c], hA[:, 4 * par + hp, :], start=True,
                             stop=True)
                    T.matmul(banks[3][r, 256 * hp + P:256 * hp + 256], hgv[:, 0, c], hX[:, 2 * par + hp, :],
                             start=True, stop=False)
                    last = T.matmul(banks[3][r, 256 * hp + P:256 * hp + 256], hgv[:, 1, c],
                                    hA[:, 4 * par + 2 + hp, :], start=False, stop=True)
            last.then_inc(sem("hg_o"), 1)
            for m in range(2):
                pe.wait_ge(sem("hgo"), m + 2)
                T.matmul(banks[3][0:4, 0:256], sel[:, m, 0:4], sq2[:, m, :], start=(m == 0), stop=(m == 1)).then_inc(
                    sem("hg_stat"), 1)

            def m_scores(it):
                h, t = it // 2, it % 2
                need(pe, "m_max", it - 1)
                r = slice(64 * (h % 2), 64 * (h % 2) + 64)
                T.matmul(banks[4 + it % 2][:, 0:P * t + P], cq[r, h // 2, P * t:P * t + P],
                         ck[r, h // 2, 0:P * t + P], start=True, stop=True).then_inc(sem("m_s"), 1)

            def m_turn(it):
                h, t = it // 2, it % 2
                pe.wait_ge(sem("m_w"), it + 1)
                if t == 0:
                    need(pe, "m_copied", h - 1)
                    if h < 2:
                        pe.wait_ge(sem("hg_n"), h + 1)
                b = banks[6 + h % 2]
                last = T.transpose(b[:, P * t:P * t + P], mp[:, it % 2, 0:P], ident[:])
                if t:
                    last = T.transpose(b[:, 256:384], mp[:, it % 2, P:256], ident[:])
                last.then_inc(sem("m_T"), 1)

            def m_values(h):
                pe.wait_ge(sem("m_copied"), h + 1)
                if h % 2 == 0:
                    need(pe, "m_out", h // 2)
                r = slice(64 * (h % 2), 64 * (h % 2) + 64)
                c = slice(64 * h, 64 * h + 64)
                T.matmul(banks[3][r, 0:256], cv[:, 0, c], mpT[:, h % 2, 0:256], start=True, stop=False)
                T.matmul(banks[3][r, P:256], cv[:, 1, c], mpT[:, h % 2, 256:384], start=False, stop=True).then_inc(
                    sem("m_val"), 1)

            for m in range(2):
                taken(pe, group(("cv", 1), m))
            m_scores(0)
            pe.wait_ge(sem("hg_r"), 1)
            for m in range(2):
                T.matmul(banks[6 + m][:, 0:256], selT[0:4, m, :], rsm2[:, :], start=True, stop=True).then_inc(
                    sem("hg_bc"), 1)
            for it in range(16):
                if it < 15:
                    m_scores(it + 1)
                if it == 0:
                    unit("hg_g", 0, x2n, 8, 256)
                if it == 2:
                    unit("lru_y", 0, x2n, 8, 256)
                m_turn(it)
                if it == 4:
                    need(pe, "m_out", 0)
                    for m in range(2):
                        stat("ya_stat", "ya_sq", sq2, None, m, 2, slice(256, 512))
                    pe.wait_ge(sem("ya_rms"), 1)
                if it % 2 == 1 and it >= 5:
                    m_values((it - 5) // 2)
            m_values(6)
            m_values(7)
            for p_ in range(4):
                stat("yc_stat", "yc_sq", sq2, None, p_, 4)
            pe.wait_ge(sem("ycat_lo"), 8)
            for i in range(4):
                unit("w_out2", i, (ycat_hi, ycat_lo, 0, 256), 8, 256)
                if i:
                    stat("x3_stat", "x3_stat_sq", sq2, None, 2 * i - 2, 8)
                    stat("x3_stat", "x3_stat_sq", sq2, None, 2 * i - 1, 8)
            stat("x3_stat", "x3_stat_sq", sq2, None, 6, 8)
            stat("x3_stat", "x3_stat_sq", sq2, None, 7, 8)
            for t in range(2):
                for kt in range(KD):
                    T.matmul(banks[4 + 2 * t + kt // 4][:, P * (kt % 4):P * (kt % 4) + P], x2[:, kt, P * t:P * t + P],
                             ident[:], start=(kt % 4 == 0), stop=False, skip_group_check=True)
            pe.wait_ge(sem("x3_lo"), 8)

            def ff2(i):
                un = unit_at[("ff2", i)]["n"]
                pe.wait_ge(sem("lo_ready"), un + 1)
                pe.wait_ge(sem("u_lo"), 2 * i + 2)
                wh = w_hi[:, un % NW, :].rearrange("p (k n) -> p k n", k=2)
                wl = w_lo[:, un % NW, :].rearrange("p (k n) -> p k n", k=2)
                for kt in range(2):
                    for t in range(2):
                        uh = u_hi[:, i % 2, kt, P * t:P * t + P]
                        ul = u_lo[:, i % 2, kt, P * t:P * t + P]
                        for h in range(2):
                            z = i == KF2 // 2 - 1 and kt == 1
                            c = slice(512 * h, 512 * h + 512)
                            o = banks[4 + 2 * t + h]
                            T.matmul(o, uh, wh[:, kt, c], start=False, stop=False, skip_group_check=True)
                            T.matmul(o, uh, wl[:, kt, c], start=False, stop=False, skip_group_check=True)
                            last = T.matmul(o, ul, wh[:, kt, c], start=False, stop=z, skip_group_check=True)
                last.then_inc(sem("acc_unit_done"), 1)

            for i in range(KF2 // 2):
                unit("ff1", i, x2n, 8, 256)
                if i:
                    ff2(i - 1)
            ff2(KF2 // 2 - 1)


_INS = ["x", "meta_tokens", "norm1_g", "w_in", "ssm_a_re", "ssm_a_im", "ssm_log_dt", "ssm_b_re", "ssm_b_im", "ssm_c_re",
        "ssm_c_im", "ssm_d", "ssm_glu_w", "ssm_glu_b", "q_norm_g", "k_norm_g", "lam_q1", "lam_k1", "lam_q2", "lam_k2",
        "subln_g", "w_ssm_out", "w_att_out", "w_o", "norm2_g", "w_up", "conv_w", "conv_b", "w_down", "w_in_2",
        "w_out_2", "norm_mix_2", "norm_mlp_2", "lru_conv_w_2", "lru_conv_b_2", "lru_wa_2", "lru_ba_2", "lru_wx_2",
        "lru_bx_2", "lru_lambda_2", "hg_lower_bounds_2", "hg_norm_w_2", "lru_out_norm_2", "att_out_norm_2", "w_ff1_2",
        "w_ff2_2", "norm_final_2"]


def kernel(**inputs):
    import numpy as _np
    import concourse.bacc as _bacc
    from concourse import mybir as _mybir
    from concourse.bass_utils import run_bass_kernel_spmd as _run

    nc = _bacc.Bacc("TRN2", target_bir_lowering=False, num_devices=1)
    arrays, args = {}, {}
    for name in _INS:
        a = _np.ascontiguousarray(inputs[name])
        arrays[f"in_{name}_dram"] = a
        args[name] = nc.dram_tensor(f"in_{name}_dram", a.shape, _mybir.dt.from_np(a.dtype), kind="ExternalInput").ap()
    out = nc.dram_tensor("out_0_dram", (1, SEQ, D), _mybir.dt.float32, kind="ExternalOutput").ap()
    program(nc, args, out)
    r = _run(nc, [arrays], core_ids=[0])
    return r.results[0]["out_0_dram"]
```

```python
import concourse.bass as bass
from concourse import mybir
from contextlib import ExitStack

F32 = mybir.dt.float32
F32R = mybir.dt.float32r
I32 = mybir.dt.int32
ALU = mybir.AluOpType
ACT = mybir.ActivationFunctionType
AXX = mybir.AxisListType.X

P = 128
D = 1024
KD = D // P
META = 16
SEQ = 256
TOK = META + SEQ
T0 = META - 2
NQ = TOK - T0
FF = 2816
KF = FF // P
FF2 = 4 * D
KF2 = FF2 // P
NS = 16
LC = TOK // 2
EPS = 1e-6
BIG = 1e30 * 256.0
TINY = 1e-30
SQRT_MIN = 2.0 ** -110
TWO_PI_1 = 6.28125
TWO_PI_2 = 0.0019350051879882812
TWO_PI_3 = 3.0198120544e-07
INV_TWO_PI = 0.15915494309189535
ROUND = 12582912.0
NRAW, NW = 3, 3
UNIT = 2048
CONSTANTS = {"ident": 1, "small": 2, "ones": 3, "half": 4, "sel": 5, "bias": 6, "masks": 7}
NH = 4
NM = 4
NB = 3
KEYS_B = META + P
POOL_LO = range(3, 23)
PROWS = {}
at_ = 0
for name_, n_ in (("norm1", 8), ("a_re", 16), ("a_im", 16), ("ssm_d", 4), ("glu_b", 4), ("qn", 1), ("kn", 1),
                  ("subln", 1), ("norm2", 8), ("conv_b", 22), ("norm_mix", 8), ("norm_mlp", 8), ("att_norm", 4),
                  ("lru_norm", 2), ("hg_norm", 1)):
    PROWS[name_] = at_
    at_ += n_
NP1 = at_
PROWS2 = {}
at_ = 0
for name_, n_ in (("conv_w", 66), ("lru_w", 8), ("lru_b", 2), ("lru_ba", 2), ("lru_bx", 2), ("lru_lam", 2),
                  ("hg_lb", 2)):
    PROWS2[name_] = at_
    at_ += n_
NP2 = at_
PTILES = [(0, 8), (8, 36), (44, NP1 - 44), (0, NP2)]


def weight_units(ins):
    def rows(w):
        return w.rearrange("(k p) n -> p k n", p=P)
    units = []

    def add(name, src, kk, kind, groups):
        units.append(dict(name=name, src=src, kk=kk, kind=kind, groups=groups))

    w_in = rows(ins["w_in"][0])
    for name, c0 in (("u", 0), ("k", 1024), ("q", 512)):
        for i in range(2):
            add((name, i), w_in[:, :, c0 + 256 * i:c0 + 256 * i + 256], 8, "feat", 2)
    for i in range(2):
        add(("v", i), w_in[:, :, 1536 + 256 * i:1792 + 256 * i], 8, "tok", 3)
    for i in range(8):
        if i == 6:
            add(("glu", 0), rows(ins["ssm_glu_w"][0]), 4, "feat", 4)
        add(("gate", i), w_in[:, :, 2048 + 256 * i:2304 + 256 * i], 8, "feat", 2)
    for name, key in (("ssm_out", "w_ssm_out"), ("att_out", "w_att_out")):
        for i in range(2):
            add((name, i), rows(ins[key][0])[:, :, 512 * i:512 * i + 512], 4, "feat", 4)
    for i in range(4):
        add(("w_o", i), rows(ins["w_o"][0])[:, :, 256 * i:256 * i + 256], 8, "feat", 2)
    w_up, w_down = rows(ins["w_up"][0]), rows(ins["w_down"][0])
    for i in range(KF // 2 + 1):
        if i < KF // 2:
            add(("up_a", i), w_up[:, :, 256 * i:256 * i + 256], 8, "feat", 2)
            add(("up_b", i), w_up[:, :, FF + 256 * i:FF + 256 * i + 256], 8, "feat", 2)
        if i:
            add(("down", i - 1), w_down[:, 2 * i - 2:2 * i, :], 2, "acc", 0)
    w2 = rows(ins["w_in_2"][0])
    for name, c0, n in (("lru_x", 0, 1), ("hg_f", 768, 1), ("hg_q", 512, 1), ("hg_i", 1024, 1), ("cq", 1536, 2),
                        ("ck", 2048, 2), ("cv", 2560, 2), ("hg_g", 1280, 1), ("lru_y", 256, 1)):
        for i in range(n):
            tok = name in ("hg_i", "cv")
            add((name, i), w2[:, :, c0 + 256 * i:c0 + 256 * i + 256], 8, "tok" if tok else "feat", 2)
    for i in range(4):
        add(("w_out2", i), rows(ins["w_out_2"][0])[:, :, 256 * i:256 * i + 256], 8, "feat", 2)
    w_ff1, w_ff2 = rows(ins["w_ff1_2"][0]), rows(ins["w_ff2_2"][0])
    for i in range(KF2 // 2 + 1):
        if i < KF2 // 2:
            add(("ff1", i), w_ff1[:, :, 256 * i:256 * i + 256], 8, "feat", 2)
        if i:
            add(("ff2", i - 1), w_ff2[:, 2 * i - 2:2 * i, :], 2, "acc", 0)
    g = a = 0
    for n, u in enumerate(units):
        u["n"], u["g0"] = n, g
        g += u["groups"]
        a += u["kind"] == "acc"
        u["acc_done"] = a
    return units


def program(nc, ins, out):
    ctx = ExitStack()
    with ctx:
        sems = {}

        def sem(name):
            if name not in sems:
                sems[name] = ctx.enter_context(nc.semaphore(name))
            return sems[name]

        base = 16512
        top = [base]

        def sb(name, shape, dt=F32, at=None):
            size = 4
            for n in shape[1:]:
                size *= n
            size = (size + 31) // 32 * 32
            if at is None:
                at = top[0]
                top[0] += size
            assert at + size <= 229344, name
            return nc.alloc_sbuf_tensor_at(name, list(shape), dt, offset=at)

        units = weight_units(ins)
        unit_at = {u["name"]: u for u in units}

        raw = sb("w_raw", [P, NRAW, UNIT])
        w_hi = sb("w_hi", [P, NW, UNIT], F32R)
        w_lo = sb("w_lo", [P, NW, UNIT], F32R)
        ident = sb("ident", [P, P])
        ones = sb("ones", [P, P])
        sel = sb("sel", [P, 8, 16])
        selT = sb("selT", [16, 8, P])
        selH = sb("selH", [P, 4, 4])
        selHT = sb("selHT", [4, 4, P])
        C1 = sb("C1", [P, NP1])
        C2 = sb("C2", [P, NP2])
        neg_dist = sb("neg_dist", [P, 272])
        bias = sb("bias", [P, 8, 272])
        small = sb("small", [P, 86, 16])
        R = top[0]
        k = lambda off: R + off

        def col(name, i=0, n=1):
            if name in PROWS:
                return C1[:, PROWS[name] + i:PROWS[name] + i + n]
            return C2[:, PROWS2[name] + i:PROWS2[name] + i + n]

        xn_hi = sb("xn_hi", [P, KD, TOK], F32R, k(0))
        xn_lo = sb("xn_lo", [P, KD, TOK], F32R, k(8704))
        mix_hi = sb("mix_hi", [P, KD, NQ], F32R, k(0))
        mix_lo = sb("mix_lo", [P, KD, NQ], F32R, k(8704))
        hT = sb("hT", [P, KD, NQ], F32, k(17408))
        xtok = sb("xtok", [P, 3, D], F32, k(25664))
        yg = sb("yg", [P, 4, TOK], F32, k(25664))
        yg_hi = sb("yg_hi", [P, 4, NQ], F32R, k(30016))
        yg_lo = sb("yg_lo", [P, 4, NQ], F32R, k(34144))
        uT = sb("uT", [P, 4, TOK], F32, k(38272))
        qkT = sb("qkT", [P, 8, TOK], F32, k(42624))
        v_tok = sb("v_tok", [P, 3, 512], F32, k(51328))
        Ec = sb("Ec", [P, NS, LC], F32, k(57472))
        Es = sb("Es", [P, NS, LC], F32, k(66176))
        mprod = sb("mprod", [P, NM, 4, 2 * LC], F32, k(74880))
        zbuf = sb("zbuf", [P, 2, 2 * LC], F32, k(92288))
        xr = sb("xr", [P, 3, D], F32, k(74880))
        BT = sb("BT", [P, 4, 2, P], F32, k(30016))
        CT = sb("CT", [P, 4, 2, P], F32, k(34112))
        gate = sb("gate", [P, 16, NQ], F32, k(98304))
        b_raw = sb("b_raw", [P, 2, NS, 16], F32, k(98304))
        b_prod = sb("b_prod", [P, 4, NS, 16], F32, k(100352))
        b_blk = sb("b_blk", [P, 2, NS, 2, 16], F32, k(104448))
        c_raw = sb("c_raw", [P, 2, 4, 64], F32, k(108544))
        c_blk = sb("c_blk", [P, 2, 4, 2, 64], F32, k(110592))
        lamv = sb("lamv", [P, 4, 64], F32, k(53504))
        params = sb("params", [P, 4, P], F32, k(51328))
        log_dt = sb("log_dt", [P, 32], F32, k(53376))
        junk_x = sb("junk_x", [P, D], F32, k(57472))
        e_tmp = sb("e_tmp", [P, 2, NS, 64], F32, k(74880))
        glu_t = sb("glu_t", [P, 4, NQ], F32, k(38272))
        eps_col = small[:, 83, 0:1]
        A0 = 57472
        p_a = sb("p_a", [P, 2, TOK], F32, k(A0))
        p_b = sb("p_b", [P, 2, 2, KEYS_B], F32, k(A0 + 2176))
        w_a = sb("w_a", [P, TOK], F32, k(A0 + 4480))
        w_b = sb("w_b", [P, 2, KEYS_B], F32, k(A0 + 5568))
        wT0 = sb("wT0", [16, TOK], F32, k(A0 + 6720))
        wT12 = sb("wT12", [P, 384], F32, k(A0 + 7808))
        oT = sb("oT", [P, 4, TOK], F32, k(A0 + 9344))
        yatt_hi = sb("yatt_hi", [P, 4, NQ], F32R, k(A0 + 13696))
        yatt_lo = sb("yatt_lo", [P, 4, NQ], F32R, k(A0 + 17824))
        sq = sb("sq", [P, 2, TOK], F32, k(A0 + 21952))
        rs = sb("rs", [16, TOK], F32, k(A0 + 24128))
        rs2 = sb("rs2", [4, TOK], F32, k(A0 + 25216))
        rstd = sb("rstd", [P, NQ], F32, k(A0 + 28480))
        sqsum = sb("sqsum", [P, NQ], F32, k(A0 + 29536))
        hs_hi = sb("hs_hi", [P, KD, NQ], F32R, k(98304))
        hs_lo = sb("hs_lo", [P, KD, NQ], F32R, k(106560))
        hs = sb("hs", [P, NH, NQ], F32, k(A0))
        cv_ = sb("cv_", [P, 2, 2, 256], F32, k(A0))
        gl = sb("gl", [P, 2, 2, 256], F32, k(A0 + 4096))
        ff_hi = sb("ff_hi", [P, 2, 2, 256], F32R, k(A0 + 8192))
        ff_lo = sb("ff_lo", [P, 2, 2, 256], F32R, k(A0 + 12288))
        ff = sb("ff", [P, 2, 2, 256], F32, k(A0 + 16384))
        x2 = sb("x2", [P, KD, 256], F32, k(25664))

        x2n_hi = sb("x2n_hi", [P, KD, 256], F32R, k(0))
        x2n_lo = sb("x2n_lo", [P, KD, 256], F32R, k(8704))
        hgv = sb("hgv", [P, 2, 256], F32, k(17408))
        masks = sb("masks", [P, 8, P], F32, k(19456))
        hgg = sb("hgg", [P, 2, 256], F32, k(23552))
        ycat_hi = sb("ycat_hi", [P, KD, 256], F32R, k(33856))
        ycat_lo = sb("ycat_lo", [P, KD, 256], F32R, k(42048))
        xc = sb("xc", [P, 2, 256], F32, k(50240))
        lru_r = sb("lru_r", [P, 2, 256], F32, k(52288))
        lru_i = sb("lru_i", [P, 2, 256], F32, k(54336))
        lru_a = sb("lru_a", [P, 2, 256], F32, k(56384))
        lru_t = sb("lru_t", [P, 2, 256], F32, k(58432))
        lru_g = sb("lru_g", [P, 2, 256], F32, k(60480))
        hgq = sb("hgq", [P, 2, 256], F32, k(62528))
        hgk = sb("hgk", [P, 2, 256], F32, k(64576))
        hgf = sb("hgf", [P, 2, 256], F32, k(66624))
        hqf = sb("hqf", [P, 2, 256], F32, k(68672))
        htot = sb("htot", [P, 512], F32, k(70720))
        hA = sb("hA", [P, 8, P], F32, k(72768))
        hX = sb("hX", [P, 4, P], F32, k(76864))
        hgo = sb("hgo", [P, 2, 256], F32, k(78912))
        cq = sb("cq", [P, 4, 256], F32, k(80960))
        ck = sb("ck", [P, 4, 256], F32, k(85056))
        cv = sb("cv", [P, 2, 512], F32, k(89152))
        mp = sb("mp", [P, 2, 384], F32, k(93248))
        mpT = sb("mpT", [P, 2, 384], F32, k(96320))
        mo = sb("mo", [P, 4, 256], F32, k(99392))
        sq2 = sb("sq2", [P, 2, 256], F32, k(103488))
        rst2 = sb("rst2", [P, 256], F32, k(105536))
        rsm2 = sb("rsm2", [4, 256], F32, k(106560))
        tmp2 = sb("tmp2", [P, NH, 256], F32, k(89152))
        lru_w = sb("lru_w", [P, 2, 2, P], F32, k(109632))
        rst3 = sb("rst3", [P, 256], F32, k(111680))
        relu = sb("relu", [P, 2, 2, 256], F32, k(50240))
        uu = sb("uu", [P, 2, 2, 256], F32, k(54336))
        u_hi = sb("u_hi", [P, 2, 2, 256], F32R, k(58432))
        u_lo = sb("u_lo", [P, 2, 2, 256], F32R, k(62528))
        outb = sb("outb", [P, 2, D], F32, k(66624))
        nf = sb("nf", [P, D], F32, k(74816))
        sqj = sb("sqj", [P, 2, 512], F32, k(78912))

        psum = ctx.enter_context(nc.psum_tensor("psum", [P, 8, 512], F32))
        banks = [psum[:, i, :] for i in range(8)]

        slot = {}

        def sm(name, n=16):
            if name not in slot:
                slot[name] = len(slot) + 2
            return small[:, slot[name], 0:n]

        def need(eng, name, n):
            if n > 0:
                eng.wait_ge(sem(name), n)

        def used(eng, n):
            if n < 0:
                return
            u = units[n]
            if u["kind"] == "acc":
                if u["name"] == ("down", KF // 2 - 1):
                    eng.wait_ge(sem("down_done"), 4)
                else:
                    need(eng, "acc_unit_done", u["acc_done"] - (u["name"][0] == "ff2"))
            else:
                need(eng, "group_done", u["g0"] + u["groups"])

        def free_count(g):
            return g // NB

        def taken(eng, g):
            eng.wait_ge(sem(f"group_free{g % NB}"), free_count(g) + 1)

        def group(name, m):
            u = unit_at[name]
            return u["g0"] + m

        def par(eng, signal, dst, src):
            eng.dma_start(dst, src).then_inc(sem(signal), 16)

        def par_rows(eng, signal, tile, row, key):
            src = ins[key][0]
            if len(src.shape) == 2:
                src = src.rearrange("a b -> (a b)")
            cnt = src.shape[0] // P
            par(eng, signal, params[:, tile][row:row + cnt, :], src.rearrange("(r c) -> r c", c=P))

        pool_units = [unit_at[name] for name in (("up_a", 0), ("up_b", 0), ("lru_x", 0), ("hg_f", 0), ("w_out2", 0),
                                                 ("w_out2", 1), ("ff1", 0))]

        block = ctx.enter_context(nc.Block())

        @block.sync
        def _(sp):
            x = ins["x"]
            sp.dma_start(xtok[0:META, 0, :], ins["meta_tokens"]).then_inc(sem("meta_in"), 16)
            for t in range(2):
                sp.dma_start(xtok[:, 1 + t, :], x[0, P * t:P * t + P, :]).then_inc(sem(f"x_in{t}"), 16)
            par_rows(sp, "par0_in", 0, 0, "norm1_g")
            for u in units:
                n = u["n"]
                need(sp, "hi_ready", n - NRAW + 1)
                need(sp, "lo_ready", n - NRAW + 1)
                dst = raw[:, n % NRAW, :].rearrange("p (k n) -> p k n", k=u["kk"])
                sp.dma_start(dst, u["src"]).then_inc(sem(f"w_in{n % NRAW}"), 16)
                if n == 0:
                    par(sp, "ssm_in", log_dt[:, :], ins["ssm_log_dt"].to_broadcast([P, 32]))
                    for name, key in (("a_re", "ssm_a_re"), ("a_im", "ssm_a_im"), ("ssm_d", "ssm_d")):
                        par_rows(sp, "ssm_in", 1, PROWS[name] - PROWS["a_re"], key)
                    for i, key in enumerate(("ssm_b_re", "ssm_b_im")):
                        par(sp, "bc_in", b_raw[:, i], ins[key][0].rearrange("(j g) p c -> (g p) j c", g=2))
                    for i, key in enumerate(("ssm_c_re", "ssm_c_im")):
                        par(sp, "bc_in", c_raw[:, i], ins[key][0].rearrange("(a g) c p -> (g c) a p", g=8))
                if n == NRAW - 1:
                    for name, key in (("glu_b", "ssm_glu_b"), ("norm2", "norm2_g"), ("conv_b", "conv_b"),
                                      ("subln", "subln_g"), ("norm_mix", "norm_mix_2"), ("norm_mlp", "norm_mlp_2"),
                                      ("att_norm", "att_out_norm_2"), ("lru_norm", "lru_out_norm_2")):
                        par_rows(sp, "par_in", 2, PROWS[name] - PROWS["glu_b"], key)
                    for name, key in (("qn", "q_norm_g"), ("kn", "k_norm_g"), ("hg_norm", "hg_norm_w_2")):
                        r = PROWS[name] - PROWS["glu_b"]
                        for j in range(2):
                            par(sp, "par_in", params[:, 2][r:r + 1, 64 * j:64 * j + 64], ins[key])
                    for name, key in (("conv_w", "conv_w"), ("lru_w", "lru_conv_w_2"), ("lru_b", "lru_conv_b_2"),
                                      ("lru_ba", "lru_ba_2"), ("lru_bx", "lru_bx_2"), ("lru_lam", "lru_lambda_2"),
                                      ("hg_lb", "hg_lower_bounds_2")):
                        par_rows(sp, "par_in", 3, PROWS2[name], key)
                    for i, key in enumerate(("lam_q1", "lam_k1", "lam_q2", "lam_k2")):
                        par(sp, "lam_in", lamv[:, i], ins[key].to_broadcast([P, 64]))
                if u["name"] == ("ff2", 0):
                    sp.wait_ge(sem("x3_hi"), 8)
                    sp.dma_start(nf[:, :], ins["norm_final_2"].rearrange("(a d) -> a d", a=1).to_broadcast(
                        [P, D])).then_inc(sem("nf_in"), 16)
            for t in range(2):
                for h in range(2):
                    c = slice(512 * h, 512 * h + 512)
                    sp.wait_ge(sem("out_ready"), 2 * t + h + 1)
                    sp.dma_start(out[0, P * t:P * t + P, c], outb[:, t, c]).then_inc(sem("out_done"), 16)
            sp.wait_ge(sem("out_done"), 64)

        @block.gpsimd
        def _(pool):
            n = [0]

            def seq(i):
                n[0] += 1
                i.then_inc(sem("pool_seq"), 1)
                pool.wait_ge(sem("pool_seq"), n[0])

            seq(pool.memset(ident[:], 0.0))
            pool.affine_select(out=ident[:], in_=ident[:], compare_op=ALU.not_equal, fill=1.0, base=0,
                               pattern=[[-1, P]], channel_multiplier=1).then_inc(sem("constants"), 1)
            seq(pool.memset(small[:, 0:2, :], 1.0))
            pool.memset(small[:, 83, :], EPS).then_inc(sem("constants"), 1)
            pool.memset(ones[:], 1.0).then_inc(sem("constants"), 1)
            half = small[:, 84, 0:8].rearrange("p (g a) -> p g a", g=2)
            seq(pool.memset(small[:, 84, 0:8], 1.0))
            seq(pool.affine_select(out=half, in_=half, compare_op=ALU.is_ge, fill=0.0, base=0,
                                   pattern=[[-16, 2], [-32, 4]], channel_multiplier=1))
            pool.affine_select(out=half, in_=half, compare_op=ALU.is_ge, fill=0.0, base=15,
                               pattern=[[16, 2], [32, 4]], channel_multiplier=-1).then_inc(sem("constants"), 1)
            seq(pool.memset(b_blk[:], 0.0))
            seq(pool.memset(sel[:], 1.0))
            seq(pool.affine_select(out=sel[:], in_=sel[:], compare_op=ALU.is_ge, fill=0.0, base=0,
                                   pattern=[[128, 8], [-64, 16]], channel_multiplier=1))
            seq(pool.affine_select(out=sel[:], in_=sel[:], compare_op=ALU.is_ge, fill=0.0, base=63,
                                   pattern=[[-128, 8], [64, 16]], channel_multiplier=-1))
            seq(pool.memset(selT[:], 1.0))
            seq(pool.affine_select(out=selT[:], in_=selT[:], compare_op=ALU.is_ge, fill=0.0, base=0,
                                   pattern=[[128, 8], [1, P]], channel_multiplier=-64))
            seq(pool.affine_select(out=selT[:], in_=selT[:], compare_op=ALU.is_ge, fill=0.0, base=63,
                                   pattern=[[-128, 8], [-1, P]], channel_multiplier=64))
            seq(pool.memset(selH[:], 0.0))
            for h in range(4):
                seq(pool.memset(selH[:, h, h:h + 1], 1.0))
            seq(pool.memset(selHT[:], 1.0))
            seq(pool.affine_select(out=selHT[:], in_=selHT[:], compare_op=ALU.is_equal, fill=0.0, base=0,
                                   pattern=[[-1, 4], [0, P]], channel_multiplier=1))
            seq(pool.iota(neg_dist[:], [[1, TOK]], base=-144, channel_multiplier=-1,
                          allow_small_or_imprecise_dtypes=True))
            seq(pool.affine_select(out=neg_dist[:], in_=neg_dist[:], compare_op=ALU.is_ge, fill=-BIG, base=144,
                                   pattern=[[-1, TOK]], channel_multiplier=1))
            pool.memset(small[:, 85, 1:2], 0.0).then_inc(sem("constants"), 1)

            for i in range(8):
                seq(pool.tensor_scalar(bias[:, i, :], neg_dist[:], 2.0 ** -(i + 1), None, ALU.mult))
            pool.memset(small[:, 85, 2:3], 0.0).then_inc(sem("constants"), 1)
            pool.wait_ge(sem("bc_in"), 64)
            pool.wait_ge(sem("f_ready"), 1)
            fre = sm("fre")[:, :, None].to_broadcast([P, NS, 16])
            fim = sm("fim")[:, :, None].to_broadcast([P, NS, 16])
            for i, (part, f) in enumerate(((0, fre), (1, fim), (1, fre), (0, fim))):
                seq(pool.tensor_tensor(b_prod[:, i], b_raw[:, part], f, ALU.mult))
            for g in range(2):
                r = slice(64 * g, 64 * g + 64)
                pool.tensor_tensor(b_blk[r, 0, :, g, :], b_prod[r, 0], b_prod[r, 1], ALU.subtract).then_inc(
                    sem("bc_blk"), 1)
                pool.wait_ge(sem("bc_blk"), 2 * g + 1)
                pool.tensor_tensor(b_blk[r, 1, :, g, :], b_prod[r, 2], b_prod[r, 3], ALU.add).then_inc(
                    sem("bc_blk"), 1)
                pool.wait_ge(sem("bc_blk"), 2 * g + 2)
            for i in range(2):
                for g in range(2):
                    pool.tensor_scalar(c_blk[:, i, :, g, :], c_raw[:, i], sm("halfc", 2)[:, g:g + 1], None,
                                       ALU.mult).then_inc(sem("bc_blk"), 1)

            def s5_w(b):
                pool.wait_ge(sem("s5_m"), b + 1)
                m = mprod[:, b % NM]
                pool.tensor_tensor(m[:, 0], m[:, 0], m[:, 1], ALU.add).then_inc(sem("s5_w"), 1)
                pool.tensor_tensor(m[:, 2], m[:, 2], m[:, 3], ALU.subtract).then_inc(sem("s5_w"), 1)

            def lo_half(half_):
                u, c = POOL_LO[half_ // 2], slice(UNIT // 2 * (half_ % 2), UNIT // 2 * (half_ % 2) + UNIT // 2)
                pool.wait_ge(sem("hi_ready"), u + 1)
                i = pool.tensor_tensor(w_lo[:, u % NW, c], raw[:, u % NRAW, c], w_hi[:, u % NW, c].bitcast(F32),
                                       ALU.subtract)
                if half_ % 2:
                    i.then_inc(sem("lo_ready"), 1)
                else:
                    seq(i)

            pool.wait_ge(sem("lo_ready"), POOL_LO[0])
            for b in range(16):
                if b == 0:
                    for i in range(6):
                        lo_half(i)
                s5_w(b)
                lo_half(b + 6)
            for half_ in range(22, 2 * len(POOL_LO)):
                lo_half(half_)

            def lo_unit(name):
                u = unit_at[name]["n"]
                pool.wait_ge(sem("hi_ready"), u + 1)
                pool.wait_ge(sem("lo_ready"), u)
                pool.tensor_tensor(w_lo[:, u % NW, :], raw[:, u % NRAW, :], w_hi[:, u % NW, :].bitcast(F32),
                                   ALU.subtract).then_inc(sem("lo_ready"), 1)

            def norm_low(hi, lo, src, src_hi, src_lo):
                for m in range(8):
                    pool.wait_ge(sem(hi), m + 1)
                    pool.tensor_tensor(src_lo[:, m, :], src[:, m % NH, :], src_hi[:, m, :].bitcast(F32),
                                       ALU.subtract).then_inc(sem(lo), 1)

            lo_unit(("up_a", 0))
            lo_unit(("up_b", 0))
            norm_low("hs_hi", "hs_lo", hs, hs_hi, hs_lo)
            b_last = unit_at[("up_b", KF // 2 - 1)]
            pool.wait_ge(sem("group_done"), b_last["g0"] + 2)
            seq(pool.memset(lru_w[:], 0.0))
            for i, key in enumerate(("lru_wa_2", "lru_wx_2")):
                for g in range(2):
                    r = slice(64 * g, 64 * g + 64)
                    pool.dma_start(lru_w[r, i, :, r], ins[key][0, g:4:2].rearrange("t i j -> i t j")).then_inc(
                        sem("lru_w_in"), 16)
            lo_unit(("lru_x", 0))
            lo_unit(("hg_f", 0))
            norm_low("x2n_hi", "x2n_lo", tmp2, x2n_hi, x2n_lo)
            pool.wait_ge(sem("x2_ready"), 8)
            for lv in range(8):
                m = masks[:, lv, :]
                seq(pool.memset(m, 1.0))
                if lv == 0:
                    seq(pool.affine_select(out=m, in_=m, compare_op=ALU.is_equal, fill=0.0, base=0,
                                           pattern=[[-1, P]], channel_multiplier=1))
                    continue
                L = 1 << (lv - 1)
                mv = m.rearrange("p (b h l) -> p b h l", h=2, l=L)
                seq(pool.memset(mv[:, :, 0, :], 0.0))
                mv = mv[:, :, 1, :]
                seq(pool.affine_select(out=mv, in_=mv, compare_op=ALU.is_ge, fill=0.0, base=0,
                                       pattern=[[-2 * L, P // (2 * L)], [0, L]], channel_multiplier=1))
                seq(pool.affine_select(out=mv, in_=mv, compare_op=ALU.is_ge, fill=0.0, base=L - 1,
                                       pattern=[[2 * L, P // (2 * L)], [0, L]], channel_multiplier=-1))
            pool.memset(hA[:], 0.0).then_inc(sem("constants"), 1)
            for name in (("w_out2", 0), ("w_out2", 1), ("ff1", 0)):
                lo_unit(name)
            norm_low("x3_hi", "x3_lo", tmp2, x2n_hi, x2n_lo)

        @block.scalar
        def _(act):
            A = nc.scalar

            act.wait_ge(sem("constants"), CONSTANTS["small"])
            A.activation(small[:, 1, 8:9], eps_col, ACT.Sqrt)
            ss = small[:, 0, 0:3]
            for t, rows, signal in ((0, META, "meta_in"), (1, P, "x_in0")):
                act.wait_ge(sem(signal), 16)
                A.activation(junk_x[0:rows, :], xtok[0:rows, t, :], ACT.Square,
                             accum_out=small[0:rows, 0, t:t + 1]).then_inc(sem("x_sq"), 1)
                act.wait_ge(sem("x_sq"), t + 1)
            act.wait_ge(sem("x_sq2"), 1)
            A.activation(small[:, 1, 0:3], ss, ACT.Sqrt, bias=eps_col, scale=1.0 / D).then_inc(sem("x_rms"), 1)

            done = [0]

            def split_to(n):
                while done[0] < min(n, len(units)):
                    u = done[0]
                    act.wait_ge(sem(f"w_in{u % NRAW}"), 16 * (u // NRAW + 1))
                    used(act, u - NW)
                    A.activation(w_hi[:, u % NW, :], raw[:, u % NRAW, :], ACT.Copy).then_inc(sem("hi_ready"), 1)
                    done[0] += 1

            def evac(name, i, fn, ms=None):
                u = unit_at[(name, i)]
                for m in ms or range(u["groups"]):
                    g = u["g0"] + m
                    act.wait_ge(sem("group_done"), g + 1)
                    fn(m, banks[g % NB]).then_inc(sem(f"group_free{g % NB}"), 1)

            split_to(1)
            for kt in range(KD):
                act.wait_ge(sem("xrT"), kt + 1)
                if kt == 0:
                    act.wait_ge(sem("C_ready"), 1)
                A.activation(xn_hi[:, kt, :], banks[4 + kt % 4][:, 0:TOK], ACT.Copy,
                             scale=col("norm1", kt)).then_inc(sem("xn_hi"), 1)
            split_to(2)
            act.wait_ge(sem("ssm_in"), 64)
            for g in range(2):
                r = slice(64 * g, 64 * g + 64)
                A.activation(sm("dt")[r], log_dt[r, g:32:2], ACT.Exp).then_inc(sem("s5p_a"), 1)
            act.wait_ge(sem("s5p_v"), 1)
            A.activation(sm("mag"), sm("zr"), ACT.Exp).then_inc(sem("s5p_a"), 1)
            A.activation(sm("tnh"), sm("zr"), ACT.Tanh, scale=0.5).then_inc(sem("s5p_a"), 1)
            act.wait_ge(sem("s5p_v"), 2)
            A.activation(sm("sin"), sm("thr"), ACT.Sin).then_inc(sem("s5p_a"), 1)
            A.activation(sm("sinh_"), sm("thr"), ACT.Sin, scale=0.5).then_inc(sem("s5p_a"), 1)
            split_to(3)
            evac("u", 0, lambda m, b: A.activation(uT[:, m, :], b[:, 0:TOK], ACT.Copy))
            split_to(4)
            for kt in range(KD):
                act.wait_ge(sem("xT"), kt + 1)
                A.activation(hT[:, kt, :], banks[4 + kt % 4][:, T0:TOK], ACT.Copy).then_inc(sem("hT_copy"), 1)
            act.wait_ge(sem("lam_v"), 2)
            A.activation(sm("lam_e", 2), sm("lam_s", 2), ACT.Exp).then_inc(sem("lam_a"), 1)
            evac("u", 1, lambda m, b: A.activation(uT[:, 2 + m, :], b[:, 0:TOK], ACT.Copy))
            for i in range(2):
                split_to(5 + i)
                evac("k", i, lambda m, b: A.activation(qkT[:, 2 * i + m, :], b[:, 0:TOK], ACT.Copy))
            for i in range(4):
                act.wait_ge(sem("bcT"), i + 1)
                dst = (BT, BT, CT, CT)[i][:, :, i % 2, :]
                A.activation(dst, banks[4 + i][:, :].rearrange("p (a b) -> p a b", a=4), ACT.Copy,
                             scale=-1.0 if i == 3 else 1.0).then_inc(sem("bc_ready"), 1)
            for i in range(2):
                split_to(7 + i)
                evac("q", i, lambda m, b: A.activation(qkT[:, 4 + 2 * i + m, :], b[:, 0:TOK], ACT.Copy))
            vrows = (META, P, P)
            for i in range(2):
                split_to(9 + i)
                evac("v", i, lambda m, b: A.activation(v_tok[0:vrows[m], m, 256 * i:256 * i + 256],
                                                       b[0:vrows[m], 0:256], ACT.Copy))

            def gates(i, ms=(0, 1)):
                if i == 0:
                    act.wait_ge(sem("bcT"), 4)
                evac("gate", i, lambda m, b: A.activation(gate[:, 2 * i + m, :], b[:, 0:NQ], ACT.Tanh, scale=0.5), ms)

            for i in range(4):
                split_to(unit_at[("gate", i)]["n"] + 3)
                gates(i)
            for i in range(8):
                need(act, "qk_stat", i - 1)
                if i == 0:
                    act.wait_ge(sem("s5_out"), 8)
                A.activation(sq[:, i % 2, :], qkT[:, i, :], ACT.Square).then_inc(sem("qk_sq"), 1)
                if i == 1:
                    gates(4)
            split_to(unit_at[("gate", 4)]["n"] + 4)
            act.wait_ge(sem("qk_stat"), 8)
            A.activation(rs[:, :], banks[4][0:16, 0:TOK], ACT.Sqrt, bias=eps_col[0:16, :],
                         scale=1.0 / 64).then_inc(sem("qk_rms"), 1)
            for i in range(4):
                act.wait_ge(sem("y_pre"), 4 + i + 1)
                A.activation(yg[:, i, :], yg[:, i, :], ACT.Gelu_apprx_tanh).then_inc(sem("yg"), 1)
            for i in range(4):
                act.wait_ge(sem("yg"), i + 1)
                A.activation(yg_hi[:, i, :], yg[:, i, T0:TOK], ACT.Copy).then_inc(sem("yg_hi"), 1)
            gates(5)
            split_to(unit_at[("gate", 5)]["n"] + 4)

            def exp_a(h):
                act.wait_ge(sem("max_a"), h + 1)
                for j in range(2):
                    A.activation(p_a[:, j, :], p_a[:, j, :], ACT.Exp, bias=sm("nmx_a", 2)[:, j:j + 1],
                                 accum_out=sm("l_a", 2)[:, j:j + 1]).then_inc(sem("exp_a"), 1)

            def exp_b(h):
                act.wait_ge(sem("max_b"), h + 1)
                for t, nk in ((0, KEYS_B), (1, META)):
                    for j in range(2):
                        c = 2 * t + j
                        A.activation(p_b[:, t, j, 0:nk], p_b[:, t, j, 0:nk], ACT.Exp,
                                     bias=sm("nmx_b", 4)[:, c:c + 1],
                                     accum_out=sm("l_b", 4)[:, c:c + 1]).then_inc(sem("exp_b"), 1)

            def copy_a(h):
                act.wait_ge(sem("turn_a"), h + 1)
                need(act, "att_o", h)
                A.activation(wT0[:, KEYS_B:TOK], banks[7][0:META, 256:384], ACT.Copy).then_inc(sem("copied_a"), 1)
                A.activation(wT12[:, P:384], banks[7][:, 0:256], ACT.Copy).then_inc(sem("copied_a"), 1)

            def copy_b(h):
                act.wait_ge(sem("turn_b"), h + 1)
                A.activation(wT0[:, 0:KEYS_B], banks[6][0:META, P:P + KEYS_B], ACT.Copy).then_inc(sem("copied_b"), 1)
                A.activation(wT12[:, 0:P], banks[6][:, 0:P], ACT.Copy).then_inc(sem("copied_b"), 1)

            def copy_o(h):
                act.wait_ge(sem("att_o"), h + 1)
                A.activation(oT[:, h, :], banks[3][:, 0:TOK], ACT.Copy).then_inc(sem("o_copied"), 1)

            def glu(ms):
                evac("glu", 0, lambda m, b: A.activation(glu_t[:, m, :], b[:, 0:NQ], ACT.Tanh, scale=0.5,
                                                         bias=sm("glu_bh", 4)[:, m:m + 1]), ms)

            exp_a(0)
            exp_b(0)
            for h in range(4):
                if h:
                    copy_o(h - 1)
                copy_a(h)
                if h < 3:
                    exp_a(h + 1)
                if h == 1:
                    for i in range(4):
                        act.wait_ge(sem("yssm"), i + 1)
                        A.activation(yg_hi[:, i, :], glu_t[:, i, :], ACT.Copy, scale=0.5).then_inc(sem("yssm_hi"), 1)
                if h == 0:
                    glu((0, 1))
                elif h < 3:
                    gates(5 + h, (0,))
                copy_b(h)
                if h < 3:
                    exp_b(h + 1)
                if h == 0:
                    glu((2, 3))
                    split_to(unit_at[("glu", 0)]["n"] + 4)
                elif h < 3:
                    gates(5 + h, (1,))
                    split_to(unit_at[("gate", 5 + h)]["n"] + 4)
            copy_o(3)
            act.wait_ge(sem("yssm_hi"), 4)
            act.wait_ge(sem("o_copied"), 4)
            for h in range(4):
                need(act, "o_stat", h - 1)
                A.activation(sq[:, h % 2, :], oT[:, h, :], ACT.Square).then_inc(sem("o_sq"), 1)
            act.wait_ge(sem("o_stat"), 4)
            A.activation(rs2[:, :], banks[4][0:4, 0:TOK], ACT.Sqrt, bias=eps_col[0:4, :],
                         scale=1.0 / P).then_inc(sem("o_rms"), 1)
            for h in range(4):
                act.wait_ge(sem("yatt"), h + 1)
                A.activation(yatt_hi[:, h, :], oT[:, h, T0:TOK], ACT.Copy).then_inc(sem("yatt_hi"), 1)
            split_to(unit_at[("att_out", 0)]["n"] + 2)
            for m in range(8):
                if m == 4:
                    split_to(unit_at[("att_out", 1)]["n"] + 2)
                act.wait_ge(sem("mixed"), m + 1)
                A.activation(mix_hi[:, m, :], gate[:, m, :], ACT.Copy, scale=0.5).then_inc(sem("mix_hi"), 1)
            for m in range(8):
                if m % 2 == 0:
                    split_to(unit_at[("w_o", m // 2)]["n"] + 3)
                taken(act, group(("w_o", m // 2), m % 2))
                need(act, "h1_sum", min(m - 1, max(m - 2, 1)))
                A.activation(sq[:, m % 2, 0:NQ], hT[:, m, :], ACT.Square).then_inc(sem("h1_sq"), 1)
            act.wait_ge(sem("h1_stat"), 1)
            A.activation(rstd[:, :], banks[3][:, 0:NQ], ACT.Sqrt, bias=eps_col, scale=1.0 / D).then_inc(sem("h1_rms"), 1)
            for m in range(8):
                act.wait_ge(sem("hs"), m + 1)
                A.activation(hs_hi[:, m, :], hs[:, m % NH, :], ACT.Copy).then_inc(sem("hs_hi"), 1)
            split_to(unit_at[("up_a", 0)]["n"] + 2)
            for i in range(KF // 2):
                split_to(unit_at[("up_a", i)]["n"] + 3)
                for m in range(2):
                    taken(act, group(("up_a", i), m))
                    A.activation(gl[:, i % 2, m, :], cv_[:, i % 2, m, :], ACT.Gelu_apprx_tanh).then_inc(sem("gl"), 1)
                split_to(unit_at[("up_b", i)]["n"] + 3)
                for m in range(2):
                    taken(act, group(("up_b", i), m))
                    if i >= 2:
                        need(act, "acc_unit_done", i - 1)
                    A.activation(ff_hi[:, i % 2, m, :], ff[:, i % 2, m, :], ACT.Copy).then_inc(sem("ff_hi"), 1)
            split_to(unit_at[("down", KF // 2 - 1)]["n"] + 1)

            def norm_in(ready, stat, rms, hi, src, dst_hi, first=0):
                A.activation(small[:, 1, 8:9], eps_col, ACT.Sqrt)
                split_to(first)
                for m in range(8):
                    ready(m)
                    need(act, stat + "_sum", min(m - 1, max(m - 2, 1)))
                    A.activation(sq2[:, m % 2, :], src[:, m, :], ACT.Square).then_inc(sem(stat + "_sq"), 1)
                act.wait_ge(sem(stat), 1)
                A.activation(rst2[:, :], banks[3][:, 0:256], ACT.Sqrt, bias=eps_col, scale=1.0 / D).then_inc(
                    sem(rms), 1)
                for m in range(8):
                    act.wait_ge(sem(hi + "_f"), m + 1)
                    A.activation(dst_hi[:, m, :], tmp2[:, m % NH, :], ACT.Copy).then_inc(sem(hi), 1)

            norm_in(lambda m: act.wait_ge(sem("x2_ready"), m + 1), "x2_stat", "x2_rms", "x2n_hi", x2, x2n_hi,
                    unit_at[("lru_x", 0)]["n"] + 2)
            act.wait_ge(sem("tiny_v"), 1)
            A.activation(sm("sp_e", 2), sm("sp_ab", 2), ACT.Exp, scale=-1.0).then_inc(sem("tiny_a"), 1)
            A.activation(sm("lb_e", 2), sm("lb_z", 2), ACT.Exp).then_inc(sem("tiny_a"), 1)
            act.wait_ge(sem("tiny_a"), 2)
            A.activation(sm("sp_l", 2), sm("sp_e", 2), ACT.Ln, bias=ones[:, 0:1]).then_inc(sem("tiny_a"), 1)
            split_to(unit_at[("hg_f", 0)]["n"] + 3)
            u = unit_at[("hg_f", 0)]
            for m in range(2):
                g = u["g0"] + m
                act.wait_ge(sem("group_done"), g + 1)
                A.activation(hgf[:, m, :], banks[g % NB][:, 0:256], ACT.Sigmoid).then_inc(sem("hg_sig"), 1)
                A.activation(hgk[:, m, :], banks[g % NB][:, 0:256], ACT.Sigmoid, scale=-1.0).then_inc(
                    sem(f"group_free{g % NB}"), 1)
            split_to(unit_at[("hg_q", 0)]["n"] + 3)
            for m in range(2):
                act.wait_ge(sem("lru_gate"), 2)
                A.activation(lru_r[:, m, :], banks[6][:, 256 * m:256 * m + 256], ACT.Sigmoid,
                             bias=col("lru_ba", m)).then_inc(sem("lru_ri"), 1)
                A.activation(lru_i[:, m, :], banks[7][:, 256 * m:256 * m + 256], ACT.Sigmoid,
                             bias=col("lru_bx", m)).then_inc(sem("lru_ri"), 1)
            evac("hg_q", 0, lambda m, b: A.activation(hgq[:, m, :], b[:, 0:256], ACT.Silu))
            act.wait_ge(sem("lru_ri"), 4)
            act.wait_ge(sem("tiny_v"), 2)
            for m in range(2):
                A.activation(lru_a[:, m, :], lru_r[:, m, :], ACT.Exp, scale=sm("n8sp", 2)[:, m:m + 1]).then_inc(
                    sem("lru_at"), 1)
                A.activation(lru_t[:, m, :], lru_r[:, m, :], ACT.Tanh, scale=sm("n8sp", 2)[:, m:m + 1]).then_inc(
                    sem("lru_at"), 1)
            split_to(unit_at[("hg_i", 0)]["n"] + 3)
            evac("hg_i", 0, lambda m, b: A.activation(hgv[:, m, :], b[:, 0:256], ACT.Copy))
            act.wait_ge(sem("lru_e"), 2)
            for m in range(2):
                A.activation(lru_t[:, m, :], lru_t[:, m, :], ACT.Sqrt).then_inc(sem("lru_s"), 1)
            for i in range(2):
                split_to(unit_at[("cq", i)]["n"] + 3)
                evac("cq", i, lambda m, b: A.activation(cq[:, 2 * i + m, :], b[:, 0:256], ACT.Copy, scale=0.125))
            for i in range(2):
                split_to(unit_at[("ck", i)]["n"] + 3)
                evac("ck", i, lambda m, b: A.activation(ck[:, 2 * i + m, :], b[:, 0:256], ACT.Copy))
            for i in range(2):
                split_to(unit_at[("cv", i)]["n"] + 3)
                evac("cv", i, lambda m, b: A.activation(cv[:, m, 256 * i:256 * i + 256], b[:, 0:256], ACT.Copy))
            act.wait_ge(sem("hg_o"), 1)
            A.activation(hgo[:, :, :], banks[3][:, :].rearrange("p (a t) -> p a t", a=2), ACT.Copy).then_inc(
                sem("hgo"), 1)
            act.wait_ge(sem("hgo"), 1)
            for m in range(2):
                A.activation(sq2[:, m, :], hgo[:, m, :], ACT.Square).then_inc(sem("hgo"), 1)
            split_to(unit_at[("hg_g", 0)]["n"] + 3)
            evac("hg_g", 0, lambda m, b: A.activation(hgg[:, m, :], b[:, 0:256], ACT.Silu))
            act.wait_ge(sem("hg_stat"), 2)
            A.activation(rsm2[:, :], banks[3][0:4, 0:256], ACT.Sqrt, bias=eps_col[0:4, :], scale=1.0 / 64).then_inc(
                sem("hg_rms"), 1)
            split_to(unit_at[("lru_y", 0)]["n"] + 3)
            evac("lru_y", 0, lambda m, b: A.activation(lru_g[:, m, :], b[:, 0:256], ACT.Gelu_apprx_tanh))

            def m_exp(h):
                act.wait_ge(sem("m_max"), h + 1)
                for t, c in ((0, slice(0, P)), (1, slice(P, 384))):
                    A.activation(mp[:, h % 2, c], mp[:, h % 2, c], ACT.Exp, bias=sm(f"mn{h % 2}", 2)[:, t:t + 1],
                                 accum_out=sm(f"ml{h % 2}", 2)[:, t:t + 1]).then_inc(sem("m_exp"), 1)

            def m_copy(h):
                act.wait_ge(sem("m_T"), h + 1)
                need(act, "m_val", h - 1)
                A.activation(mpT[:, h % 2, :], banks[6 + h % 2][:, 0:384], ACT.Copy).then_inc(sem("m_copied"), 1)

            def m_out(p_):
                act.wait_ge(sem("m_val"), 2 * p_ + 2)
                A.activation(mo[:, p_, :], banks[3][:, 0:256], ACT.Copy).then_inc(sem("m_out"), 1)

            def yc_square(p_):
                act.wait_ge(sem("m_out"), p_ + 1)
                need(act, "yc_stat", p_ - 1)
                A.activation(sq2[:, p_ % 2, :], mo[:, p_, :], ACT.Square).then_inc(sem("yc_sq"), 1)

            m_exp(0)
            for h in range(8):
                if h < 7:
                    m_exp(h + 1)
                m_copy(h)
                if h in (2, 4, 6):
                    m_out(h // 2 - 1)
                if h == 3:
                    for m in range(2):
                        act.wait_ge(sem("yb"), m + 1)
                        A.activation(ycat_hi[:, 2 + m, :], hgo[:, m, :], ACT.Copy).then_inc(sem("ycat_hi"), 1)
                if h == 5:
                    for m in range(2):
                        act.wait_ge(sem("lru_h"), m + 1)
                        A.activation(sq2[:, m, :], xc[:, m, :], ACT.Square).then_inc(sem("ya_sq"), 1)
            act.wait_ge(sem("ya_stat"), 2)
            A.activation(rst2[:, :], banks[4][:, 0:256], ACT.Sqrt, bias=eps_col, scale=1.0 / 256).then_inc(
                sem("ya_rms"), 1)
            for p_ in range(3):
                yc_square(p_)
            m_out(3)
            yc_square(3)
            for m in range(2):
                act.wait_ge(sem("ya"), m + 1)
                A.activation(ycat_hi[:, m, :], xc[:, m, :], ACT.Copy).then_inc(sem("ycat_hi"), 1)
            act.wait_ge(sem("yc_stat"), 4)
            A.activation(rst3[:, :], banks[5][:, 0:256], ACT.Sqrt, bias=eps_col, scale=1.0 / 512).then_inc(
                sem("yc_rms"), 1)
            split_to(unit_at[("w_out2", 0)]["n"] + 2)
            for p_ in range(4):
                act.wait_ge(sem("yc"), p_ + 1)
                A.activation(ycat_hi[:, 4 + p_, :], mo[:, p_, :], ACT.Copy).then_inc(sem("ycat_hi"), 1)

            def x3_ready(m):
                if m % 2 == 0:
                    split_to(unit_at[("w_out2", m // 2)]["n"] + 3 - m // 6)
                taken(act, group(("w_out2", m // 2), m % 2))

            norm_in(x3_ready, "x3_stat", "x3_rms", "x3_hi", x2, x2n_hi)
            for i in range(KF2 // 2):
                split_to(unit_at[("ff1", i)]["n"] + 3)
                for m in range(2):
                    g = group(("ff1", i), m)
                    act.wait_ge(sem("group_done"), g + 1)
                    A.activation(relu[:, i % 2, m, :], banks[g % NB][:, 0:256], ACT.Relu).then_inc(
                        sem(f"group_free{g % NB}"), 1)
                for m in range(2):
                    act.wait_ge(sem("uu"), 2 * i + m + 1)
                    if i >= 2:
                        used(act, unit_at[("ff2", i - 2)]["n"])
                    A.activation(u_hi[:, i % 2, m, :], uu[:, i % 2, m, :], ACT.Copy).then_inc(sem("u_hi"), 1)
            split_to(len(units))
            for t in range(2):
                act.wait_ge(sem("ff2_done"), t + 1)
                A.activation(sqj[:, :, :], psum[:, 4 + 2 * t:6 + 2 * t, :], ACT.Square,
                             accum_out=sm("fs", 2)[:, t:t + 1]).then_inc(sem("f_sq"), 1)
                act.wait_ge(sem("f_sq"), t + 1)
                A.activation(sm("fr", 2)[:, t:t + 1], sm("fs", 2)[:, t:t + 1], ACT.Sqrt, bias=eps_col,
                             scale=1.0 / D).then_inc(sem("f_rms"), 1)

        @block.vector
        def _(dve):
            V = nc.vector
            n = [0]

            def mark(i):
                n[0] += 1
                i.then_inc(sem("dve_seq"), 1)
                return n[0]

            def seq(i):
                dve.wait_ge(sem("dve_seq"), mark(i))

            dve.wait_ge(sem("constants"), CONSTANTS["small"])
            dve.wait_ge(sem("x_in1"), 16)
            V.tensor_tensor_reduce(xr[:, 2, :], xtok[:, 2, :], xtok[:, 2, :], 1.0, 0.0, ALU.mult, ALU.add,
                                   small[:, 0, 2:3]).then_inc(sem("x_sq2"), 1)
            dve.wait_ge(sem("x_rms"), 1)
            seq(V.reciprocal(small[:, 1, 4:7], small[:, 1, 0:3]))
            for t, rows in ((0, META), (1, P), (2, P)):
                V.tensor_scalar(xr[0:rows, t, :], xtok[0:rows, t, :], small[0:rows, 1, 4 + t:5 + t], None,
                                ALU.mult).then_inc(sem("xr"), 1)

            def param_cols(i):
                dst, n_ = PTILES[i]
                dve.wait_ge(sem("par_T"), (1, 2, 4, 4)[i])
                V.tensor_copy((C1[:, dst:dst + n_] if i < 3 else C2[:, 0:n_]), banks[3][:, P * i:P * i + n_]).then_inc(
                    sem("C_ready"), 1)
                dve.wait_ge(sem("C_ready"), i + 1)

            param_cols(0)

            done = [0]
            by_pool = set(POOL_LO) | {u["n"] for u in pool_units}

            def split_to(n):
                while done[0] < min(n, len(units)):
                    u = done[0]
                    done[0] += 1
                    if u in by_pool:
                        continue
                    dve.wait_ge(sem("hi_ready"), u + 1)
                    if u - 1 in by_pool:
                        dve.wait_ge(sem("lo_ready"), u)
                    V.tensor_tensor(w_lo[:, u % NW, :], raw[:, u % NRAW, :], w_hi[:, u % NW, :].bitcast(F32),
                                    ALU.subtract).then_inc(sem("lo_ready"), 1)

            split_to(1)
            for kt in range(KD):
                dve.wait_ge(sem("xn_hi"), kt + 1)
                V.scalar_tensor_tensor(out=xn_lo[:, kt, :], in0=banks[4 + kt % 4][:, 0:TOK], scalar=col("norm1", kt),
                                       in1=xn_hi[:, kt, :].bitcast(F32), op0=ALU.mult,
                                       op1=ALU.subtract).then_inc(sem("xn_lo"), 1)
            split_to(2)
            param_cols(1)
            are, aim = col("a_re", 0, 16), col("a_im", 0, 16)
            tt = lambda o, a, b, op: V.tensor_tensor(o, a, b, op)
            dve.wait_ge(sem("s5p_a"), 2)
            tt(sm("zr"), are, sm("dt"), ALU.mult).then_inc(sem("s5p_v"), 1)
            seq(tt(sm("th"), aim, sm("dt"), ALU.mult))
            seq(V.tensor_scalar(sm("kk"), sm("th"), INV_TWO_PI, ROUND, ALU.mult, ALU.add))
            seq(V.tensor_scalar(sm("kk"), sm("kk"), -ROUND, None, ALU.add))
            for c in (TWO_PI_1, TWO_PI_2, TWO_PI_3):
                seq(V.scalar_tensor_tensor(out=sm("th"), in0=sm("kk"), scalar=-c, in1=sm("th"), op0=ALU.mult,
                                           op1=ALU.add))
            V.tensor_scalar(sm("thr"), sm("th"), 3.1415925, -3.1415925, ALU.min, ALU.max).then_inc(sem("s5p_v"), 1)
            dve.wait_ge(sem("s5p_a"), 6)
            seq(V.scalar_tensor_tensor(out=sm("mm1"), in0=sm("mag"), scalar=1.0, in1=sm("tnh"), op0=ALU.add,
                                       op1=ALU.mult))
            seq(tt(sm("omc"), sm("sinh_"), sm("sinh_"), ALU.mult))
            seq(V.tensor_scalar(sm("omc"), sm("omc"), 2.0, None, ALU.mult))
            seq(tt(sm("lbi"), sm("mag"), sm("sin"), ALU.mult))
            seq(tt(sm("q1"), sm("mag"), sm("omc"), ALU.mult))
            seq(tt(sm("nre"), sm("mm1"), sm("q1"), ALU.subtract))
            seq(tt(sm("q1"), are, are, ALU.mult))
            seq(tt(sm("q2"), aim, aim, ALU.mult))
            seq(tt(sm("q1"), sm("q1"), sm("q2"), ALU.add))
            seq(V.reciprocal(sm("rden"), sm("q1")))
            seq(tt(sm("q1"), sm("nre"), are, ALU.mult))
            seq(tt(sm("q2"), sm("lbi"), aim, ALU.mult))
            seq(tt(sm("q1"), sm("q1"), sm("q2"), ALU.add))
            seq(tt(sm("fre"), sm("q1"), sm("rden"), ALU.mult))
            seq(tt(sm("q1"), sm("lbi"), are, ALU.mult))
            seq(tt(sm("q2"), sm("nre"), aim, ALU.mult))
            seq(tt(sm("q1"), sm("q1"), sm("q2"), ALU.subtract))
            dve.wait_ge(sem("constants"), CONSTANTS["half"])
            half = small[:, 84, 0:8].rearrange("p (g a) -> p g a", g=2)
            seq(V.tensor_reduce(sm("halfc", 2), half, AXX, ALU.add))
            tt(sm("fim"), sm("q1"), sm("rden"), ALU.mult).then_inc(sem("f_ready"), 1)
            dve.wait_ge(sem("lam_in"), 64)
            for i in range(2):
                V.tensor_tensor_reduce(lamv[:, i * 2], lamv[:, i * 2], lamv[:, i * 2 + 1], 1.0, 0.0, ALU.mult, ALU.add,
                                       sm("lam_s", 2)[:, i:i + 1]).then_inc(sem("lam_v"), 1)
            split_to(3)
            dve.wait_ge(sem("xrT"), 8)
            mark(V.memset(Ec[:, :, 0:1], 1.0))
            mark(V.memset(Es[:, :, 0:1], 0.0))
            mark(V.tensor_scalar(Ec[:, :, 1], sm("omc"), -1.0, 1.0, ALU.mult, ALU.add))
            seq(V.tensor_copy(Es[:, :, 1], sm("sin")))
            have = 1
            while have < LC - 1:
                m = min(have, LC - 1 - have)
                pc, ps = (e_[:, :, have:have + 1].to_broadcast([P, NS, m]) for e_ in (Ec, Es))
                lo, hi = slice(1, m + 1), slice(have + 1, have + m + 1)
                t1, t2 = e_tmp[:, 0, :, 0:m], e_tmp[:, 1, :, 0:m]
                mark(tt(t1, Es[:, :, lo], ps, ALU.mult))
                mark(tt(Ec[:, :, hi], Ec[:, :, lo], pc, ALU.mult))
                mark(tt(t2, Ec[:, :, lo], ps, ALU.mult))
                seq(tt(Es[:, :, hi], Es[:, :, lo], pc, ALU.mult))
                mark(tt(Ec[:, :, hi], Ec[:, :, hi], t1, ALU.subtract))
                seq(tt(Es[:, :, hi], Es[:, :, hi], t2, ALU.add))
                have += m
            param_cols(2)
            param_cols(3)
            dve.wait_ge(sem("lam_a"), 1)
            seq(V.tensor_scalar(sm("lam_e", 2)[:, 1:2], sm("lam_e", 2)[:, 1:2], -1.0, 0.8 - 0.6, ALU.mult, ALU.add))
            seq(tt(sm("nlam", 1), sm("lam_e", 2)[:, 0:1], sm("lam_e", 2)[:, 1:2], ALU.add))
            seq(V.tensor_scalar(sm("nlam", 1), sm("nlam", 1), -1.0, None, ALU.mult))
            seq(V.tensor_scalar(sm("qg", 1), col("qn"), 0.125, None, ALU.mult))
            seq(V.tensor_scalar(sm("subg", 1), col("subln"), 1.0 - (0.8 - 0.6), None, ALU.mult))
            seq(V.tensor_scalar(sm("glu_bh", 4), col("glu_b", 0, 4), 0.5, None, ALU.mult))
            seq(tt(sm("q1"), Ec[:, :, LC - 1], Ec[:, :, 1], ALU.mult))
            seq(tt(sm("q2"), Es[:, :, LC - 1], Es[:, :, 1], ALU.mult))
            seq(tt(sm("kc"), sm("q1"), sm("q2"), ALU.subtract))
            seq(tt(sm("q1"), Ec[:, :, LC - 1], Es[:, :, 1], ALU.mult))
            seq(tt(sm("q2"), Es[:, :, LC - 1], Ec[:, :, 1], ALU.mult))
            seq(tt(sm("ks"), sm("q1"), sm("q2"), ALU.add))

            def s5_mults(b):
                jp = b % 8
                c, s = Ec[:, 2 * jp:2 * jp + 2, :], Es[:, 2 * jp:2 * jp + 2, :]
                pair = psum[:, 4 + 2 * (b % 2):6 + 2 * (b % 2), :]
                xre, xim = pair[:, :, 0:LC], pair[:, :, LC:2 * LC]
                m = mprod[:, b % NM].rearrange("p n (a t) -> p n a t", a=2)
                dve.wait_ge(sem("s5_x"), b + 1)
                need(dve, "s5_out", b // 2 - 1)
                mark(tt(m[:, 0], xre, c, ALU.mult))
                mark(tt(m[:, 1], xim, s, ALU.mult))
                mark(tt(m[:, 2], xim, c, ALU.mult))
                tt(m[:, 3], xre, s, ALU.mult).then_inc(sem("s5_m"), 1)

            def s5_scan(b):
                jp, m = b % 8, mprod[:, b % NM]
                dve.wait_ge(sem("s5_w"), 2 * (b + 1))
                last = 0
                for p_ in range(2):
                    for i in range(2):
                        j = 2 * jp + i
                        init = 0.0 if b < 8 else sm("zi" if p_ else "zr0")[:, j:j + 1]
                        last = mark(V.tensor_tensor_scan(zbuf[:, p_, LC * i:LC * i + LC],
                                                         sm("mag")[:, j:j + 1].to_broadcast([P, LC]),
                                                         m[:, 2 * p_, LC * i:LC * i + LC], init, ALU.mult, ALU.add))
                dve.wait_ge(sem("dve_seq"), last)
                c = Ec[:, 2 * jp:2 * jp + 2, :].rearrange("p a t -> p (a t)")
                s = Es[:, 2 * jp:2 * jp + 2, :].rearrange("p a t -> p (a t)")
                if b < 8:
                    for p_, nm in ((0, "zer"), (1, "zei")):
                        src = zbuf[:, p_].rearrange("p (a t) -> p a t", a=2)[:, :, LC - 1]
                        mark(V.tensor_copy(sm(nm)[:, 2 * jp:2 * jp + 2], src))
                mark(tt(m[:, 0], zbuf[:, 0], c, ALU.mult))
                mark(V.scalar_tensor_tensor(out=m[:, 1], in0=zbuf[:, 1], scalar=-1.0, in1=s, op0=ALU.mult,
                                            op1=ALU.mult))
                mark(tt(m[:, 2], zbuf[:, 0], s, ALU.mult))
                tt(m[:, 3], zbuf[:, 1], c, ALU.mult).then_inc(sem("s5_n"), 1)
                dve.wait_ge(sem("s5_n"), b + 1)

            def carry():
                a, b, c, s = sm("zer"), sm("zei"), sm("kc"), sm("ks")
                mark(tt(sm("q1"), a, c, ALU.mult))
                mark(tt(sm("q2"), b, s, ALU.mult))
                mark(tt(sm("q3"), a, s, ALU.mult))
                seq(tt(sm("q4"), b, c, ALU.mult))
                mark(tt(sm("zr0"), sm("q1"), sm("q2"), ALU.subtract))
                seq(tt(sm("zi"), sm("q3"), sm("q4"), ALU.add))

            def s5_y(kk):
                c, jj = divmod(kk, 4)
                dve.wait_ge(sem("s5_out"), kk + 1)
                V.scalar_tensor_tensor(out=yg[:, jj, LC * c:LC * c + LC], in0=uT[:, jj, LC * c:LC * c + LC],
                                       scalar=col("ssm_d", jj), in1=banks[3][:, 0:LC], op0=ALU.mult,
                                       op1=ALU.add).then_inc(sem("y_pre"), 1)

            dve.wait_ge(sem("xT"), 8)
            s5_mults(0)
            for b in range(1, 16):
                s5_mults(b)
                if b % 2 == 0 and b > 2:
                    s5_y(b // 2 - 2)
                s5_scan(b - 1)
                if b == 8:
                    carry()
            s5_y(6)
            s5_scan(15)
            split_to(12)
            s5_y(7)
            split_to(13)
            dve.wait_ge(sem("qk_rms"), 1)
            V.reciprocal(rs[:, :], rs[:, :]).then_inc(sem("qk_r"), 1)
            for i in range(8):
                dve.wait_ge(sem("qk_bc"), i + 1)
                V.scalar_tensor_tensor(out=qkT[:, i, :], in0=qkT[:, i, :], scalar=col("kn") if i < 4 else sm("qg", 1),
                                       in1=banks[5 + i % 3][:, 0:TOK], op0=ALU.mult, op1=ALU.mult).then_inc(
                                           sem("qkn"), 1)


            for i in range(4):
                dve.wait_ge(sem("yg_hi"), i + 1)
                tt(yg_lo[:, i, :], yg[:, i, T0:TOK], yg_hi[:, i, :].bitcast(F32), ALU.subtract).then_inc(
                    sem("yg_lo"), 1)

            def att_max(part, h, pieces):
                dve.wait_ge(sem(f"scores_{part}"), h + 1)
                n_ = len(pieces)
                need(dve, f"w_{part}", n_ // 2 * h)
                for c, (dst, src, b0, nk) in enumerate(pieces):
                    mark(V.tensor_tensor_reduce(dst, src, bias[:, 2 * h + 1, b0:b0 + nk], 1.0, -3e38, ALU.add,
                                                ALU.max, sm(f"mx_{part}", n_)[:, c:c + 1]))
                dve.wait_ge(sem("dve_seq"), n[0])
                V.tensor_scalar(sm(f"nmx_{part}", n_), sm(f"mx_{part}", n_), -1.0, None, ALU.mult).then_inc(
                    sem(f"max_{part}"), 1)

            def max_a(h):
                if h == 0:
                    dve.wait_ge(sem("constants"), CONSTANTS["bias"])
                att_max("a", h, [(p_a[:, j, :], banks[4 + j][:, 0:TOK], 0, TOK) for j in range(2)])

            def max_b(h):
                att_max("b", h, [(p_b[:, 0, j, :], banks[6 + j][:, 0:KEYS_B], P, KEYS_B) for j in range(2)]
                        + [(p_b[:, 1, j, 0:META], banks[6 + j][:, KEYS_B:KEYS_B + META], KEYS_B, META)
                           for j in range(2)])

            def att_mix(part, h, pieces):
                n_ = 2 * len(pieces)
                dve.wait_ge(sem(f"exp_{part}"), n_ * (h + 1))
                need(dve, f"turn_{part}", h)
                rl = sm(f"rl_{part}", n_)
                seq(V.reciprocal(rl, sm(f"l_{part}", n_)))
                pair = rl.rearrange("p (t j) -> p t j", j=2)
                mark(V.tensor_scalar(pair[:, :, 1], pair[:, :, 1], sm("nlam", 1), None, ALU.mult))
                for c, (w, p0, _) in enumerate(pieces):
                    mark(V.tensor_scalar(w, p0, rl[:, 2 * c:2 * c + 1], None, ALU.mult))
                dve.wait_ge(sem("dve_seq"), n[0])
                for c, (w, _, p1) in enumerate(pieces):
                    i = V.scalar_tensor_tensor(out=w, in0=p1, scalar=rl[:, 2 * c + 1:2 * c + 2], in1=w,
                                               op0=ALU.mult, op1=ALU.add)
                    i.then_inc(sem(f"w_{part}"), 1)

            def mix_a(h):
                att_mix("a", h, [(w_a[:, :], p_a[:, 0, :], p_a[:, 1, :])])

            def mix_b(h):
                att_mix("b", h, [(w_b[:, t, 0:nk], p_b[:, t, 0, 0:nk], p_b[:, t, 1, 0:nk])
                                 for t, nk in ((0, KEYS_B), (1, META))])

            max_a(0)
            max_b(0)
            for h in range(4):
                mix_a(h)
                if h == 1:
                    for i in range(4):
                        taken(dve, unit_at[("glu", 0)]["g0"] + i)
                        V.scalar_tensor_tensor(out=glu_t[:, i, :], in0=glu_t[:, i, :], scalar=1.0,
                                               in1=yg[:, i, T0:TOK], op0=ALU.add, op1=ALU.mult).then_inc(
                                                   sem("yssm"), 1)
                if h < 3:
                    max_a(h + 1)
                mix_b(h)
                if h < 3:
                    max_b(h + 1)
                if h == 1:
                    for i in range(4):
                        dve.wait_ge(sem("yssm_hi"), i + 1)
                        V.scalar_tensor_tensor(out=yg_lo[:, i, :], in0=glu_t[:, i, :], scalar=0.5,
                                               in1=yg_hi[:, i, :].bitcast(F32), op0=ALU.mult,
                                               op1=ALU.subtract).then_inc(sem("yssm_lo"), 1)

            def evac(name, i, fn):
                u = unit_at[(name, i)]
                for m in range(u["groups"]):
                    g = u["g0"] + m
                    dve.wait_ge(sem("group_done"), g + 1)
                    fn(m, banks[g % NB]).then_inc(sem(f"group_free{g % NB}"), 1)

            for i in range(2):
                evac("ssm_out", i, lambda m, b: V.scalar_tensor_tensor(
                    out=gate[:, 4 * i + m, :], in0=gate[:, 4 * i + m, :], scalar=1.0, in1=b[:, 0:NQ],
                    op0=ALU.add, op1=ALU.mult))

            def yatt_low(h):
                dve.wait_ge(sem("yatt_hi"), h + 1)
                tt(yatt_lo[:, h, :], oT[:, h, T0:TOK], yatt_hi[:, h, :].bitcast(F32), ALU.subtract).then_inc(
                    sem("yatt_lo"), 1)

            dve.wait_ge(sem("o_rms"), 1)
            V.reciprocal(rs2[:, :], rs2[:, :]).then_inc(sem("o_r"), 1)
            for h in range(4):
                dve.wait_ge(sem("o_bc"), h + 1)
                V.scalar_tensor_tensor(out=oT[:, h, T0:TOK], in0=oT[:, h, T0:TOK], scalar=sm("subg", 1),
                                       in1=banks[4 + h][:, T0:TOK], op0=ALU.mult, op1=ALU.mult).then_inc(
                                           sem("yatt"), 1)
                if h:
                    yatt_low(h - 1)
            yatt_low(3)
            def mix_low(j):
                dve.wait_ge(sem("mix_hi"), j + 1)
                V.scalar_tensor_tensor(out=mix_lo[:, j, :], in0=gate[:, j, :], scalar=0.5,
                                       in1=mix_hi[:, j, :].bitcast(F32), op0=ALU.mult,
                                       op1=ALU.subtract).then_inc(sem("mix_lo"), 1)

            for j in range(8):
                if j % 4 == 0:
                    split_to(unit_at[("att_out", j // 4)]["n"] + 2)
                g = group(("att_out", j // 4), j % 4)
                dve.wait_ge(sem("group_done"), g + 1)
                V.scalar_tensor_tensor(out=gate[:, 8 + j, :], in0=gate[:, 8 + j, :], scalar=1.0,
                                       in1=banks[g % NB][:, 0:NQ], op0=ALU.add, op1=ALU.mult).then_inc(
                                           sem(f"group_free{g % NB}"), 1)
                taken(dve, g)
                tt(gate[:, j, :], gate[:, j, :], gate[:, 8 + j, :], ALU.add).then_inc(sem("mixed"), 1)
                if j:
                    mix_low(j - 1)
            mix_low(7)

            def add_square(sums, name, acc, squares, m):
                if m > 0:
                    dve.wait_ge(sem(name), m + 1)
                    need(dve, sums, m - 1)
                    tt(acc, squares(0) if m == 1 else acc, squares(m), ALU.add).then_inc(sem(sums), 1)

            def h1_square(m):
                add_square("h1_sum", "h1_sq", sqsum[:, :], lambda m: sq[:, m % 2, 0:NQ], m)

            for i in range(4):
                u = unit_at[("w_o", i)]
                split_to(u["n"] + 2)
                for m in range(2):
                    g = u["g0"] + m
                    dve.wait_ge(sem("group_done"), g + 1)
                    dve.wait_ge(sem("hT_copy"), 8)
                    j = 2 * i + m
                    tt(hT[:, j, :], hT[:, j, :], banks[g % NB][:, 0:NQ], ALU.add).then_inc(sem(f"group_free{g % NB}"), 1)
                    h1_square(j - 1)
            h1_square(7)
            split_to(unit_at[("up_a", 0)]["n"] + 2)
            dve.wait_ge(sem("h1_rms"), 1)
            seq(V.reciprocal(rstd[:, :], rstd[:, :]))
            for m in range(8):
                taken(dve, group(("w_o", m // 2), m % 2))
                need(dve, "hs_lo", m - NH + 1)
                V.scalar_tensor_tensor(out=hs[:, m % NH, :], in0=hT[:, m, :], scalar=col("norm2", m),
                                       in1=rstd[:, :], op0=ALU.mult, op1=ALU.mult).then_inc(sem("hs"), 1)
            for i in range(KF // 2):
                ua, ub = unit_at[("up_a", i)], unit_at[("up_b", i)]
                split_to(ua["n"] + 3)
                for m in range(2):
                    j, g = 2 * i + m, ua["g0"] + m
                    dve.wait_ge(sem("group_done"), g + 1)
                    ps = banks[g % NB]
                    c = cv_[:, i % 2, m, :]
                    seq(V.tensor_scalar(c, ps[:, 0:256], col("conv_w", j), col("conv_b", j), ALU.mult, ALU.add))
                    seq(V.scalar_tensor_tensor(out=c, in0=ps[:, 1:257], scalar=col("conv_w", KF + j), in1=c,
                                               op0=ALU.mult, op1=ALU.add))
                    V.scalar_tensor_tensor(out=c, in0=ps[:, 2:258], scalar=col("conv_w", 2 * KF + j), in1=c,
                                           op0=ALU.mult, op1=ALU.add).then_inc(sem(f"group_free{g % NB}"), 1)
                split_to(ub["n"] + 3)
                for m in range(2):
                    j, g = 2 * i + m, ub["g0"] + m
                    dve.wait_ge(sem("group_done"), g + 1)
                    dve.wait_ge(sem("gl"), j + 1)
                    tt(ff[:, i % 2, m, :], gl[:, i % 2, m, :], banks[g % NB][:, 0:256], ALU.mult).then_inc(
                        sem(f"group_free{g % NB}"), 1)
                for m in range(2):
                    taken(dve, group(("up_b", i), m))
                    dve.wait_ge(sem("ff_hi"), 2 * i + m + 1)
                    tt(ff_lo[:, i % 2, m, :], ff[:, i % 2, m, :], ff_hi[:, i % 2, m, :].bitcast(F32),
                       ALU.subtract).then_inc(sem("ff_lo"), 1)
            split_to(unit_at[("lru_x", 0)]["n"] + 2)

            def x_square(x_, m):
                add_square(x_ + "_stat_sum", x_ + "_stat_sq", rst3[:, :], lambda m: sq2[:, m % 2, :], m)

            for m in range(8):
                dve.wait_ge(sem("down_done"), m // 2 + 1)
                tt(x2[:, m, :], hT[:, m, 2:NQ], banks[4 + m // 2][:, 256 * (m % 2):256 * (m % 2) + 256],
                   ALU.add).then_inc(sem("x2_ready"), 1)
                x_square("x2", m - 1)
            x_square("x2", 7)

            STT = V.scalar_tensor_tensor
            lam, lb = col("lru_lam", 0, 2), col("hg_lb", 0, 2)
            seq(STT(out=sm("sp_ab", 2), in0=lam, scalar=-1.0, in1=lam, op0=ALU.mult, op1=ALU.max))
            tt(sm("lb_z", 2), lb, lb, ALU.subtract).then_inc(sem("tiny_v"), 1)

            def norm_in(rms, hi, lo, src, gain):
                dve.wait_ge(sem(rms), 1)
                seq(V.reciprocal(rst2[:, :], rst2[:, :]))
                for m in range(8):
                    need(dve, lo, m - NH + 1)
                    STT(out=tmp2[:, m % NH, :], in0=src[:, m, :], scalar=col(gain, m), in1=rst2[:, :],
                        op0=ALU.mult, op1=ALU.mult).then_inc(sem(hi + "_f"), 1)

            dve.wait_ge(sem("x2_ready"), 8)
            norm_in("x2_rms", "x2n_hi", "x2n_lo", x2, "norm_mix")
            dve.wait_ge(sem("tiny_a"), 3)
            seq(V.tensor_scalar(sm("sp_m", 2), lam, -1.0, 0.0, ALU.mult, ALU.max))
            seq(tt(sm("sp_m", 2), sm("sp_m", 2), sm("sp_l", 2), ALU.add))
            seq(V.reciprocal(sm("lb_s", 2), sm("lb_e", 2)))
            seq(tt(sm("lb_s", 2), sm("lb_s", 2), sm("lb_e", 2), ALU.mult))
            seq(tt(sm("lb_0", 2), sm("lb_s", 2), sm("lb_s", 2), ALU.subtract))
            seq(V.tensor_scalar(sm("lb_m", 2), sm("lb_0", 2), TINY, None, ALU.max))
            seq(V.tensor_scalar(sm("lb_c", 2), sm("lb_0", 2), -1.0, 1.0, ALU.mult, ALU.add))
            V.tensor_scalar(sm("n8sp", 2), sm("sp_m", 2), -8.0, None, ALU.mult).then_inc(sem("tiny_v"), 1)
            u = unit_at[("lru_x", 0)]
            split_to(u["n"] + 3)
            for m in range(2):
                g = u["g0"] + m
                dve.wait_ge(sem("group_done"), g + 1)
                ps = banks[g % NB]
                seq(V.tensor_scalar(xc[:, m, :], ps[:, 0:256], col("lru_w", 6 + m), col("lru_b", m), ALU.mult,
                                    ALU.add))
                for d in range(1, 4):
                    i = STT(out=xc[:, m, d:256], in0=ps[:, 0:256 - d], scalar=col("lru_w", 2 * (3 - d) + m),
                            in1=xc[:, m, d:256], op0=ALU.mult, op1=ALU.add)
                    if d < 3:
                        seq(i)
                i.then_inc(sem(f"group_free{g % NB}"), 1)
            split_to(unit_at[("hg_f", 0)]["n"] + 3)
            dve.wait_ge(sem("hg_sig"), 2)
            for m in range(2):
                taken(dve, group(("hg_f", 0), m))
                seq(V.tensor_scalar(hgf[:, m, :], hgf[:, m, :], sm("lb_c", 2)[:, m:m + 1], sm("lb_m", 2)[:, m:m + 1],
                                    ALU.mult, ALU.add))
                seq(V.tensor_scalar(hgk[:, m, :], hgk[:, m, :], sm("lb_c", 2)[:, m:m + 1], None, ALU.mult))
            split_to(unit_at[("hg_q", 0)]["n"] + 3)
            for m in range(2):
                taken(dve, group(("hg_q", 0), m))
            tt(hqf[:, :, :], hgq[:, :, :], hgf[:, :, :], ALU.mult).then_inc(sem("h_level"), 1)
            split_to(unit_at[("hg_i", 0)]["n"] + 3)
            dve.wait_ge(sem("lru_at"), 4)
            seq(tt(hgo[:, :, :], lru_a[:, :, :], lru_a[:, :, :], ALU.mult))
            seq(STT(out=lru_t[:, :, :], in0=hgo[:, :, :], scalar=1.0, in1=lru_t[:, :, :], op0=ALU.add, op1=ALU.mult))
            V.tensor_scalar(lru_t[:, 0, :], lru_t[:, 0, :], -1.0, SQRT_MIN, ALU.mult, ALU.max).then_inc(sem("lru_e"), 1)
            V.tensor_scalar(lru_t[:, 1, :], lru_t[:, 1, :], -1.0, SQRT_MIN, ALU.mult, ALU.max).then_inc(sem("lru_e"), 1)
            seq(tt(lru_i[:, :, :], lru_i[:, :, :], xc[:, :, :], ALU.mult))

            def level(lv):
                dve.wait_ge(sem("h_scores"), lv + 1)
                if 0 < lv < 8:
                    L = 1 << (lv - 1)
                    nb = 512 // (2 * L)
                    src = (hgf[:, :, :].rearrange("p a t -> p (a t)") if L == 1
                           else htot[:, 512 - 1024 // L:512 - 512 // L])
                    dst = htot[:, 512 - 512 // L:512 - 256 // L]
                    tot = src.rearrange("p (b h) -> p b h", h=2)
                    qv = hqf[:, :, :].rearrange("p a t -> p (a t)").rearrange("p (b h l) -> p b h l", h=2, l=L)
                    kv = hgk[:, :, :].rearrange("p a t -> p (a t)").rearrange("p (b h l) -> p b h l", h=2, l=L)
                    mark(tt(qv[:, :, 1, :], qv[:, :, 1, :], tot[:, :, 0:1].to_broadcast([P, nb, L]), ALU.mult))
                    seq(tt(kv[:, :, 0, :], kv[:, :, 0, :], tot[:, :, 1:2].to_broadcast([P, nb, L]), ALU.mult))
                    tt(dst, tot[:, :, 0], tot[:, :, 1], ALU.mult).then_inc(sem("h_level"), 1)
                    dve.wait_ge(sem("h_level"), lv + 1)
                if lv == 0:
                    dve.wait_ge(sem("constants"), CONSTANTS["masks"])
                b = 4 + 2 * (lv % 2)
                if lv == 8:
                    V.tensor_copy(hX[:, :, :].rearrange("p (a b) t -> p a (b t)", a=2),
                                  psum[:, b:b + 2, 0:256]).then_inc(sem("h_taken"), 1)
                    return
                data = psum[:, b:b + 2, :].rearrange("p a (b t) -> p (a b) t", t=P)
                m = masks[:, lv, :][:, None, :].to_broadcast([P, 8, P]).bitcast(I32)
                if lv:
                    dve.wait_ge(sem("h_taken"), lv)
                V.copy_predicated(hA[:, :, :], m, data).then_inc(sem("h_taken"), 1)

            level(0)
            level(1)
            split_to(unit_at[("cq", 0)]["n"] + 3)
            dve.wait_ge(sem("lru_s"), 2)
            seq(tt(lru_i[:, :, :], lru_i[:, :, :], lru_t[:, :, :], ALU.mult))
            for m in range(2):
                mark(V.tensor_tensor_scan(lru_r[:, m, :], lru_a[:, m, :], lru_i[:, m, :], 0.0, ALU.mult, ALU.add))
            level(2)
            level(3)
            split_to(unit_at[("cq", 1)]["n"] + 3)
            level(4)
            level(5)
            split_to(unit_at[("ck", 0)]["n"] + 3)
            level(6)
            split_to(unit_at[("ck", 1)]["n"] + 3)
            level(7)
            level(8)
            split_to(unit_at[("cv", 1)]["n"] + 3)
            split_to(unit_at[("hg_g", 0)]["n"] + 2)
            dve.wait_ge(sem("hg_rms"), 1)
            V.reciprocal(rsm2[:, :], rsm2[:, :]).then_inc(sem("hg_r"), 1)

            def m_max(h):
                dve.wait_ge(sem("m_s"), h + 1)
                need(dve, "m_T", h - 1)
                last = 0
                for t, c, b0 in ((0, slice(0, P), 144), (1, slice(P, 384), 16)):
                    last = mark(V.tensor_tensor_reduce(mp[:, h % 2, c], banks[4 + h % 2][:, c],
                                                       bias[:, h, b0:b0 + P * (t + 1)], 1.0, -3e38, ALU.add, ALU.max,
                                                       sm(f"m_mx{h % 2}", 2)[:, t:t + 1]))
                dve.wait_ge(sem("dve_seq"), last)
                V.tensor_scalar(sm(f"mn{h % 2}", 2), sm(f"m_mx{h % 2}", 2), -1.0, None, ALU.mult).then_inc(
                    sem("m_max"), 1)

            def m_norm(h):
                dve.wait_ge(sem("m_exp"), 2 * h + 2)
                seq(V.reciprocal(sm(f"mr{h % 2}", 2), sm(f"ml{h % 2}", 2)))
                for t, c in ((0, slice(0, P)), (1, slice(P, 384))):
                    V.tensor_scalar(mp[:, h % 2, c], mp[:, h % 2, c], sm(f"mr{h % 2}", 2)[:, t:t + 1], None,
                                    ALU.mult).then_inc(sem("m_w"), 1)

            m_max(0)
            m_max(1)
            split_to(unit_at[("lru_y", 0)]["n"] + 3)
            for m in range(2):
                dve.wait_ge(sem("hg_bc"), m + 1)
                STT(out=hgo[:, m, :], in0=hgo[:, m, :], scalar=col("hg_norm"), in1=banks[6 + m][:, 0:256],
                    op0=ALU.mult, op1=ALU.mult).then_inc(sem("hg_n"), 1)
            for h in range(8):
                m_norm(h)
                if 0 < h < 7:
                    m_max(h + 1)
                if h == 1:
                    for m in range(2):
                        taken(dve, group(("hg_g", 0), m))
                        dve.wait_ge(sem("hg_n"), m + 1)
                        tt(hgo[:, m, :], hgo[:, m, :], hgg[:, m, :], ALU.mult).then_inc(sem("yb"), 1)
                if h == 2:
                    for m in range(2):
                        taken(dve, group(("lru_y", 0), m))
                        tt(xc[:, m, :], lru_r[:, m, :], lru_g[:, m, :], ALU.mult).then_inc(sem("lru_h"), 1)
                if h == 5:
                    for m in range(2):
                        dve.wait_ge(sem("ycat_hi"), m + 1)
                        tt(ycat_lo[:, 2 + m, :], hgo[:, m, :], ycat_hi[:, 2 + m, :].bitcast(F32),
                           ALU.subtract).then_inc(sem("ycat_lo"), 1)
            dve.wait_ge(sem("ya_rms"), 1)
            seq(V.reciprocal(rst2[:, :], rst2[:, :]))
            for m in range(2):
                STT(out=xc[:, m, :], in0=xc[:, m, :], scalar=col("lru_norm", m), in1=rst2[:, :],
                    op0=ALU.mult, op1=ALU.mult).then_inc(sem("ya"), 1)
            for m in range(2):
                dve.wait_ge(sem("ycat_hi"), 3 + m)
                tt(ycat_lo[:, m, :], xc[:, m, :], ycat_hi[:, m, :].bitcast(F32), ALU.subtract).then_inc(
                    sem("ycat_lo"), 1)
            split_to(unit_at[("w_out2", 0)]["n"] + 2)
            dve.wait_ge(sem("yc_rms"), 1)
            seq(V.reciprocal(rst3[:, :], rst3[:, :]))
            for p_ in range(5):
                if p_ < 4:
                    STT(out=mo[:, p_, :], in0=mo[:, p_, :], scalar=col("att_norm", p_), in1=rst3[:, :],
                        op0=ALU.mult, op1=ALU.mult).then_inc(sem("yc"), 1)
                if p_:
                    dve.wait_ge(sem("ycat_hi"), 4 + p_)
                    tt(ycat_lo[:, 3 + p_, :], mo[:, p_ - 1, :], ycat_hi[:, 3 + p_, :].bitcast(F32),
                       ALU.subtract).then_inc(sem("ycat_lo"), 1)
            for i in range(4):
                split_to(unit_at[("w_out2", i)]["n"] + 3 - i // 3)
                for m in range(2):
                    g = group(("w_out2", i), m)
                    dve.wait_ge(sem("group_done"), g + 1)
                    tt(x2[:, 2 * i + m, :], x2[:, 2 * i + m, :], banks[g % NB][:, 0:256], ALU.add).then_inc(
                        sem(f"group_free{g % NB}"), 1)
                    x_square("x3", 2 * i + m - 1)
            x_square("x3", 7)
            for m in range(8):
                taken(dve, group(("w_out2", m // 2), m % 2))
            norm_in("x3_rms", "x3_hi", "x3_lo", x2, "norm_mlp")
            for i in range(KF2 // 2):
                split_to(unit_at[("ff1", i)]["n"] + 3)
                for m in range(2):
                    taken(dve, group(("ff1", i), m))
                    r = relu[:, i % 2, m, :]
                    tt(uu[:, i % 2, m, :], r, r, ALU.mult).then_inc(sem("uu"), 1)
                for m in range(2):
                    dve.wait_ge(sem("u_hi"), 2 * i + m + 1)
                    tt(u_lo[:, i % 2, m, :], uu[:, i % 2, m, :], u_hi[:, i % 2, m, :].bitcast(F32),
                       ALU.subtract).then_inc(sem("u_lo"), 1)
            split_to(len(units))
            dve.wait_ge(sem("nf_in"), 16)
            for t in range(2):
                dve.wait_ge(sem("f_rms"), t + 1)
                seq(V.reciprocal(sm("fr", 2)[:, t:t + 1], sm("fr", 2)[:, t:t + 1]))
                for h in range(2):
                    c = slice(512 * h, 512 * h + 512)
                    STT(out=outb[:, t, c], in0=banks[4 + 2 * t + h][:, :], scalar=sm("fr", 2)[:, t:t + 1],
                        in1=nf[:, c], op0=ALU.mult, op1=ALU.mult).then_inc(sem("out_ready"), 1)

        @block.tensor
        def _(pe):
            T = nc.tensor

            def mm3(out_, lh, ll, rh, rl, start, stop):
                T.matmul(out_, lh, rh, start=start, stop=False)
                T.matmul(out_, lh, rl, start=False, stop=False)
                return T.matmul(out_, ll, rh, start=False, stop=stop)

            def unit(name, i, acts, kk, tok_cols=None, ready=None, between=None, ms=None,
                     ready_from=1):
                u = unit_at[(name, i)]
                un = u["n"]
                pe.wait_ge(sem("lo_ready"), un + 1)
                ah, al, lo_c, hi_c = acts
                wh = w_hi[:, un % NW, :].rearrange("p (k n) -> p k n", k=kk)
                wl = w_lo[:, un % NW, :].rearrange("p (k n) -> p k n", k=kk)
                for m in ms or range(u["groups"]):
                    g = u["g0"] + m
                    need(pe, f"group_free{g % NB}", free_count(g))
                    bank = banks[g % NB]
                    for kt in range(kk):
                        a, z = kt == 0, kt == kk - 1
                        if ready and m == 0:
                            pe.wait_ge(sem(ready), max(kt + 1, ready_from))
                        if u["kind"] == "feat":
                            c = slice(P * m, P * m + P)
                            last = mm3(bank[:, 0:hi_c - lo_c], wh[:, kt, c], wl[:, kt, c], ah[:, kt, lo_c:hi_c],
                                       al[:, kt, lo_c:hi_c], a, z)
                        else:
                            c = slice(tok_cols[m], tok_cols[m] + P)
                            last = mm3(bank[:, 0:256], ah[:, kt, c], al[:, kt, c], wh[:, kt, :], wl[:, kt, :], a, z)
                    last.then_inc(sem("group_done"), 1)
                    if between and m == 0:
                        between()

            def param_cols(i, signal, n_):
                pe.wait_ge(sem(signal), 16 * n_)
                w = PTILES[i][1]
                need(pe, "C_ready", min(i, 2))
                T.transpose(banks[3][:, P * i:P * i + w], params[:, i][0:w, :], ident[0:w, 0:w]).then_inc(
                    sem("par_T"), 1)

            pe.wait_ge(sem("constants"), CONSTANTS["ident"])
            param_cols(0, "par0_in", 1)

            def to_features(src, kt):
                b = banks[4 + kt % 4]
                T.transpose(b[:, 0:META], src[0:META, 0, P * kt:P * kt + P], ident[0:META, 0:META])
                T.transpose(b[:, META:META + P], src[:, 1, P * kt:P * kt + P], ident[:])
                return T.transpose(b[:, META + P:TOK], src[:, 2, P * kt:P * kt + P], ident[:])

            pe.wait_ge(sem("xr"), 3)
            for kt in range(KD):
                need(pe, "xn_lo", kt - 3)
                to_features(xr, kt).then_inc(sem("xrT"), 1)
            param_cols(1, "ssm_in", 4)
            xn = (xn_hi, xn_lo, 0, TOK)
            xq = (xn_hi, xn_lo, T0, TOK)
            unit("u", 0, xn, 8, ready="xn_lo")
            unit("u", 1, xn, 8)
            for kt in range(KD):
                need(pe, "hT_copy", kt - 3)
                to_features(xtok, kt).then_inc(sem("xT"), 1)
            param_cols(2, "par_in", 21)
            param_cols(3, "par_in", 21)
            unit("k", 0, xn, 8)
            unit("k", 1, xn, 8)
            pe.wait_ge(sem("bc_blk"), 8)
            pe.wait_ge(sem("hT_copy"), 8)
            for i in range(4):
                src = (b_blk, c_blk)[i // 2][:, i % 2]
                src = src.rearrange("p a b c -> p (a b c)")
                for a in range(4):
                    last = T.transpose(banks[4 + i][:, P * a:P * a + P], src[:, P * a:P * a + P], ident[:])
                last.then_inc(sem("bcT"), 1)
            pe.wait_ge(sem("bc_ready"), 4)
            u1 = unit_at[("u", 1)]
            for m in range(2):
                g = u1["g0"] + m
                taken(pe, g)

            def s5_in(b):
                c, jp = divmod(b, 8)
                jj = jp // 2
                need(pe, "s5_m", b - 1)
                for part in range(2):
                    for i in range(2):
                        bank = banks[4 + 2 * (b % 2) + i]
                        r = 64 * (jp % 2) + 32 * i
                        last = T.matmul(bank[:, LC * part:LC * part + LC], BT[r:r + 32, jj, part, :],
                                        uT[r:r + 32, jj, LC * c:LC * c + LC], start=True, stop=True)
                last.then_inc(sem("s5_x"), 1)

            def s5_out(kk):
                jj = kk % 4
                pe.wait_ge(sem("s5_n"), 2 * kk + 2)
                need(pe, "y_pre", kk)
                for q in range(4):
                    for i in range(4):
                        r = 32 * i
                        last = T.matmul(banks[3][r:r + 32, 0:LC], CT[:, jj, q // 2, r:r + 32],
                                        mprod[:, (2 * kk + i // 2) % NM, q, LC * (i % 2):LC * (i % 2) + LC],
                                        start=(q == 0), stop=(q == 3))
                last.then_inc(sem("s5_out"), 1)

            v_cols = (0, META, META + P)
            seq_units = [("q", 0, xn, None), ("q", 1, xn, None),
                         ("v", 0, xn, v_cols), ("v", 1, xn, v_cols), ("gate", 0, xq, None), ("gate", 1, xq, None),
                         ("gate", 2, xq, None), ("gate", 3, xq, None)]

            def s5_step(b):
                if b < 16:
                    s5_in(b)
                if b % 2 == 0 and b >= 4:
                    s5_out(b // 2 - 2)

            s5_in(0)
            s5_in(1)
            for i, (name, j, x_, tc) in enumerate(seq_units):
                s5_step(2 * i + 2)
                unit(name, j, x_, 8, tc, between=lambda: s5_step(2 * i + 3))
            unit("gate", 4, xq, 8, between=lambda: s5_out(7))
            pe.wait_ge(sem("constants"), CONSTANTS["sel"])
            for i in range(8):
                pe.wait_ge(sem("qk_sq"), i + 1)
                T.matmul(banks[4][0:16, 0:TOK], sel[:, i, :], sq[:, i % 2, :], start=(i == 0),
                         stop=(i == 7)).then_inc(sem("qk_stat"), 1)
            unit("gate", 5, xq, 8)
            pe.wait_ge(sem("qk_r"), 1)

            def norm_bc(i):
                need(pe, "qkn", i - 2)
                T.matmul(banks[5 + i % 3][:, 0:TOK], selT[:, i, :], rs[:, :], start=True, stop=True).then_inc(
                    sem("qk_bc"), 1)

            for i in range(8):
                norm_bc(i)
            pe.wait_ge(sem("qkn"), 8)

            def scores_a(h):
                need(pe, "max_a", h)
                for j in range(2):
                    r = slice(64 * j, 64 * j + 64)
                    last = T.matmul(banks[4 + j][:, 0:TOK], qkT[r, 4 + h, KEYS_B:TOK], qkT[r, h, 0:TOK],
                                    start=True, stop=True)
                last.then_inc(sem("scores_a"), 1)

            def scores_b(h):
                need(pe, "copied_a", 2 * h)
                need(pe, "copied_b", 2 * h)
                for t, t0, nk in ((0, META, KEYS_B), (1, 0, META)):
                    for j in range(2):
                        r, c = slice(64 * j, 64 * j + 64), KEYS_B * t
                        last = T.matmul(banks[6 + j][:, c:c + nk], qkT[r, 4 + h, t0:t0 + P], qkT[r, h, 0:nk],
                                        start=True, stop=True)
                last.then_inc(sem("scores_b"), 1)

            def turn_a(h):
                pe.wait_ge(sem("w_a"), h + 1)
                need(pe, "copied_a", 2 * h)
                T.transpose(banks[7][:, 0:P], w_a[:, META:META + P], ident[:])
                T.transpose(banks[7][:, P:2 * P], w_a[:, META + P:TOK], ident[:])
                T.transpose(banks[7][0:META, 2 * P:3 * P], w_a[:, 0:META], ident[:]).then_inc(sem("turn_a"), 1)

            def turn_b(h):
                pe.wait_ge(sem("w_b"), 2 * h + 2)
                T.transpose(banks[6][:, 0:P], w_b[:, 0, META:KEYS_B], ident[:])
                T.transpose(banks[6][0:META, P:P + META], w_b[0:META, 1, 0:META], ident[0:META, 0:META])
                T.transpose(banks[6][0:META, P + META:P + KEYS_B], w_b[:, 0, 0:META], ident[:]).then_inc(
                    sem("turn_b"), 1)

            def values(h):
                pe.wait_ge(sem("copied_a"), 2 * h + 2)
                pe.wait_ge(sem("copied_b"), 2 * h + 2)
                need(pe, "o_copied", h)
                c = slice(P * h, P * h + P)
                T.matmul(banks[3][:, 0:TOK], v_tok[0:META, 0, c], wT0[:, :], start=True, stop=False)
                T.matmul(banks[3][:, META:TOK], v_tok[:, 1, c], wT12[:, 0:256], start=False, stop=False)
                T.matmul(banks[3][:, META + P:TOK], v_tok[:, 2, c], wT12[:, 256:384], start=False,
                         stop=True).then_inc(sem("att_o"), 1)

            def step_a(h):
                if h:
                    scores_b(h)
                    values(h - 1)
                if h < 3:
                    scores_a(h + 1)
                turn_a(h)

            y_in = (yg_hi, yg_lo, 0, NQ)
            scores_a(0)
            scores_b(0)
            step_a(0)
            pe.wait_ge(sem("yg_lo"), 4)
            unit("glu", 0, y_in, 4, ms=(0, 1))
            turn_b(0)
            unit("glu", 0, y_in, 4, ms=(2, 3))
            for h in (1, 2):
                step_a(h)
                unit("gate", 5 + h, xq, 8, ms=(0,))
                turn_b(h)
                unit("gate", 5 + h, xq, 8, ms=(1,))
            step_a(3)
            unit("ssm_out", 0, y_in, 4, ms=(0, 1), ready="yssm_lo")
            turn_b(3)
            unit("ssm_out", 0, y_in, 4, ms=(2, 3))
            values(3)
            unit("ssm_out", 1, y_in, 4, ms=(0, 1))
            for h in range(4):
                pe.wait_ge(sem("o_sq"), h + 1)
                T.matmul(banks[4][0:4, 0:TOK], selH[:, h, :], sq[:, h % 2, :], start=(h == 0),
                         stop=(h == 3)).then_inc(sem("o_stat"), 1)
            unit("ssm_out", 1, y_in, 4, ms=(2, 3))
            pe.wait_ge(sem("o_r"), 1)
            for h in range(4):
                T.matmul(banks[4 + h][:, 0:TOK], selHT[:, h, :], rs2[:, :], start=True, stop=True).then_inc(
                    sem("o_bc"), 1)
            for i in range(2):
                unit("att_out", i, (yatt_hi, yatt_lo, 0, NQ), 4, ready=None if i else "yatt_lo")

            for i in range(4):
                unit("w_o", i, (mix_hi, mix_lo, 0, NQ), 8, ready=None if i else "mix_lo")
            pe.wait_ge(sem("h1_sum"), 7)
            T.matmul(banks[3][:, 0:NQ], ones[:], sqsum[:, :], start=True, stop=True).then_inc(sem("h1_stat"), 1)

            def down(i):
                un = unit_at[("down", i)]["n"]
                pe.wait_ge(sem("lo_ready"), un + 1)
                pe.wait_ge(sem("ff_lo"), 2 * i + 2)
                wh = w_hi[:, un % NW, :].rearrange("p (k n) -> p k n", k=2)
                wl = w_lo[:, un % NW, :].rearrange("p (k n) -> p k n", k=2)
                for m in range(8):
                    for kt in range(2):
                        o = banks[4 + m // 2][:, 256 * (m % 2):256 * (m % 2) + 256]
                        c = slice(P * m, P * m + P)
                        first = i == 0 and kt == 0 and m % 2 == 0
                        z = i == KF // 2 - 1 and kt == 1 and m % 2 == 1
                        T.matmul(o, wh[:, kt, c], ff_hi[:, i % 2, kt, :], start=first, stop=False,
                                 skip_group_check=True)
                        T.matmul(o, wh[:, kt, c], ff_lo[:, i % 2, kt, :], start=False, stop=False,
                                 skip_group_check=True)
                        last = T.matmul(o, wl[:, kt, c], ff_hi[:, i % 2, kt, :], start=False, stop=z,
                                        skip_group_check=True)
                    if i == KF // 2 - 1 and m % 2 == 1:
                        last.then_inc(sem("down_done"), 1)
                if i < KF // 2 - 1:
                    last.then_inc(sem("acc_unit_done"), 1)

            for i in range(KF // 2):
                unit("up_a", i, (hs_hi, hs_lo, 0, NQ), 8, ready=None if i else "hs_lo")
                unit("up_b", i, (hs_hi, hs_lo, 2, NQ), 8)
                if i:
                    down(i - 1)
            down(KF // 2 - 1)

            def stat(name, ready, i, n_, bank=3):
                pe.wait_ge(sem(ready), i + 1)
                T.matmul(banks[bank][:, 0:256], ones[:], sq2[:, i % 2, :], start=(i == 0), stop=(i == n_ - 1)).then_inc(
                    sem(name), 1)

            def x_stat(x_):
                pe.wait_ge(sem(x_ + "_stat_sum"), 7)
                T.matmul(banks[3][:, 0:256], ones[:], rst3[:, :], start=True, stop=True).then_inc(sem(x_ + "_stat"), 1)

            x_stat("x2")
            x2n = (x2n_hi, x2n_lo, 0, 256)
            unit("lru_x", 0, x2n, 8, ready="x2n_lo")
            unit("hg_f", 0, x2n, 8)
            for m in range(2):
                taken(pe, group(("lru_x", 0), m))
            pe.wait_ge(sem("lru_w_in"), 64)
            for i in range(2):
                for m in range(2):
                    last = T.matmul(banks[6 + i][:, 256 * m:256 * m + 256], lru_w[:, i, m, :], xc[:, m, :], start=True,
                                    stop=True)
                last.then_inc(sem("lru_gate"), 1)
            unit("hg_q", 0, x2n, 8)
            unit("hg_i", 0, x2n, 8, (0, P))

            def h_scores(lv):
                pe.wait_ge(sem("h_level"), max(lv, 1))
                need(pe, "h_taken", lv - 1)
                if lv == 1:
                    pe.wait_ge(sem("lru_ri"), 4)
                q = hgq if lv == 0 else hqf
                for par in range(2):
                    r = slice(64 * par, 64 * par + 64)
                    bank = banks[4 + 2 * (lv % 2) + par]
                    for hp in range(2):
                        for t in range(1 if lv == 8 else 2):
                            c = P * (hp if lv == 8 else 2 * t + hp)
                            tq = P if lv == 8 else P * t
                            last = T.matmul(bank[:, c:c + P], hgk[r, hp, P * t:P * t + P], q[r, hp, tq:tq + P],
                                            start=True, stop=True)
                last.then_inc(sem("h_scores"), 1)

            for i, (name, j, tc) in enumerate((("cq", 0, None), ("cq", 1, None), ("ck", 0, None), ("ck", 1, None),
                                               ("cv", 0, (0, P)))):
                unit(name, j, x2n, 8, tc, between=lambda: h_scores(2 * i))
                if i < 4:
                    h_scores(2 * i + 1)
            unit("cv", 1, x2n, 8, (0, P))
            for m in range(2):
                taken(pe, group(("hg_i", 0), m))
            pe.wait_ge(sem("h_taken"), 9)
            for par in range(2):
                r = slice(64 * par, 64 * par + 64)
                for hp in range(2):
                    c = slice(64 * (2 * hp + par), 64 * (2 * hp + par) + 64)
                    T.matmul(banks[3][r, 256 * hp:256 * hp + P], hgv[:, 0, c], hA[:, 4 * par + hp, :], start=True,
                             stop=True)
                    T.matmul(banks[3][r, 256 * hp + P:256 * hp + 256], hgv[:, 0, c], hX[:, 2 * par + hp, :],
                             start=True, stop=False)
                    last = T.matmul(banks[3][r, 256 * hp + P:256 * hp + 256], hgv[:, 1, c],
                                    hA[:, 4 * par + 2 + hp, :], start=False, stop=True)
            last.then_inc(sem("hg_o"), 1)
            unit("hg_g", 0, x2n, 8)
            for m in range(2):
                pe.wait_ge(sem("hgo"), m + 2)
                T.matmul(banks[3][0:4, 0:256], sel[:, m, 0:4], sq2[:, m, :], start=(m == 0), stop=(m == 1)).then_inc(
                    sem("hg_stat"), 1)

            def m_scores(h):
                need(pe, "m_max", h - 1)
                r = slice(64 * (h % 2), 64 * (h % 2) + 64)
                for t, c in ((0, slice(0, P)), (1, slice(P, 384))):
                    last = T.matmul(banks[4 + h % 2][:, c], cq[r, h // 2, P * t:P * t + P],
                                    ck[r, h // 2, 0:P * t + P], start=True, stop=True)
                last.then_inc(sem("m_s"), 1)

            def m_turn(h):
                pe.wait_ge(sem("m_w"), 2 * h + 2)
                need(pe, "m_copied", h - 1)
                if h < 2:
                    pe.wait_ge(sem("hg_n"), h + 1)
                for i in range(3):
                    last = T.transpose(banks[6 + h % 2][:, P * i:P * i + P], mp[:, h % 2, P * i:P * i + P], ident[:])
                last.then_inc(sem("m_T"), 1)

            def m_values(h):
                pe.wait_ge(sem("m_copied"), h + 1)
                if h % 2 == 0:
                    need(pe, "m_out", h // 2)
                if h == 0:
                    pe.wait_ge(sem("hg_rms"), 1)
                r = slice(64 * (h % 2), 64 * (h % 2) + 64)
                c = slice(64 * h, 64 * h + 64)
                T.matmul(banks[3][r, 0:256], cv[:, 0, c], mpT[:, h % 2, 0:256], start=True, stop=False)
                T.matmul(banks[3][r, P:256], cv[:, 1, c], mpT[:, h % 2, 256:384], start=False, stop=True).then_inc(
                    sem("m_val"), 1)

            for m in range(2):
                taken(pe, group(("cv", 1), m))
            m_scores(0)
            m_scores(1)
            unit("lru_y", 0, x2n, 8)
            pe.wait_ge(sem("hg_r"), 1)
            for m in range(2):
                T.matmul(banks[6 + m][:, 0:256], selT[0:4, m, :], rsm2[:, :], start=True, stop=True).then_inc(
                    sem("hg_bc"), 1)
            for h in range(8):
                if 0 < h < 7:
                    m_scores(h + 1)
                m_turn(h)
                if h:
                    m_values(h - 1)
            for m in range(2):
                stat("ya_stat", "ya_sq", m, 2, 4)
            for p_ in range(3):
                stat("yc_stat", "yc_sq", p_, 4, 5)
            m_values(7)
            stat("yc_stat", "yc_sq", 3, 4, 5)
            for i in range(4):
                unit("w_out2", i, (ycat_hi, ycat_lo, 0, 256), 8, ready=None if i else "ycat_lo", ready_from=4)
            x_stat("x3")
            for t in range(2):
                for kt in range(KD):
                    T.matmul(banks[4 + 2 * t + kt // 4][:, P * (kt % 4):P * (kt % 4) + P], x2[:, kt, P * t:P * t + P],
                             ident[:], start=(kt % 4 == 0), stop=False, skip_group_check=True)

            def ff2(i):
                un = unit_at[("ff2", i)]["n"]
                pe.wait_ge(sem("lo_ready"), un + 1)
                pe.wait_ge(sem("u_lo"), 2 * i + 2)
                wh = w_hi[:, un % NW, :].rearrange("p (k n) -> p k n", k=2)
                wl = w_lo[:, un % NW, :].rearrange("p (k n) -> p k n", k=2)
                final = i == KF2 // 2 - 1
                for kt, t in (((0, 0), (1, 0), (0, 1), (1, 1)) if final else ((0, 0), (0, 1), (1, 0), (1, 1))):
                    uh = u_hi[:, i % 2, kt, P * t:P * t + P]
                    ul = u_lo[:, i % 2, kt, P * t:P * t + P]
                    for h in range(2):
                        c = slice(512 * h, 512 * h + 512)
                        o = banks[4 + 2 * t + h]
                        T.matmul(o, uh, wh[:, kt, c], start=False, stop=False, skip_group_check=True)
                        T.matmul(o, uh, wl[:, kt, c], start=False, stop=False, skip_group_check=True)
                        last = T.matmul(o, ul, wh[:, kt, c], start=False, stop=final and kt == 1,
                                        skip_group_check=True)
                    if final and kt == 1:
                        last.then_inc(sem("ff2_done"), 1)
                if not final:
                    last.then_inc(sem("acc_unit_done"), 1)

            for i in range(KF2 // 2):
                unit("ff1", i, x2n, 8, ready=None if i else "x3_lo")
                if i:
                    ff2(i - 1)
            ff2(KF2 // 2 - 1)


_INS = ["x", "meta_tokens", "norm1_g", "w_in", "ssm_a_re", "ssm_a_im", "ssm_log_dt", "ssm_b_re", "ssm_b_im", "ssm_c_re",
        "ssm_c_im", "ssm_d", "ssm_glu_w", "ssm_glu_b", "q_norm_g", "k_norm_g", "lam_q1", "lam_k1", "lam_q2", "lam_k2",
        "subln_g", "w_ssm_out", "w_att_out", "w_o", "norm2_g", "w_up", "conv_w", "conv_b", "w_down", "w_in_2",
        "w_out_2", "norm_mix_2", "norm_mlp_2", "lru_conv_w_2", "lru_conv_b_2", "lru_wa_2", "lru_ba_2", "lru_wx_2",
        "lru_bx_2", "lru_lambda_2", "hg_lower_bounds_2", "hg_norm_w_2", "lru_out_norm_2", "att_out_norm_2", "w_ff1_2",
        "w_ff2_2", "norm_final_2"]


def kernel(**inputs):
    import numpy as _np
    import concourse.bacc as _bacc
    from concourse import mybir as _mybir
    from concourse.bass_utils import run_bass_kernel_spmd as _run

    nc = _bacc.Bacc("TRN2", target_bir_lowering=False, num_devices=1)
    arrays, args = {}, {}
    for name in _INS:
        a = _np.ascontiguousarray(inputs[name])
        arrays[f"in_{name}_dram"] = a
        args[name] = nc.dram_tensor(f"in_{name}_dram", a.shape, _mybir.dt.from_np(a.dtype), kind="ExternalInput").ap()
    out = nc.dram_tensor("out_0_dram", (1, SEQ, D), _mybir.dt.float32, kind="ExternalOutput").ap()
    program(nc, args, out)
    r = _run(nc, [arrays], core_ids=[0])
    return r.results[0]["out_0_dram"]
```
